# Optimizing a Trainium2 kernel written in Bass

```python
import jax, jax.numpy as jnp
from jax import lax
import numpy as np

D_MODEL = 1024
BATCH = 1
SEQ = 1024
DEPTH = 1
DEC_BATCH = 1
DEC_SEQ = 512
PAST_LEN = 128

D_MIX = D_MODEL
HEAD_DIM = 64
CONV_W = 3 * D_MIX // 8
FOURIER_W = D_MIX // 4
SGU_W = D_MIX - CONV_W - FOURIER_W
CONV_HEADS = CONV_W // HEAD_DIM
FOURIER_GROUPS = FOURIER_W // HEAD_DIM
SGU_HEADS = SGU_W // HEAD_DIM
CONV_K = 3
CHUNK = 128
IN_W = 3 * CONV_W + FOURIER_W + 2 * SGU_W
SPLITS = (CONV_W, 2 * CONV_W, 3 * CONV_W, 3 * CONV_W + FOURIER_W, 3 * CONV_W + FOURIER_W + SGU_W)
N_EXPERTS = 16
CAPACITY_FACTOR = 2
D_EXPERT = D_MODEL
N_MOD = 6
EPS = 1e-6

kernel_name = 'hybrid_parallel_conv_fourier_sgu_ec_moe_encoder'

def rms_norm(x, g):
    xf = x.astype(jnp.float32)
    y = xf * lax.rsqrt(jnp.mean(xf * xf, axis=-1, keepdims=True) + EPS)
    return y.astype(x.dtype) * g

def modulate(x, g, shift, scale):
    return rms_norm(x, g) * (1 + scale[:, None, :]) + shift[:, None, :]

def short_conv_mixer(zb, zc, za, conv_w):
    a = zc * za
    a_prev = jnp.pad(a[:, :-1], ((0, 0), (1, 0), (0, 0)))
    a_next = jnp.pad(a[:, 1:], ((0, 0), (0, 1), (0, 0)))
    return zb * (conv_w[0] * a_prev + conv_w[1] * a + conv_w[2] * a_next)

def fourier_mixer(zf):
    b, s, _ = zf.shape
    f = zf.reshape(b, s, FOURIER_GROUPS, HEAD_DIM).astype(jnp.float32)
    y = jnp.real(jnp.fft.fft2(f, axes=(1, 3), norm='ortho'))
    return y.reshape(b, s, FOURIER_W).astype(zf.dtype)

def spatial_gating_mixer(zu, zv, g_sgu, w_sp, b_sp):
    b, s, _ = zu.shape
    u = jax.nn.gelu(zu)
    v = rms_norm(jax.nn.gelu(zv), g_sgu)
    v = v.reshape(b, s // CHUNK, CHUNK, SGU_HEADS, HEAD_DIM)
    sv = jnp.einsum('hpq,bnqhd->bnphd', w_sp, v) + b_sp.T[None, None, :, :, None]
    return u * sv.reshape(b, s, SGU_W)

def token_mixer(h, w_in, conv_w, g_sgu, w_sp, b_sp, g_grp, w_out):
    z = h @ w_in
    zb, zc, za, zf, zu, zv = jnp.split(z, SPLITS, axis=-1)
    ya = rms_norm(short_conv_mixer(zb, zc, za, conv_w), g_grp[:CONV_W])
    yf = rms_norm(fourier_mixer(zf), g_grp[CONV_W:CONV_W + FOURIER_W])
    yc = rms_norm(spatial_gating_mixer(zu, zv, g_sgu, w_sp, b_sp), g_grp[CONV_W + FOURIER_W:])
    return jnp.concatenate([ya, yf, yc], axis=-1) @ w_out

def expert_choice_moe(h, w_router, w_gate, w_up, w_down):
    b, s, d = h.shape
    n = b * s
    cap = CAPACITY_FACTOR * n // N_EXPERTS
    hf = h.reshape(n, d)
    aff = jax.nn.softmax(hf.astype(jnp.float32) @ w_router.astype(jnp.float32), axis=-1)
    gates, idx = lax.top_k(aff.T, cap)
    xe = hf[idx]
    hid = jax.nn.silu(jnp.einsum('ecd,edf->ecf', xe, w_gate)) * jnp.einsum('ecd,edf->ecf', xe, w_up)
    ye = jnp.einsum('ecf,efd->ecd', hid, w_down) * gates[..., None].astype(h.dtype)
    out = jnp.zeros_like(hf).at[idx.reshape(-1)].add(ye.reshape(-1, d))
    return out.reshape(b, s, d)

def encoder(x, c, w_ada, b_ada, g_mix, w_in, conv_w, g_sgu, w_spatial, b_spatial, g_grp, w_out,
            g_ffn, w_router, w_gate, w_up, w_down, g_final):
    for l in range(DEPTH):
        mod = jax.nn.silu(c) @ w_ada[l] + b_ada[l]
        sh_m, sc_m, gt_m, sh_f, sc_f, gt_f = jnp.split(mod, N_MOD, axis=-1)
        h = modulate(x, g_mix[l], sh_m, sc_m)
        x = x + gt_m[:, None, :] * token_mixer(h, w_in[l], conv_w[l], g_sgu[l], w_spatial[l],
                                               b_spatial[l], g_grp[l], w_out[l])
        h = modulate(x, g_ffn[l], sh_f, sc_f)
        x = x + gt_f[:, None, :] * expert_choice_moe(h, w_router[l], w_gate[l], w_up[l], w_down[l])
    return rms_norm(x, g_final)

def setup_inputs(seed: int = 0) -> dict:
    key = jax.random.key(seed)
    ks = jax.random.split(key, 24)
    nrm = jax.random.normal
    f32 = jnp.float32
    return {
        'x_prompt': nrm(ks[0], (BATCH, SEQ, D_MODEL), f32),
        'x_sample': nrm(ks[1], (DEC_BATCH, DEC_SEQ, D_MODEL), f32),
        'c_prompt': nrm(ks[2], (BATCH, D_MODEL), f32),
        'c_sample': nrm(ks[3], (DEC_BATCH, D_MODEL), f32),
        'w_ada': nrm(ks[4], (DEPTH, D_MODEL, N_MOD * D_MODEL), f32) * (0.5 * D_MODEL ** -0.5),
        'b_ada': nrm(ks[5], (DEPTH, N_MOD * D_MODEL), f32) * 0.02,
        'g_mix': 1.0 + 0.02 * nrm(ks[6], (DEPTH, D_MODEL), f32),
        'w_in': nrm(ks[7], (DEPTH, D_MODEL, IN_W), f32) * D_MODEL ** -0.5,
        'conv_w': nrm(ks[8], (DEPTH, CONV_K, CONV_W), f32) * CONV_K ** -0.5,
        'g_sgu': 1.0 + 0.02 * nrm(ks[9], (DEPTH, SGU_W), f32),
        'w_spatial': nrm(ks[10], (DEPTH, SGU_HEADS, CHUNK, CHUNK), f32) * CHUNK ** -0.5,
        'b_spatial': 1.0 + 0.02 * nrm(ks[11], (DEPTH, SGU_HEADS, CHUNK), f32),
        'g_grp': 1.0 + 0.02 * nrm(ks[12], (DEPTH, D_MIX), f32),
        'w_out': nrm(ks[13], (DEPTH, D_MIX, D_MODEL), f32) * D_MIX ** -0.5,
        'g_ffn': 1.0 + 0.02 * nrm(ks[14], (DEPTH, D_MODEL), f32),
        'w_router': nrm(ks[15], (DEPTH, D_MODEL, N_EXPERTS), f32) * D_MODEL ** -0.5,
        'w_gate': nrm(ks[16], (DEPTH, N_EXPERTS, D_MODEL, D_EXPERT), f32) * D_MODEL ** -0.5,
        'w_up': nrm(ks[17], (DEPTH, N_EXPERTS, D_MODEL, D_EXPERT), f32) * D_MODEL ** -0.5,
        'w_down': nrm(ks[18], (DEPTH, N_EXPERTS, D_EXPERT, D_MODEL), f32) * D_EXPERT ** -0.5,
        'g_final': 1.0 + 0.02 * nrm(ks[19], (D_MODEL,), f32),
    }

def reference(x_prompt, x_sample, c_prompt, c_sample, w_ada, b_ada, g_mix, w_in, conv_w, g_sgu,
              w_spatial, b_spatial, g_grp, w_out, g_ffn, w_router, w_gate, w_up, w_down, g_final):
    y_prompt = encoder(x_prompt, c_prompt, w_ada, b_ada, g_mix, w_in, conv_w, g_sgu, w_spatial,
                       b_spatial, g_grp, w_out, g_ffn, w_router, w_gate, w_up, w_down, g_final)
    y_sample = encoder(x_sample, c_sample, w_ada, b_ada, g_mix, w_in, conv_w, g_sgu, w_spatial,
                       b_spatial, g_grp, w_out, g_ffn, w_router, w_gate, w_up, w_down, g_final)
    return (y_prompt, y_sample)


_drawn_inputs = setup_inputs


def setup_inputs(seed=0):
    import zlib

    import numpy as np

    out = dict(_drawn_inputs(seed))
    spreads = {}
    factors = {'g_mix': 5.952,
     'g_sgu': 8.0,
     'b_spatial': 8.0,
     'g_grp': 8.0,
     'g_ffn': 8.0,
     'g_final': 2.829}
    for name, (base, spread) in spreads.items():
        noise = np.random.default_rng([zlib.crc32(name.encode()), seed]).standard_normal(out[name].shape)
        drawn = base * np.exp(spread * noise) if base else spread * noise
        out[name] = __import__('jax').numpy.asarray(drawn.astype(out[name].dtype))
    for name, factor in factors.items():
        out[name] = (out[name] * factor).astype(out[name].dtype)
    return out
```

```python
import numpy as np
import concourse.bass as bass
from concourse import mybir

P = 128
D = 1024
KB = D // P
S_P, S_S = 1024, 512
TOK = S_P + S_S
NT = TOK // P
GT = 4
GW = GT * P
NG = NT // GT
CONV_W, FOUR_W, SGU_W = 384, 256, 384
HD = 64
IN_W = 3 * CONV_W + FOUR_W + 2 * SGU_W
Z_B, Z_C, Z_A = 0, CONV_W, 2 * CONV_W
Z_F = 3 * CONV_W
Z_U = Z_F + FOUR_W
Z_V = Z_U + SGU_W
N_SGU = SGU_W // HD
EPS = 1e-6
NE = 16
CAP_P, CAP_S = 2 * S_P // NE, 2 * S_S // NE
CAP = CAP_P + CAP_S
ADA_W = 6 * D
ADA_C = 256
GRP_C = 8
N_ADA_G = ADA_W // (ADA_C * GRP_C)
CW = 256
N_CH = 12
RAW = 4
SPL = 6
FB = D // P
ROW_S = 32

F32, F32R, U32 = mybir.dt.float32, mybir.dt.float32r, mybir.dt.uint32
ACT = mybir.ActivationFunctionType
ALU = mybir.AluOpType
AX = mybir.AxisListType

V_C, V_GMIX, V_GGRP, V_CONV, V_GSGU, V_N = 0, 16, 24, 32, 41, 44


def conv_blocks():
    out = []
    for i in range(3):
        out += [("zc", i, Z_C + P * i), ("za", i, Z_A + P * i), ("zb", i, Z_B + P * i)]
    out += [("zf", i, Z_F + P * i) for i in range(2)]
    out += [("zu", i, Z_U + P * i) for i in range(3)]
    return out


def bank_jobs():
    jobs = [(("vec",), "dve")]

    def ada(g):
        return [(("ada", c), "dve") for c in range(GRP_C * g, GRP_C * (g + 1))]

    jobs += ada(0) + [(("mod", 0), "dve")]
    jobs += [(("hT", g, b), "act" if b % 2 == 0 else "dve") for g in range(NG) for b in range(KB)]
    jobs += [(("wsp", 0), "dve"), (("wsp", 1), "dve")]
    jobs += [(("zv", t), "act") for t in range(NT)]
    who = {"zc": "act", "za": "dve", "zb": "dve", "zf": "act", "zu": "act"}
    for n, (kind, i, _) in enumerate(conv_blocks()):
        if n == 3:
            jobs += ada(1)
        if n == 6:
            jobs += ada(2)
        if n == 9:
            jobs += [(("mod", 1), "dve"), (("mod", 2), "dve")]
        jobs += [((kind, i, g), who[kind]) for g in range(NG)]
        if n == 10:
            jobs += [(("ab", t), "act" if t % 2 else "dve") for t in range(NT)]
    jobs += [(("sv", i, g), "dve") for i in range(3) for g in range(NG)]
    for s in range(2):
        for fb in range(2):
            jobs += [(("even", s, fb), "act"), (("odd", s, fb), "dve")]
    jobs += [(("ssq", t), "dve") for t in range(NT)]
    for t in range(NT):
        jobs += [(("out", t, h, k), "act" if k == 0 else "dve") for h in range(2) for k in range(3)]
        if t in (4, 8, 11):
            g = (t - 1) // GT if t != 11 else 2
            jobs += [(("h2T", g, b), "act" if b % 2 == 0 else "dve") for b in range(KB)]
            jobs += [(("lg", g), "act")]
    jobs += [(("lt",), "dve"), (("aff", 0), "dve"), (("aff", 1), "dve"), (("idx",), "dve")]
    return jobs


def dft_constants():
    def seq(s):
        half = s // 2
        n = np.arange(s).reshape(s // 256, P, 2)
        n = n.transpose(2, 0, 1).reshape(s // P, P)
        ang = 2 * np.pi * ((n[:, :, None] * np.arange(half)) % s) / s
        both = np.stack([np.cos(ang), -np.sin(ang)], 2) / np.sqrt(s * HD)
        return np.ascontiguousarray(both.transpose(1, 0, 2, 3)).astype(np.float32)

    ang = 2 * np.pi * (np.outer(np.arange(HD), np.arange(HD)) % HD) / HD
    head = np.zeros((P, 2, P))
    for q in range(2):
        head[HD * q:HD * (q + 1), 0, HD * q:HD * (q + 1)] = np.cos(ang)
        head[HD * q:HD * (q + 1), 1, HD * q:HD * (q + 1)] = np.sin(ang)
    return {"dft_p": seq(S_P), "dft_s": seq(S_S), "dft_head": head.astype(np.float32),
            "ident": np.eye(P, dtype=np.float32)}


def encoder_kernel(nc, a, y_p, y_s):
    K = 1024
    base = (nc.sbuf_base + 63) // 64 * 64

    def at(name, offset, shape, dt=F32):
        return nc.alloc_sbuf_tensor_at(name, [P] + shape, dt, offset=base + int(offset))

    hT = at("hT", 0, [KB, TOK])
    dftp = at("dftp", 0, [KB, 2, S_P // 2])
    dfts = at("dfts", 32 * K, [GT, 2, S_S // 2])
    h2T = at("h2T", 32 * K, [KB, GW])
    Y = at("Y", 48 * K, [KB, TOK])
    brow = at("brow", 72 * K, [ADA_W])
    ada_w = at("ada_w", 96 * K, [2, KB, ADA_C])
    v = at("v", 112 * K, [NT, SGU_W])
    wo = at("wo", 96 * K, [KB, D])
    xg = at("xg", 130 * K, [2, GT, D])
    zc_sb = at("zc_sb", 130 * K, [TOK])
    a_pad = at("a_pad", 136 * K, [TOK + 4])
    cv = at("cv", 143 * K, [TOK + 4])
    AB = at("AB", 130 * K, [NT, 2, 2, P])
    e_sb = at("e_sb", 154 * K, [GW])
    svt = at("svt", 156 * K, [GW])
    SQ = at("SQ", 130 * K, [3, TOK])
    sqt = [at("sqt0", 148 * K, [TOK]), at("sqt1", 154 * K, [TOK])]
    h2 = at("h2", 130 * K, [GT, D])
    shf_b = at("shf_b", 146 * K, [2, D])
    gsf_b = at("gsf_b", 154 * K, [2, D])
    wi = at("wi", 162 * K, [3, KB, P])
    wv = at("wv", 174 * K, [KB, SGU_W])
    zfT = at("zfT", 174 * K, [2, TOK])
    gtm_b = at("gtm_b", 162 * K, [2, D])
    xr = at("xr", 170 * K, [2, D])
    x2 = at("x2", 178 * K, [2, D])
    stage = at("stage", 186 * K, [GRP_C * ADA_C])
    gffn_b = at("gffn_b", 186 * K, [D])
    raw = at("raw", 0, [RAW, KB * CW])
    gfin_b = at("gfin_b", 40 * K, [D])
    whi = at("whi", 48 * K, [SPL, KB * CW], F32R)
    wlo = at("wlo", 96 * K, [SPL, KB * CW], F32R)
    xe = at("xe", 32 * K, [2, D])
    xT = at("xT", 174 * K, [KB, 2 * CAP], F32R)
    hid = at("hid", 144 * K, [FB, 2 * CAP], F32R)
    aff = at("aff", 44 * K, [S_P])
    gu_l = at("gu_l", 156 * K, [2, 2, CAP])
    gu = at("gu", 159 * K, [2, 2, CAP])
    sg = at("sg", 186 * K, [2, CAP])
    hidf = at("hidf", 187.5 * K, [2, CAP])
    fin = at("fin", 0, [8, D])
    fjunk = at("fjunk", 44 * K, [D])
    ye = at("ye", 162 * K, [2, D])
    ysl = at("ysl", 170 * K, [D])
    gtf_b = at("gtf_b", 190 * K, [2, D])
    top = [198 * K]

    def small(name, shape, dt=F32):
        t = at(name, top[0], shape, dt)
        n = 4
        for s in shape:
            n *= s
        top[0] += (n + 31) // 32 * 32
        return t

    ident = small("ident_sb", [P])
    ones = small("ones", [P])
    rows = small("rows", [P])
    VT = small("VT", [V_N])
    silc = small("silc", [16])
    modrow = small("modrow", [3, P])
    modT = small("modT", [3, 32])
    gsm = small("gsm", [2, KB])
    ssx = small("ssx", [NT])
    rsx = small("rsx", [NT])
    ssv = small("ssv", [NT])
    ssy = small("ssy", [NT, 3])
    rsy = small("rsy", [NT, 3])
    ss2 = small("ss2", [NT])
    rs2 = small("rs2", [NT])
    ssf = small("ssf", [NT])
    rsf = small("rsf", [NT])
    wrt = small("wrt", [KB, NE])
    chs = small("chs", [2, P])
    wspT = small("wspT", [N_SGU, P])
    gates = small("gates", [2, ROW_S])
    rowid = small("rowid", [2, ROW_S], U32)
    gcur = small("gcur", [2])
    icur = small("icur", [2], U32)
    iscat = small("iscat", [2], U32)
    smax = small("smax", [NT])
    assert base + top[0] <= nc.sbuf_usable_end, (base + top[0], nc.sbuf_usable_end)
    bsp = at("bsp", 158 * K, [3, P])
    wsp6 = at("wsp6", 194 * K, [N_SGU, P])
    xjunk = at("xjunk", 112 * K, [D])
    vjunk = at("vjunk", 143 * K, [SGU_W])
    lgT = at("lgT", 128 * K, [GW])
    L = at("L", 162 * K, [GT, NG, ROW_S])
    L2 = at("L2", 164 * K, [GT, NG, NE])
    affm = at("affm", 166 * K, [KB, 2 * ROW_S])
    vals = at("vals", 168 * K, [P])
    idxu = at("idxu", 168.5 * K, [P], U32)
    idxf = at("idxf", 169 * K, [P])

    ps = nc.alloc_psum_tensor("ps", [P, 8, GW], F32)

    mod_d = nc.dram_tensor("mod_d", [2, ADA_W], F32).ap()
    h2_d = nc.dram_tensor("h2_d", [TOK, D], F32).ap()
    acc_d = nc.dram_tensor("acc_d", [TOK, D], F32).ap()

    sem = nc.alloc_semaphore
    jobs = bank_jobs()
    index = {k: n for n, (k, _) in enumerate(jobs)}
    drainer = dict(jobs)
    nth = {}
    for who in ("act", "dve"):
        nth |= {k: n + 1 for n, k in enumerate(k for k, w in jobs if w == who)}
    bank_filled = sem("bank_filled")
    drained = {"act": sem("bank_drained_by_act"), "dve": sem("bank_drained_by_dve")}

    def wait_filled(eng, *key):
        eng.wait_ge(bank_filled, index[key] + 1)

    def wait_drained(eng, *key):
        eng.wait_ge(drained[drainer[key]], nth[key])

    def bank(*key):
        return ps[:, index[key] % 8, :]

    rows_in, brow_in, small_in, wsp_in, bsp_in = map(sem, ("rows_in", "brow_in", "small_in", "wsp_in", "bsp_in"))
    x_in = [sem(f"x_in{i}") for i in range(2)]
    ada_in = [sem(f"ada_in{i}") for i in range(2)]
    mod_out, modrow_in = sem("mod_out"), [sem(f"modrow_in{i}") for i in range(N_ADA_G)]
    wv_in, wi_in = sem("wv_in"), [sem(f"wi_in{i}") for i in range(3)]
    dft_in, wo_in, gtm_in, ffn_in, gtf_in = map(sem, ("dft_in", "wo_in", "gtm_in", "ffn_in", "gtf_in"))
    xr_in = [sem(f"xr_in{i}") for i in range(2)]
    x2_out, h2_out = [sem(f"x2_out{i}") for i in range(2)], [sem(f"h2_out{i}") for i in range(GT)]
    raw_in = [sem(f"raw_in{i}") for i in range(RAW)]
    gfin_in, fin_in, fin_out = sem("gfin_in"), [sem(f"fin_in{i}") for i in range(8)], sem("fin_out")
    xe_in, scattered = sem("xe_in"), sem("scattered")
    sp_tick, pool_tick = sem("sp_tick"), sem("pool_tick")
    dve_step = sem("dve_step")
    ones_set, pads_set, silc_ready = sem("ones_set"), sem("pads_set"), sem("silc_ready")
    ssx_ready, var_x, std_x, xn_ready = map(sem, ("ssx_ready", "var_x", "std_x", "xn_ready"))
    gsm_ready, var_v, std_v, v_ready = map(sem, ("gsm_ready", "var_v", "std_v", "v_ready"))
    sq_done, sq_added, var_y, std_y, rsy_ready, wo_ready = map(
        sem, ("sq_done", "sq_added", "var_y", "std_y", "rsy_ready", "wo_ready"))
    x2_ready, ss2_ready, var_2, std_2, h2_ready = map(sem, ("x2_ready", "ss2_ready", "var_2", "std_2", "h2_ready"))
    lgt_zero, exp_in, exp_out, aff_ready, topk_ready, routed = map(
        sem, ("lgt_zero", "exp_in", "exp_out", "aff_ready", "topk_ready", "routed"))
    w_hi, w_split = sem("w_hi"), sem("w_split")
    t_filled, t_hi, t_lo = sem("t_filled"), sem("t_hi"), sem("t_lo")
    gu_filled, lo_copied, gu_summed = sem("gu_filled"), sem("lo_copied"), sem("gu_summed")
    silu_done, hid_done, hid_hi, hid_lo = map(sem, ("silu_done", "hid_done", "hid_hi", "hid_lo"))
    d_used, ysl_copied, ye_sum, ye_ready, ye_free = map(sem, ("d_used", "ysl_copied", "ye_sum", "ye_ready", "ye_free"))
    gate_cur, idx_cur = sem("gate_cur"), sem("idx_cur")
    ssf_ready, var_f, std_f, rsf_ready, fin_ready = map(sem, ("ssf_ready", "var_f", "std_f", "rsf_ready", "fin_ready"))

    x_src = [(a["x_prompt"][0], 0), (a["x_prompt"][0], GW), (a["x_sample"][0], 0)]

    def x_rows(t):
        src, off = x_src[t // GT]
        off += P * (t % GT)
        return src[off:off + P, :]

    def seq(g):
        return 0 if g < 2 else 1

    w_in, w_ada = a["w_in"][0], a["w_ada"][0]
    w_g = a["w_gate"][0].rearrange("e (k p) f -> e p k f", p=P)
    w_u = a["w_up"][0].rearrange("e (k p) f -> e p k f", p=P)
    w_d = a["w_down"][0].rearrange("e (k p) f -> e p k f", p=P)

    def out_rows(t):
        return y_p[0, P * t:P * (t + 1), :] if t < S_P // P else y_s[0, P * t - S_P:P * (t + 1) - S_P, :]

    def load_chunk(eng, e, j):
        slot = raw[:, j % RAW, :]
        if j < 8:
            src = (w_g, w_u)[j % 2][e, :, :, CW * (j // 2):CW * (j // 2 + 1)]
            dst = slot.rearrange("p (k f) -> p k f", k=KB)
        else:
            src = w_d[e, :, 2 * (j - 8):2 * (j - 8) + 2, :]
            dst = slot.rearrange("p (k f) -> p k f", k=2)
        eng.dma_start(dst, src).then_inc(raw_in[j % RAW], 16)

    with nc.Block() as block:

        @block.sync
        def _(sp):
            for name, at_row, n in (("c_prompt", V_C, 8), ("c_sample", V_C + 8, 8), ("g_mix", V_GMIX, 8),
                                    ("g_grp", V_GGRP, 8), ("g_sgu", V_GSGU, 3)):
                sp.dma_start(rows[at_row:at_row + n, :], a[name].rearrange("a (b n) -> (a b) n", n=P)
                             ).then_inc(rows_in, 16)
            sp.dma_start(rows[V_CONV:V_CONV + 9, :], a["conv_w"].rearrange("a k (b n) -> (a k b) n", n=P)
                         ).then_inc(rows_in, 16)

            def load_ada(c):
                if c >= 2:
                    wait_filled(sp, "ada", c - 2)
                src = w_ada[:, ADA_C * c:ADA_C * (c + 1)].rearrange("(k p) n -> p k n", p=P)
                sp.dma_start(ada_w[:, c % 2, :, :], src).then_inc(ada_in[c % 2], 16)

            def load_x(g):
                if g >= 2:
                    wait_filled(sp, "hT", g - 2, KB - 1)
                src, off = x_src[g]
                sp.dma_start(xg[:, g % 2, :, :], src[off:off + GW, :].rearrange("(t p) d -> p t d", p=P)
                             ).then_inc(x_in[g % 2], 16)

            def load_wi(n):
                if n >= 3:
                    wait_filled(sp, *conv_blocks()[n - 3][:2], NG - 1)
                col = conv_blocks()[n][2]
                sp.dma_start(wi[:, n % 3, :, :], w_in[:, col:col + P].rearrange("(k p) n -> p k n", p=P)
                             ).then_inc(wi_in[n % 3], 16)

            def mod_round_trip(g):
                n = GRP_C * ADA_C
                wait_drained(sp, "ada", GRP_C * (g + 1) - 1)
                sp.dma_start(mod_d[:, n * g:n * (g + 1)], stage[0:2, :]).then_inc(mod_out, 16)
                sp.wait_ge(mod_out, 16 * (g + 1))
                for s in range(2):
                    sp.dma_start(modrow[16 * s:16 * s + 16, g, :],
                                 mod_d[s, n * g:n * (g + 1)].rearrange("(j n) -> j n", n=P)
                                 ).then_inc(modrow_in[g], 16)

            load_ada(0)
            for s in range(2):
                sp.dma_start(brow[s:s + 1, :], a["b_ada"]).then_inc(brow_in, 16)
            load_ada(1)
            load_x(0)
            load_ada(2)
            load_ada(3)
            load_x(1)
            for c in range(4, GRP_C):
                load_ada(c)
            sp.dma_start(wv[:, :, :], w_in[:, Z_V:Z_V + SGU_W].rearrange("(k p) n -> p k n", p=P)
                         ).then_inc(wv_in, 16)
            for n in range(3):
                load_wi(n)
            mod_round_trip(0)
            load_x(2)
            wait_filled(sp, "hT", 1, KB - 1)
            for h in range(N_SGU):
                sp.dma_start(bsp[HD * (h % 2):HD * (h % 2) + HD, h // 2, :],
                             a["b_spatial"][0, h:h + 1, :].to_broadcast([HD, P])).then_inc(bsp_in, 16)
            for c in range(GRP_C, GRP_C + 2):
                load_ada(c)
            for n in range(3, 14):
                if n == 6:
                    for c in range(GRP_C + 2, 2 * GRP_C + 2):
                        load_ada(c)
                    mod_round_trip(1)
                if n == 9:
                    for c in range(2 * GRP_C + 2, 3 * GRP_C):
                        load_ada(c)
                    mod_round_trip(2)
                load_wi(n)
            wait_filled(sp, "zu", 2, NG - 1)
            sp.dma_start(dftp[:, :, :, :], a["dft_p"]).then_inc(dft_in, 16)
            sp.dma_start(dfts[:, :, :, :], a["dft_s"]).then_inc(dft_in, 16)
            for s in range(2):
                sp.dma_start(gtm_b[:, s, :], mod_d[s:s + 1, 2 * D:3 * D].to_broadcast([P, D])).then_inc(gtm_in, 16)
            wait_filled(sp, "sv", 2, NG - 1)
            sp.dma_start(wo[:, :, :], a["w_out"][0].rearrange("(k p) n -> p k n", p=P)).then_inc(wo_in, 16)
            for t in range(2):
                sp.dma_start(xr[:, t, :], x_rows(t)).then_inc(xr_in[t], 16)
            wait_filled(sp, "ssq", NT - 1)
            for s in range(2):
                sp.dma_start(shf_b[:, s, :], mod_d[s:s + 1, 3 * D:4 * D].to_broadcast([P, D])).then_inc(ffn_in, 16)
                sp.dma_start(gsf_b[:, s, :], mod_d[s:s + 1, 4 * D:5 * D].to_broadcast([P, D])).then_inc(ffn_in, 16)
                sp.dma_start(gtf_b[:, s, :], mod_d[s:s + 1, 5 * D:6 * D].to_broadcast([P, D])).then_inc(gtf_in, 16)
            sp.dma_start(gffn_b[:, :], a["g_ffn"].to_broadcast([P, D])).then_inc(ffn_in, 16)
            for j in range(RAW):
                load_chunk(sp, 0, j)
            for t in range(NT):
                sp.wait_ge(h2_ready, t + 1)
                sp.dma_start(acc_d[P * t:P * (t + 1), :], x2[:, t % 2, :]).then_inc(x2_out[t % 2], 16)
                sp.dma_start(h2_d[P * t:P * (t + 1), :], h2[:, t % GT, :]).then_inc(h2_out[t % GT], 16)
                if t + 2 < NT:
                    sp.dma_start(xr[:, t % 2, :], x_rows(t + 2)).then_inc(xr_in[t % 2], 16)

            with sp.Fori(0, NE - 1) as e:
                for j in range(N_CH):
                    sp.wait_ge(w_split, e * N_CH + (j + 1))
                    sp.sem_inc(sp_tick, 1)
                    if j < N_CH - RAW:
                        load_chunk(sp, e, j + RAW)
                    else:
                        load_chunk(sp, e + 1, j + RAW - N_CH)
            for j in range(N_CH - RAW):
                sp.wait_ge(w_split, (NE - 1) * N_CH + j + 1)
                load_chunk(sp, NE - 1, j + RAW)
            sp.dma_start(gfin_b[:, :], a["g_final"].rearrange("(a n) -> a n", a=1).to_broadcast([P, D])
                         ).then_inc(gfin_in, 16)

            sp.wait_ge(ye_free, NE + 1)
            for t in range(8):
                sp.dma_start(fin[:, t, :], acc_d[P * t:P * (t + 1), :]).then_inc(fin_in[t], 16)
            for t in range(NT):
                sp.wait_ge(fin_ready, t + 1)
                sp.dma_start(out_rows(t), fin[:, t % 8, :]).then_inc(fin_out, 16)
                if t + 8 < NT:
                    sp.wait_ge(fin_out, 16 * (t + 1))
                    sp.dma_start(fin[:, t, :], acc_d[P * (t + 8):P * (t + 9), :]).then_inc(fin_in[t], 16)
            sp.wait_ge(fin_out, 16 * NT)

        @block.gpsimd
        def _(pool):
            pool.memset(ones[:, :], 1.0).then_inc(ones_set, 1)

            def gather(e, copies):
                pool.tensor_copy(icur[:, :], rowid[:, :, bass.ds(e, 1)].rearrange("p a b -> p (a b)")
                                 ).then_inc(idx_cur, 1)
                pool.wait_ge(idx_cur, copies)
                pool.sem_inc(pool_tick, 1)
                pool.indirect_dma_start(xe[:, 0, :], None, h2_d, bass.IndirectOffsetOnAxis(ap=icur[:, 0:1], axis=0)
                                        ).then_inc(xe_in, 16)
                pool.indirect_dma_start(xe[0:CAP_S, 1, :], None, h2_d,
                                        bass.IndirectOffsetOnAxis(ap=icur[0:CAP_S, 1:2], axis=0)
                                        ).then_inc(xe_in, 16)

            def scatter(e, copies):
                pool.tensor_copy(iscat[:, :], rowid[:, :, bass.ds(e, 1)].rearrange("p a b -> p (a b)")
                                 ).then_inc(idx_cur, 1)
                pool.wait_ge(idx_cur, copies)
                pool.wait_ge(ye_ready, e * 3 + 3)
                pool.sem_inc(pool_tick, 1)
                pool.indirect_dma_start(acc_d, bass.IndirectOffsetOnAxis(ap=iscat[:, 0:1], axis=0), ye[:, 0, :],
                                        None, compute_op=ALU.add).then_inc(scattered, 16)
                pool.indirect_dma_start(acc_d, bass.IndirectOffsetOnAxis(ap=iscat[0:CAP_S, 1:2], axis=0),
                                        ye[0:CAP_S, 1, :], None, compute_op=ALU.add).then_inc(scattered, 16)
                pool.wait_ge(scattered, e * 32 + 32)
                pool.nop().then_inc(ye_free, 1)

            pool.wait_ge(routed, 2)
            for i in range(2):
                pool.wait_ge(x2_out[i], 16 * NT // 2)
            for i in range(GT):
                pool.wait_ge(h2_out[i], 16 * NT // GT)
            pool.nop().then_inc(ye_free, 1)
            gather(0, 1)
            with pool.Fori(0, NE - 1) as e:
                pool.wait_ge(t_filled, e * 4 + 4)
                gather(e + 1, e * 2 + 2)
                scatter(e, e * 2 + 3)
            scatter(NE - 1, NE * 2)

        @block.scalar
        def _(act):
            def drain(ins, *key):
                assert drainer[key] == "act"
                ins.then_inc(drained["act"], 1)

            act.dma_start(ident[:, :], a["ident"]).then_inc(small_in, 16)
            act.dma_start(chs[:, :, :], a["dft_head"]).then_inc(small_in, 16)
            act.dma_start(wrt[:, :, :], a["w_router"][0].rearrange("(k p) n -> p k n", p=P)).then_inc(small_in, 16)
            act.dma_start(wsp6[:, :, :], a["w_spatial"][0].rearrange("h p q -> p h q")).then_inc(wsp_in, 16)
            wait_drained(act, "vec")
            act.activation(silc[:, :], VT[:, V_C:V_C + 16], ACT.Silu).then_inc(silc_ready, 1)

            def x_stats(g):
                act.wait_ge(x_in[g % 2], 16 * (g // 2 + 1))
                for t in range(GT * g, GT * g + GT):
                    if t:
                        act.wait_ge(ssx_ready, t)
                    act.activation(xjunk[:, :], xg[:, g % 2, t % GT, :], ACT.Square,
                                   accum_out=ssx[:, t:t + 1]).then_inc(ssx_ready, 1)
                act.wait_ge(var_x, g + 1)
                act.activation(rsx[:, GT * g:GT * g + GT], rsx[:, GT * g:GT * g + GT], ACT.Sqrt).then_inc(std_x, 1)

            def hT_drains(g):
                act.wait_ge(gsm_ready, 2)
                for b in range(0, KB, 2):
                    wait_filled(act, "hT", g, b)
                    s = seq(g)
                    drain(act.activation(hT[:, b, GW * g:GW * (g + 1)], bank("hT", g, b), ACT.Identity,
                                         bias=modT[:, 0, 16 * s + b:16 * s + b + 1], scale=gsm[:, s, b:b + 1]),
                          "hT", g, b)

            x_stats(0)
            x_stats(1)
            hT_drains(0)
            x_stats(2)
            hT_drains(1)
            hT_drains(2)
            for t in range(NT):
                wait_filled(act, "zv", t)
                drain(act.activation(v[:, t, :], bank("zv", t)[:, 0:SGU_W], ACT.Gelu_apprx_tanh), "zv", t)
            act.wait_ge(var_v, 1)
            act.activation(ssv[:, :], ssv[:, :], ACT.Sqrt).then_inc(std_v, 1)
            for kind, i, _ in conv_blocks():
                for g in range(NG):
                    cols = slice(GW * g, GW * (g + 1))
                    if kind == "zc":
                        wait_filled(act, "zc", i, g)
                        if i:
                            wait_drained(act, "za", i - 1, g)
                        drain(act.activation(zc_sb[:, cols], bank("zc", i, g), ACT.Copy), "zc", i, g)
                    if kind == "zf":
                        wait_filled(act, "zf", i, g)
                        drain(act.activation(zfT[:, i, cols], bank("zf", i, g), ACT.Copy), "zf", i, g)
                    if kind == "zu":
                        wait_filled(act, "zu", i, g)
                        drain(act.activation(Y[:, 5 + i, cols], bank("zu", i, g), ACT.Gelu_apprx_tanh), "zu", i, g)
                if kind == "zf" and i == 1:
                    for t in range(1, NT, 2):
                        wait_filled(act, "ab", t)
                        drain(act.activation(AB[:, t, :, :, :].rearrange("p a b c -> p (a b c)"), bank("ab", t),
                                             ACT.Copy), "ab", t)
            last = None
            for s, half in ((0, S_P // 2), (1, S_S // 2)):
                for fb in range(2):
                    wait_filled(act, "even", s, fb)
                    if last:
                        wait_drained(act, *last)
                    else:
                        wait_drained(act, "sv", 2, NG - 1)
                    drain(act.activation(e_sb[:, 0:half], bank("even", s, fb)[:, 0:half], ACT.Copy), "even", s, fb)
                    if not last:
                        act.wait_ge(wo_in, 16)
                        for b in range(KB):
                            act.activation(wo[:, b, :], wo[:, b, :], ACT.Copy,
                                           scale=VT[:, V_GGRP + b:V_GGRP + b + 1]).then_inc(wo_ready, 1)
                    last = ("odd", s, fb)
            wait_drained(act, "odd", 1, 1)
            for n, (b, dst, adds) in enumerate(
                    ((0, SQ[:, 0, :], 0), (1, sqt[0][:, :], 0), (2, sqt[1][:, :], 0), (3, SQ[:, 1, :], 0),
                     (4, sqt[0][:, :], 1), (5, SQ[:, 2, :], 1), (6, sqt[1][:, :], 2), (7, sqt[0][:, :], 3))):
                if adds:
                    act.wait_ge(sq_added, adds)
                act.activation(dst, Y[:, b, :], ACT.Square).then_inc(sq_done, 1)
            act.wait_ge(var_y, 3)
            act.activation(rsy[:, :, :], rsy[:, :, :], ACT.Sqrt).then_inc(std_y, 1)
            act.wait_ge(rsy_ready, 1)

            def h2T_drains(g):
                for b in range(0, KB, 2):
                    wait_filled(act, "h2T", g, b)
                    if g and not b:
                        wait_filled(act, "lg", g - 1)
                    drain(act.activation(h2T[:, b, :], bank("h2T", g, b), ACT.Copy), "h2T", g, b)
                wait_filled(act, "lg", g)
                if not g:
                    act.wait_ge(lgt_zero, 1)
                drain(act.activation(lgT[32 * g:32 * g + NE, :], bank("lg", g)[0:NE, :], ACT.Copy), "lg", g)

            for t in range(NT):
                for h in range(2):
                    wait_filled(act, "out", t, h, 0)
                    if t >= 2:
                        act.wait_ge(x2_out[t % 2], 16 * (t // 2))
                    drain(act.activation(x2[:, t % 2, GW * h:GW * (h + 1)], bank("out", t, h, 0), ACT.Copy,
                                         scale=rsy[:, t, 0:1]), "out", t, h, 0)
                if t in (4, 8):
                    h2T_drains(t // 4 - 1)
                act.wait_ge(x2_ready, t + 1)
                if t >= GT:
                    act.wait_ge(h2_out[t % GT], 16 * (t // GT))
                act.activation(h2[:, t % GT, :], x2[:, t % 2, :], ACT.Square, accum_out=ss2[:, t:t + 1]
                               ).then_inc(ss2_ready, 1)
                act.wait_ge(var_2, t + 1)
                act.activation(rs2[:, t:t + 1], rs2[:, t:t + 1], ACT.Sqrt).then_inc(std_2, 1)
            h2T_drains(2)
            act.wait_ge(exp_in, 1)
            act.activation(L2[:, :, :, :], L2[:, :, :, :], ACT.Exp).then_inc(exp_out, 1)

            def split(e, j, free=None):
                act.wait_ge(raw_in[j % RAW], e * (16 * N_CH // RAW) + 16 * (j // RAW + 1))
                if free:
                    act.wait_ge(*free)
                act.activation(whi[:, j % SPL, :], raw[:, j % RAW, :], ACT.Copy).then_inc(w_hi, 1)

            def tokens_hi(e):
                for k in range(4):
                    act.wait_ge(t_filled, e * 4 + (k + 1))
                    act.activation(xT[:, 2 * k:2 * k + 2, 0:CAP],
                                   ps[:, k, 0:2 * CAP].rearrange("p (a n) -> p a n", a=2), ACT.Copy).then_inc(t_hi, 1)

            def hidden_hi(e, f):
                act.wait_ge(hid_done, e * FB + (f + 1))
                act.activation(hid[:, f, 0:CAP], hidf[:, f % 2, :], ACT.Copy).then_inc(hid_hi, 1)

            def expert(e, last=False):
                for f in range(FB):
                    b = 2 * (f % 2)
                    act.wait_ge(gu_filled, e * FB + (f + 1))
                    act.activation(gu_l[:, f % 2, :, :], ps[:, b:b + 2, CAP:2 * CAP], ACT.Copy).then_inc(lo_copied, 1)
                    if f:
                        hidden_hi(e, f - 1)
                    split(e, f + 4)
                    act.wait_ge(gu_summed, e * FB + (f + 1))
                    act.activation(sg[:, f % 2, :], gu[:, f % 2, 0, :], ACT.Silu).then_inc(silu_done, 1)
                hidden_hi(e, FB - 1)
                if not last:
                    for i in range(2):
                        split(e + 1, i)
                    tokens_hi(e + 1)
                    for i in range(2):
                        split(e + 1, 2 + i, (d_used, e * 4 + (i + 1)))
                act.wait_ge(d_used, e * 4 + 4)
                act.activation(ysl[0:CAP_S, :].rearrange("p (a n) -> p a n", a=2), ps[CAP_S:2 * CAP_S, 6:8, :],
                               ACT.Copy).then_inc(ysl_copied, 1)

            act.wait_ge(routed, 2)
            for i in range(4):
                split(0, i)
            tokens_hi(0)
            with act.Fori(0, NE - 1) as e:
                expert(e)
            expert(NE - 1, last=True)

            for t in range(NT):
                act.wait_ge(fin_in[t % 8], 16 * (t // 8 + 1))
                if t:
                    act.wait_ge(ssf_ready, t)
                act.activation(fjunk[:, :], fin[:, t % 8, :], ACT.Square, accum_out=ssf[:, t:t + 1]
                               ).then_inc(ssf_ready, 1)
                act.wait_ge(var_f, t + 1)
                act.activation(rsf[:, t:t + 1], rsf[:, t:t + 1], ACT.Sqrt).then_inc(std_f, 1)

        @block.tensor
        def _(pe):
            order = [0]

            def open_bank(*key):
                n = index[key]
                assert n == order[0], (key, n, order[0])
                order[0] += 1
                if n >= 8:
                    wait_drained(pe, *jobs[n - 8][0])
                return ps[:, n % 8, :]

            def fill(ins):
                ins.then_inc(bank_filled, 1)

            def ada(c):
                pe.wait_ge(ada_in[c % 2], 16 * (c // 2 + 1))
                out = open_bank("ada", c)
                for b in range(KB):
                    mm = pe.matmul(out[0:2, 0:ADA_C], silc[:, b:16:KB], ada_w[:, c % 2, b, :],
                                   start=b == 0, stop=b == KB - 1)
                fill(mm)

            def mod(g):
                pe.wait_ge(modrow_in[g], 32)
                out = open_bank("mod", g)
                fill(pe.transpose(out[:, 0:32], modrow[0:32, g, :], ident[0:32, 0:32]))

            pe.wait_ge(rows_in, 16 * 6)
            pe.wait_ge(small_in, 16 * 3)
            out = open_bank("vec")
            fill(pe.transpose(out[:, 0:V_N], rows[0:V_N, :], ident[0:V_N, 0:V_N]))
            pe.wait_ge(silc_ready, 1)
            for c in range(GRP_C):
                ada(c)
            mod(0)
            for g in range(NG):
                pe.wait_ge(xn_ready, GT * (g + 1))
                for b in range(KB):
                    out = open_bank("hT", g, b)
                    for t in range(GT):
                        tr = pe.transpose(out[:, P * t:P * (t + 1)], xg[:, g % 2, t, P * b:P * (b + 1)], ident[:, :])
                    fill(tr)
            pe.wait_ge(wsp_in, 16)
            for n, heads in enumerate((range(4), range(4, N_SGU))):
                out = open_bank("wsp", n)
                for i, h in enumerate(heads):
                    tr = pe.transpose(out[:, P * i:P * (i + 1)], wsp6[:, h, :], ident[:, :])
                fill(tr)
            pe.wait_ge(wv_in, 16)
            for b in (KB - 2, KB - 1):
                wait_drained(pe, "hT", NG - 1, b)
            for t in range(NT):
                out = open_bank("zv", t)
                for b in range(KB):
                    mm = pe.matmul(out[:, 0:SGU_W], hT[:, b, P * t:P * (t + 1)], wv[:, b, :],
                                   start=b == 0, stop=b == KB - 1)
                fill(mm)
            for n, (kind, i, _) in enumerate(conv_blocks()):
                if n in (3, 6):
                    for c in range(GRP_C * (n // 3), GRP_C * (n // 3 + 1)):
                        ada(c)
                if n == 9:
                    mod(1)
                    mod(2)
                pe.wait_ge(wi_in[n % 3], 16 * (n // 3 + 1))
                for g in range(NG):
                    out = open_bank(kind, i, g)
                    for b in range(KB):
                        mm = pe.matmul(out, wi[:, n % 3, b, :], hT[:, b, GW * g:GW * (g + 1)],
                                       start=b == 0, stop=b == KB - 1)
                    fill(mm)
                if n == 10:
                    wait_drained(pe, "zf", 1, NG - 1)
                    for t in range(NT):
                        s, tt = (0, t) if t < 8 else (1, t - 8)
                        half = (4, 2)[s]
                        first = S_P * s + 2 * P * (tt % half) + tt // half
                        out = open_bank("ab", t)
                        for fb in range(2):
                            mm = pe.matmul(out[:, 2 * P * fb:2 * P * (fb + 1)], zfT[:, fb, first:first + 2 * P - 1:2],
                                           chs[:, :, :].rearrange("p a n -> p (a n)"), start=True, stop=True)
                        fill(mm)
            pe.wait_ge(v_ready, NT)
            wait_drained(pe, "wsp", 1)
            for i in range(3):
                for g in range(NG):
                    out = open_bank("sv", i, g)
                    for t in range(GT):
                        for q in range(2):
                            h = 2 * i + q
                            mm = pe.matmul(out[HD * q:HD * (q + 1), P * t:P * (t + 1)],
                                           v[:, GT * g + t, HD * h:HD * (h + 1)], wspT[:, h, :], start=True, stop=True)
                    fill(mm)
            pe.wait_ge(dft_in, 32)
            wait_drained(pe, "ab", NT - 1)
            wait_drained(pe, "ab", NT - 2)
            for s, mats in ((0, dftp), (1, dfts)):
                half, tiles = (S_P // 2, S_S // 2)[s], (4, 2)[s]
                for fb in range(2):
                    for par, name in enumerate(("even", "odd")):
                        out = open_bank(name, s, fb)
                        for n in range(2 * tiles):
                            m, ab = par * tiles + n // 2, n % 2
                            mm = pe.matmul(out[:, 0:half], AB[:, 8 * s + m, fb, ab, :], mats[:, m, ab, :],
                                           start=n == 0, stop=n == 2 * tiles - 1)
                        fill(mm)
            pe.wait_ge(sq_added, 5)
            pe.wait_ge(ones_set, 1)
            for t in range(NT):
                out = open_bank("ssq", t)
                for k in range(3):
                    mm = pe.matmul(out[:, P * k:P * (k + 1)], SQ[:, k, P * t:P * (t + 1)], ones[:, :],
                                   start=True, stop=True)
                fill(mm)

            def router(g):
                pe.wait_ge(h2_ready, GT * (g + 1))
                for b in range(KB):
                    out = open_bank("h2T", g, b)
                    for t in range(GT):
                        tr = pe.transpose(out[:, P * t:P * (t + 1)], h2[:, t, P * b:P * (b + 1)], ident[:, :])
                    fill(tr)
                out = open_bank("lg", g)
                wait_drained(pe, "h2T", g, KB - 2)
                wait_drained(pe, "h2T", g, KB - 1)
                for b in range(KB):
                    mm = pe.matmul(out[0:NE, :], wrt[:, b, :], h2T[:, b, :], start=b == 0, stop=b == KB - 1)
                fill(mm)

            pe.wait_ge(wo_ready, KB)
            for t in range(NT):
                for h in range(2):
                    for k, blocks in enumerate((range(0, 3), range(3, 5), range(5, 8))):
                        out = open_bank("out", t, h, k)
                        for b in blocks:
                            mm = pe.matmul(out, Y[:, b, P * t:P * (t + 1)], wo[:, b, GW * h:GW * (h + 1)],
                                           start=b == blocks[0], stop=b == blocks[-1])
                        fill(mm)
                if t in (4, 8):
                    router(t // 4 - 1)
            router(2)
            wait_drained(pe, "lg", NG - 1)
            out = open_bank("lt")
            for t in range(GT):
                tr = pe.transpose(out[:, 96 * t:96 * (t + 1)], lgT[0:96, P * t:P * (t + 1)], ident[0:96, 0:96])
            fill(tr)
            pe.wait_ge(aff_ready, 1)
            for n in range(2):
                out = open_bank("aff", n)
                for t in range(GT):
                    tr = pe.transpose(out[0:2 * ROW_S, P * t:P * (t + 1)], affm[:, GT * n + t, :], ident[:, :])
                fill(tr)
            pe.wait_ge(topk_ready, 1)
            out = open_bank("idx")
            pe.transpose(out[:, 0:64], vals[0:64, :], ident[0:64, 0:64])
            fill(pe.transpose(out[:, 64:128], idxf[0:64, :], ident[0:64, 0:64]))

            def tokens(e):
                pe.wait_ge(xe_in, e * 32 + 32)
                for k in range(4):
                    for i in range(2):
                        cols = slice(P * (2 * k + i), P * (2 * k + i + 1))
                        pe.transpose(ps[:, k, CAP * i:CAP * i + CAP_P], xe[:, 0, cols], ident[:, :])
                        tr = pe.transpose(ps[:, k, CAP * i + CAP_P:CAP * (i + 1)], xe[0:CAP_S, 1, cols],
                                          ident[0:CAP_S, 0:CAP_S])
                    tr.then_inc(t_filled, 1)

            def product(out, slot, f):
                for k in range(KB):
                    w = slice(CW * k + P * (f % 2), CW * k + P * (f % 2) + P)
                    if k:
                        pe.matmul(out[:, 0:CAP], wlo[:, slot, w], xT[:, k, 0:CAP], start=False, stop=False,
                                  skip_group_check=True)
                    mm = pe.matmul(out[:, 0:2 * CAP], whi[:, slot, w], xT[:, k, :], start=k == 0, stop=k == KB - 1,
                                   skip_group_check=True)
                    if not k:
                        pe.matmul(out[:, 0:CAP], wlo[:, slot, w], xT[:, k, 0:CAP], start=False, stop=False,
                                  skip_group_check=True)
                return mm

            def down(e, k):
                for f in (2 * k, 2 * k + 1):
                    part = slice(0, CAP_P), slice(2 * CAP - CAP_P, 2 * CAP)
                    start, stop = f == 0, f == FB - 1
                    for n in range(2):
                        w = slice(D * (f % 2) + GW * n, D * (f % 2) + GW * (n + 1))
                        pe.matmul(ps[:, 4 + n, :], hid[:, f, part[0]], whi[:, (8 + k) % SPL, w], start=start, stop=False)
                        pe.matmul(ps[:, 4 + n, :], hid[:, f, part[0]], wlo[:, (8 + k) % SPL, w], start=False, stop=False)
                    for n in range(2):
                        w = slice(D * (f % 2) + GW * n, D * (f % 2) + GW * (n + 1))
                        pe.matmul(ps[:, 4 + n, :], hid[:, f, part[1]], whi[:, (8 + k) % SPL, w], start=False, stop=stop)
                    both = hid[:, f, CAP_P:CAP_P + 2 * CAP_S]
                    for n in range(2):
                        w = slice(D * (f % 2) + GW * n, D * (f % 2) + GW * (n + 1))
                        pe.matmul(ps[:, 6 + n, :], both, whi[:, (8 + k) % SPL, w], start=start, stop=False)
                        mm = pe.matmul(ps[:, 6 + n, :], both, wlo[:, (8 + k) % SPL, w], start=False, stop=stop)
                mm.then_inc(d_used, 1)

            def expert(e, last=False):
                for f in range(FB):
                    c, b = f // 2, 2 * (f % 2)
                    if f == 0:
                        pe.wait_ge(t_lo, e * 4 + 4)
                    if f >= 2:
                        pe.wait_ge(gu_summed, e * FB + (f - 1))
                    if f % 2 == 0:
                        pe.wait_ge(w_split, e * N_CH + (2 * c + 1))
                    product(ps[:, b, :], 2 * c % SPL, f)
                    if f % 2 == 0:
                        pe.wait_ge(w_split, e * N_CH + (2 * c + 2))
                    product(ps[:, b + 1, :], (2 * c + 1) % SPL, f).then_inc(gu_filled, 1)
                for k in range(4):
                    pe.wait_ge(w_split, e * N_CH + (9 + k))
                    pe.wait_ge(hid_lo, e * (2 * FB) + (4 * k + 4))
                    if k == 0:
                        pe.wait_ge(ye_sum, e * 1 + 1)
                    down(e, k)
                    if k == 1 and not last:
                        pe.wait_ge(gu_summed, e * FB + FB)
                        tokens(e + 1)

            wait_drained(pe, "idx")
            tokens(0)
            with pe.Fori(0, NE - 1) as e:
                expert(e)
            expert(NE - 1, last=True)

        @block.vector
        def _(dve):
            n_step = [0]

            def step(ins):
                ins.then_inc(dve_step, 1)
                n_step[0] += 1

            def after_step():
                dve.wait_ge(dve_step, n_step[0])

            def drain(ins, *key):
                assert drainer[key] == "dve"
                ins.then_inc(drained["dve"], 1)

            wait_filled(dve, "vec")
            drain(dve.tensor_copy(VT[:, :], bank("vec")[:, 0:V_N]), "vec")

            def x_norm(g):
                dve.wait_ge(ssx_ready, GT * (g + 1))
                r = rsx[:, GT * g:GT * (g + 1)]
                dve.tensor_scalar(r, ssx[:, GT * g:GT * (g + 1)], 1.0 / D, EPS, ALU.mult, ALU.add).then_inc(var_x, 1)
                dve.wait_ge(std_x, g + 1)
                step(dve.reciprocal(r, r))
                after_step()
                for t in range(GT):
                    x = xg[:, g % 2, t, :]
                    dve.tensor_scalar(x, x, rsx[:, GT * g + t:GT * g + t + 1], None, ALU.mult).then_inc(xn_ready, 1)

            def ada_drains(chunks):
                dve.wait_ge(brow_in, 32)
                for c in chunks:
                    if c % GRP_C == 0 and c:
                        dve.wait_ge(mod_out, 16 * (c // GRP_C))
                    wait_filled(dve, "ada", c)
                    cols = slice(ADA_C * (c % GRP_C), ADA_C * (c % GRP_C + 1))
                    drain(dve.tensor_tensor(stage[0:2, cols], bank("ada", c)[0:2, 0:ADA_C],
                                            brow[0:2, ADA_C * c:ADA_C * (c + 1)], ALU.add), "ada", c)

            def mod_drain(g):
                wait_filled(dve, "mod", g)
                drain(dve.tensor_copy(modT[:, g, :], bank("mod", g)[:, 0:32]), "mod", g)

            def hT_drains(g):
                s = seq(g)
                for b in range(1, KB, 2):
                    wait_filled(dve, "hT", g, b)
                    drain(dve.tensor_scalar(hT[:, b, GW * g:GW * (g + 1)], bank("hT", g, b), gsm[:, s, b:b + 1],
                                            modT[:, 0, 16 * s + b:16 * s + b + 1], ALU.mult, ALU.add), "hT", g, b)

            x_norm(0)
            ada_drains(range(4))
            x_norm(1)
            ada_drains(range(4, GRP_C))
            mod_drain(0)
            wait_drained(dve, "mod", 0)
            for s in range(2):
                dve.scalar_tensor_tensor(out=gsm[:, s, :], in0=modT[:, 0, 16 * s + 8:16 * s + 16], scalar=1.0,
                                         in1=VT[:, V_GMIX:V_GMIX + KB], op0=ALU.add, op1=ALU.mult).then_inc(gsm_ready, 1)
            dve.wait_ge(gsm_ready, 2)
            hT_drains(0)
            x_norm(2)
            hT_drains(1)
            hT_drains(2)
            for n, (h0, h1) in enumerate(((0, 4), (4, N_SGU))):
                wait_filled(dve, "wsp", n)
                drain(dve.tensor_copy(wspT[:, h0:h1, :].rearrange("p a n -> p (a n)"),
                                      bank("wsp", n)[:, 0:P * (h1 - h0)]), "wsp", n)
            for col in (0, S_P + 1, S_P + 2, TOK + 3):
                dve.memset(a_pad[:, col:col + 1], 0.0).then_inc(pads_set, 1)
            for t in range(NT):
                wait_drained(dve, "zv", t)
                if t:
                    after_step()
                step(dve.tensor_tensor_reduce(vjunk[:, :], v[:, t, :], v[:, t, :], 1.0, 0.0, ALU.mult, ALU.add,
                                              ssv[:, t:t + 1]))
            after_step()
            dve.tensor_scalar(ssv[:, :], ssv[:, :], 1.0 / SGU_W, EPS, ALU.mult, ALU.add).then_inc(var_v, 1)
            dve.wait_ge(std_v, 1)
            step(dve.reciprocal(ssv[:, :], ssv[:, :]))
            after_step()
            for t in range(NT):
                dve.tensor_scalar(v[:, t, :], v[:, t, :], ssv[:, t:t + 1], None, ALU.mult).then_inc(v_ready, 1)
            dve.wait_ge(pads_set, 4)
            for n, (kind, i, _) in enumerate(conv_blocks()):
                if n in (3, 6):
                    ada_drains(range(GRP_C * (n // 3), GRP_C * (n // 3 + 1)))
                if n == 9:
                    mod_drain(1)
                    mod_drain(2)
                for g in range(NG):
                    off = 1 + GW * g + (2 if g == 2 else 0)
                    cols = slice(GW * g, GW * (g + 1))
                    if kind == "za":
                        wait_filled(dve, "za", i, g)
                        wait_drained(dve, "zc", i, g)
                        drain(dve.tensor_tensor(a_pad[:, off:off + GW], bank("za", i, g), zc_sb[:, cols], ALU.mult),
                              "za", i, g)
                    if kind == "zb":
                        wait_filled(dve, "zb", i, g)
                        drain(dve.tensor_tensor(Y[:, i, cols], bank("zb", i, g), cv[:, off:off + GW], ALU.mult),
                              "zb", i, g)
                if kind == "za":
                    wait_drained(dve, "za", i, NG - 1)
                    n_c = TOK + 2
                    w = [VT[:, V_CONV + 3 * k + i:V_CONV + 3 * k + i + 1] for k in range(3)]
                    step(dve.tensor_scalar(cv[:, 1:1 + n_c], a_pad[:, 1:1 + n_c], w[1], None, ALU.mult))
                    for k in (0, 2):
                        after_step()
                        step(dve.scalar_tensor_tensor(out=cv[:, 1:1 + n_c], in0=a_pad[:, k:k + n_c], scalar=w[k],
                                                      in1=cv[:, 1:1 + n_c], op0=ALU.mult, op1=ALU.add))
                    after_step()
                if n == 10:
                    for t in range(0, NT, 2):
                        wait_filled(dve, "ab", t)
                        drain(dve.tensor_copy(AB[:, t, :, :, :].rearrange("p a b c -> p (a b c)"), bank("ab", t)),
                              "ab", t)
            dve.wait_ge(bsp_in, 16 * N_SGU)
            for i in range(3):
                for g in range(NG):
                    cols = slice(GW * g, GW * (g + 1))
                    wait_filled(dve, "sv", i, g)
                    if i or g:
                        wait_drained(dve, *[("sv", i, g - 1), ("sv", i - 1, NG - 1)][g == 0])
                    step(dve.scalar_tensor_tensor(
                        out=svt[:, :].rearrange("p (a n) -> p a n", a=GT),
                        in0=bank("sv", i, g).rearrange("p (a n) -> p a n", a=GT),
                        scalar=VT[:, V_GSGU + i:V_GSGU + i + 1],
                        in1=bsp[:, i:i + 1, :].to_broadcast([P, GT, P]), op0=ALU.mult, op1=ALU.add))
                    after_step()
                    wait_drained(dve, "zu", i, g)
                    drain(dve.tensor_tensor(Y[:, 5 + i, cols], Y[:, 5 + i, cols], svt[:, :], ALU.mult), "sv", i, g)
            for s, half in ((0, S_P // 2), (1, S_S // 2)):
                for fb in range(2):
                    wait_filled(dve, "odd", s, fb)
                    wait_drained(dve, "even", s, fb)
                    o = bank("odd", s, fb)[:, 0:half]
                    step(dve.tensor_tensor(Y[:, 3 + fb, S_P * s:S_P * s + half], o, e_sb[:, 0:half], ALU.add))
                    drain(dve.tensor_tensor(Y[:, 3 + fb, S_P * s + half:S_P * s + 2 * half], e_sb[:, 0:half], o,
                                            ALU.subtract), "odd", s, fb)
            dve.memset(lgT[:, :], 0.0).then_inc(lgt_zero, 1)
            for n, (k, i, need) in enumerate(((0, 0, 2), (0, 1, 3), (1, 0, 5), (2, 1, 7), (2, 0, 8))):
                dve.wait_ge(sq_done, need)
                if n:
                    dve.wait_ge(sq_added, n)
                dve.tensor_tensor(SQ[:, k, :], SQ[:, k, :], sqt[i][:, :], ALU.add).then_inc(sq_added, 1)
            for t in range(NT):
                wait_filled(dve, "ssq", t)
                drain(dve.tensor_copy(ssy[:, t, :], bank("ssq", t)[:, 0:3 * P:P]), "ssq", t)
            wait_drained(dve, "ssq", NT - 1)
            for k, width in enumerate((CONV_W, FOUR_W, SGU_W)):
                dve.tensor_scalar(rsy[:, :, k:k + 1], ssy[:, :, k:k + 1], 1.0 / width, EPS, ALU.mult, ALU.add
                                  ).then_inc(var_y, 1)
            dve.wait_ge(std_y, 1)
            dve.reciprocal(rsy[:, :, :], rsy[:, :, :]).then_inc(rsy_ready, 1)
            dve.wait_ge(rsy_ready, 1)
            dve.wait_ge(ffn_in, 16 * 5)
            for s in range(2):
                step(dve.scalar_tensor_tensor(out=gsf_b[:, s, :], in0=gsf_b[:, s, :], scalar=1.0, in1=gffn_b[:, :],
                                              op0=ALU.add, op1=ALU.mult))
            dve.wait_ge(gtm_in, 32)

            def h2T_drains(g):
                for b in range(1, KB, 2):
                    wait_filled(dve, "h2T", g, b)
                    if g and b == 1:
                        wait_filled(dve, "lg", g - 1)
                    drain(dve.tensor_copy(h2T[:, b, :], bank("h2T", g, b)), "h2T", g, b)

            for t in range(NT):
                s = seq(t // GT)
                for h in range(2):
                    cols = slice(GW * h, GW * (h + 1))
                    o = x2[:, t % 2, cols]
                    for k in (1, 2):
                        wait_filled(dve, "out", t, h, k)
                        wait_drained(dve, "out", t, h, k - 1)
                        drain(dve.scalar_tensor_tensor(out=o, in0=bank("out", t, h, k), scalar=rsy[:, t, k:k + 1],
                                                       in1=o, op0=ALU.mult, op1=ALU.add), "out", t, h, k)
                    wait_drained(dve, "out", t, h, 2)
                    step(dve.tensor_tensor(o, o, gtm_b[:, s, cols], ALU.mult))
                dve.wait_ge(xr_in[t % 2], 16 * (t // 2 + 1))
                after_step()
                dve.tensor_tensor(x2[:, t % 2, :], x2[:, t % 2, :], xr[:, t % 2, :], ALU.add).then_inc(x2_ready, 1)
                if t in (4, 8):
                    h2T_drains(t // 4 - 1)
                dve.wait_ge(ss2_ready, t + 1)
                dve.tensor_scalar(rs2[:, t:t + 1], ss2[:, t:t + 1], 1.0 / D, EPS, ALU.mult, ALU.add).then_inc(var_2, 1)
                dve.wait_ge(std_2, t + 1)
                step(dve.reciprocal(rs2[:, t:t + 1], rs2[:, t:t + 1]))
                after_step()
                hh = h2[:, t % GT, :]
                step(dve.scalar_tensor_tensor(out=hh, in0=x2[:, t % 2, :], scalar=rs2[:, t:t + 1], in1=gsf_b[:, s, :],
                                              op0=ALU.mult, op1=ALU.mult))
                after_step()
                dve.tensor_tensor(hh, hh, shf_b[:, s, :], ALU.add).then_inc(h2_ready, 1)
            h2T_drains(2)
            wait_filled(dve, "lt")
            drain(dve.tensor_copy(L[:, :, :, :].rearrange("p a b c -> p (a b c)"), bank("lt")[:, 0:GT * NG * ROW_S]), "lt")
            wait_drained(dve, "lt")
            for t in range(GT):
                step(dve.tensor_reduce(smax[:, NG * t:NG * (t + 1)], L[:, t, :, 0:NE], AX.X, ALU.max))
            after_step()
            for n in range(NT):
                t, g = n // NG, n % NG
                ins = dve.tensor_scalar(L2[:, t, g, :], L[:, t, g, 0:NE], smax[:, n:n + 1], None, ALU.subtract)
                step(ins) if n < NT - 1 else ins.then_inc(exp_in, 1)
            step(dve.memset(affm[:, :, :], -1.0))
            dve.wait_ge(exp_out, 1)
            for t in range(GT):
                step(dve.tensor_reduce(smax[:, NG * t:NG * (t + 1)], L2[:, t, :, :], AX.X, ALU.add))
            after_step()
            step(dve.reciprocal(smax[:, :], smax[:, :]))
            after_step()
            for n in range(NT):
                t, g = n // NG, n % NG
                dst = affm[:, GT * g + t, 0:NE] if g < 2 else affm[:, t, ROW_S:ROW_S + NE]
                ins = dve.tensor_scalar(dst, L2[:, t, g, :], smax[:, n:n + 1], None, ALU.mult)
                step(ins) if n < NT - 1 else ins.then_inc(aff_ready, 1)
            for n in range(2):
                wait_filled(dve, "aff", n)
                drain(dve.tensor_copy(aff[0:64, GW * n:GW * (n + 1)], bank("aff", n)[0:64, :]), "aff", n)
            wait_drained(dve, "aff", 1)
            for n in range(CAP_P // 8):
                eight = slice(8 * n, 8 * n + 8)
                if n:
                    after_step()
                step(dve.max(vals[0:64, eight], aff[0:64, :]))
                after_step()
                step(dve.max_index(idxu[0:64, eight], vals[0:64, eight], aff[0:64, :]))
                step(dve.match_replace(aff[0:64, :], vals[0:64, eight], aff[0:64, :], -2.0))
            after_step()
            dve.tensor_copy(idxf[0:64, :], idxu[0:64, :]).then_inc(topk_ready, 1)
            wait_filled(dve, "idx")
            step(dve.tensor_copy(gates[:, :, :].rearrange("p a n -> p (a n)"), bank("idx")[:, 0:64]))
            dve.tensor_copy(rowid[:, 0, :], bank("idx")[:, 64:96]).then_inc(routed, 1)
            dve.tensor_scalar(rowid[:, 1, :], bank("idx")[:, 96:128], float(S_P), None, ALU.add).then_inc(routed, 1)
            dve.wait_ge(routed, 2)
            drain(dve.memset(smax[:, 0:1], 0.0), "idx")
            after_step()

            def split(e, j):
                dve.wait_ge(w_hi, e * N_CH + (j + 1))
                dve.tensor_tensor(wlo[:, j % SPL, :], raw[:, j % RAW, :], whi[:, j % SPL, :].bitcast(F32), ALU.subtract
                                  ).then_inc(w_split, 1)

            def tokens_lo(e):
                for k in range(4):
                    dve.wait_ge(t_hi, e * 4 + (k + 1))
                    dve.tensor_tensor(xT[:, 2 * k:2 * k + 2, CAP:2 * CAP],
                                      ps[:, k, 0:2 * CAP].rearrange("p (a n) -> p a n", a=2),
                                      xT[:, 2 * k:2 * k + 2, 0:CAP].bitcast(F32), ALU.subtract).then_inc(t_lo, 1)

            def hidden_lo(e, f):
                dve.wait_ge(hid_hi, e * FB + (f + 1))
                for dst, src in ((CAP, slice(CAP_P, CAP)), (CAP + CAP_S, slice(0, CAP_P))):
                    n = src.stop - src.start
                    dve.tensor_tensor(hid[:, f, dst:dst + n], hidf[:, f % 2, src], hid[:, f, src].bitcast(F32), ALU.subtract
                                      ).then_inc(hid_lo, 1)

            def outputs(e):
                dve.tensor_copy(gcur[:, :], gates[:, :, bass.ds(e, 1)].rearrange("p a b -> p (a b)")
                                ).then_inc(gate_cur, 1)
                dve.wait_ge(gate_cur, e + 1)
                dve.wait_ge(ye_free, e + 1)
                dve.wait_ge(d_used, e * 4 + 4)
                for n in range(2):
                    cols = slice(GW * n, GW * (n + 1))
                    dve.scalar_tensor_tensor(out=ye[:, 0, cols], in0=ps[:, 4 + n, :], scalar=gcur[:, 0:1],
                                             in1=gtf_b[:, 0, cols], op0=ALU.mult, op1=ALU.mult).then_inc(ye_ready, 1)
                dve.wait_ge(ysl_copied, e + 1)
                y = ye[0:CAP_S, 1, :]
                dve.tensor_tensor(y.rearrange("p (a n) -> p a n", a=2), ps[0:CAP_S, 6:8, :],
                                  ysl[0:CAP_S, :].rearrange("p (a n) -> p a n", a=2), ALU.add).then_inc(ye_sum, 1)
                dve.wait_ge(ye_sum, e + 2)
                dve.scalar_tensor_tensor(out=y, in0=y, scalar=gcur[0:CAP_S, 1:2], in1=gtf_b[0:CAP_S, 1, :],
                                         op0=ALU.mult, op1=ALU.mult).then_inc(ye_ready, 1)

            def expert(e, last=False):
                for f in range(FB):
                    b = 2 * (f % 2)
                    dve.wait_ge(lo_copied, e * FB + (f + 1))
                    dve.tensor_tensor(gu[:, f % 2, :, :], ps[:, b:b + 2, 0:CAP], gu_l[:, f % 2, :, :], ALU.add).then_inc(gu_summed, 1)
                    if f:
                        hidden_lo(e, f - 1)
                    split(e, f + 4)
                    dve.wait_ge(silu_done, e * FB + (f + 1))
                    dve.tensor_tensor(hidf[:, f % 2, :], sg[:, f % 2, :], gu[:, f % 2, 1, :], ALU.mult).then_inc(hid_done, 1)
                hidden_lo(e, FB - 1)
                if not last:
                    for i in range(2):
                        split(e + 1, i)
                    tokens_lo(e + 1)
                    for i in range(2):
                        split(e + 1, 2 + i)
                outputs(e)

            dve.memset(smax[:, 1:2], 0.0).then_inc(ye_sum, 1)
            dve.wait_ge(gtf_in, 32)
            for i in range(4):
                split(0, i)
            tokens_lo(0)
            with dve.Fori(0, NE - 1) as e:
                expert(e)
            expert(NE - 1, last=True)

            dve.wait_ge(gfin_in, 16)
            for t in range(NT):
                dve.wait_ge(ssf_ready, t + 1)
                r = rsf[:, t:t + 1]
                dve.tensor_scalar(r, ssf[:, t:t + 1], 1.0 / D, EPS, ALU.mult, ALU.add).then_inc(var_f, 1)
                dve.wait_ge(std_f, t + 1)
                dve.reciprocal(r, r).then_inc(rsf_ready, 1)
                dve.wait_ge(rsf_ready, t + 1)
                y = fin[:, t % 8, :]
                dve.scalar_tensor_tensor(out=y, in0=y, scalar=r, in1=gfin_b[:, :], op0=ALU.mult, op1=ALU.mult
                                         ).then_inc(fin_ready, 1)


_INS = ["x_prompt", "x_sample", "c_prompt", "c_sample", "w_ada", "b_ada", "g_mix", "w_in", "conv_w", "g_sgu",
        "w_spatial", "b_spatial", "g_grp", "w_out", "g_ffn", "w_router", "w_gate", "w_up", "w_down", "g_final"]
_OUTS = [(1, S_P, D), (1, S_S, D)]


def kernel(**inputs):
    import concourse.bacc as bacc
    from concourse.bass_utils import run_bass_kernel_spmd

    nc = bacc.Bacc("TRN2", target_bir_lowering=False, num_devices=1)
    sent, aps = {}, {}
    arrays = {name: np.ascontiguousarray(inputs[name]) for name in _INS} | dft_constants()
    for name, x in arrays.items():
        sent[f"in_{name}"] = x
        aps[name] = nc.dram_tensor(f"in_{name}", x.shape, mybir.dt.from_np(x.dtype), kind="ExternalInput").ap()
    outs = [nc.dram_tensor(f"out_{i}", s, F32, kind="ExternalOutput").ap() for i, s in enumerate(_OUTS)]
    encoder_kernel(nc, aps, *outs)
    r = run_bass_kernel_spmd(nc, [sent], core_ids=[0])
    return tuple(r.results[0][f"out_{i}"] for i in range(2))
```

```python
import numpy as np
import concourse.bass as bass
from concourse import mybir

P = 128
D = 1024
KB = D // P
W = (1024, 512)
BASE = (0, W[0])
TOK = sum(W)
NT = TOK // P
GT = 4
GW = GT * P
NG = tuple(w // GW for w in W)
TL = tuple(w // P for w in W)
T0 = (0, TL[0])
CONV_W, FOUR_W, SGU_W = 384, 256, 384
HD = 64
N_SGU = SGU_W // HD
COL = {"zb": 0, "zc": CONV_W, "za": 2 * CONV_W, "zf": 3 * CONV_W, "zu": 3 * CONV_W + FOUR_W,
       "zv": 3 * CONV_W + FOUR_W + SGU_W}
EPS = 1e-6
NE = 16
CAP_P, CAP_S = 2 * W[0] // NE, 2 * W[1] // NE
CAP = CAP_P + CAP_S
CAPS = (CAP_P, CAP_S)
N_ADA = 6 * D // GW
RS = 3
CW = 256
N_CH = 12
RAW = 4
SPL = 6
FB = D // P

F32, F32R, U32 = mybir.dt.float32, mybir.dt.float32r, mybir.dt.uint32
ACT = mybir.ActivationFunctionType
ALU = mybir.AluOpType
AX = mybir.AxisListType

V_C, V_GMIX, V_GGRP, V_CONV, V_GSGU, V_N = 0, 16, 24, 32, 41, 44


def z_steps(s):
    out, blocks, ada = [], 0, 4
    for i in range(3):
        out += [("zc", i), ("za", i), ("zb", i)]
    out += [("zv", 0), ("zv", 1), ("vt", 0), ("zv", 2), ("vt", 1), ("zf", 0), ("vt", 2), ("zf", 1), ("zu", 0),
            ("ab", 0), ("zu", 1), ("zu", 2)]
    if s:
        return out
    mixed = []
    for n, step in enumerate(out):
        mixed.append(step)
        blocks += step[0] in COL
        if 2 * (ada - 3) <= blocks and out[min(n + 1, len(out) - 1)][0] != "vt":
            mixed.append(("ada", ada))
            ada += 1
    assert ada == N_ADA
    return mixed


def weight_stream():
    out = [("ada", j, i) for j in range(4) for i in range(4)]
    for s in range(2):
        for kind, i in z_steps(s):
            if kind == "ada":
                out += [("ada", i, q) for q in range(4)]
            elif kind in COL:
                out.append(("wi", s, kind, i))
        if s == 0:
            out += [("wo", b) for b in range(KB - 1)] + [("dft", 0, 0), ("dft", 0, 1), ("wo", KB - 1)]
            out += [("dft", 0, m) for m in range(2, TL[0])]
        else:
            out += [("dft", 1, m) for m in range(TL[1])]
    return out


def bank_jobs():
    who = {"zc": "act", "za": "dve", "zb": "dve", "zf": "act", "zu": "act", "zv": "act", "vt": "dve"}
    jobs = [(("vec",), "dve")] + [(("ada", j), "dve") for j in range(4)] + [(("mod",), "dve")]

    def x_blocks(s):
        return [(("hT", s, g, b), "act" if b % 2 == 0 else "dve") for g in range(NG[s]) for b in range(KB)]

    def router(s, g):
        r = []
        for b in range(KB):
            r.append((("h2T", s, g, b), "act" if b % 2 == 0 else "dve"))
        return r + [(("lg", s, g), "act")]

    jobs += x_blocks(0) + [(("wsp", 0), "dve"), (("wsp", 1), "dve")]
    for s in range(2):
        for kind, i in z_steps(s):
            if kind == "ada":
                jobs.append((("ada", i), "dve"))
            elif kind == "ab":
                jobs += [(("ab", s, t), "act" if t % 2 else "dve") for t in range(TL[s])]
            else:
                jobs += [((kind, s, i, g), who[kind]) for g in range(NG[s])]
        if s:
            jobs.append((("idx", 0), "dve"))
        jobs += [(("sv", s, i, g), "dve") for i in range(3) for g in range(NG[s])]
        jobs += [(("even", s, fb), "act") for fb in range(2)] + [(("odd", s, fb), "dve") for fb in range(2)]
        for t in range(TL[s]):
            jobs += [(("out", s, t, k, h), "act" if k == 0 else "dve") for k in range(3) for h in range(2)]
            if t == 0:
                jobs.append((("ssq", s), "dve_sums"))
            if t == GT:
                jobs += router(s, 0)
        jobs += router(s, NG[s] - 1) + [(("lt", s), "dve")]
        if s == 0:
            jobs += x_blocks(1)
        jobs += [(("aff", s, g), "dve") for g in range(NG[s])]
    return jobs + [(("idx", 1), "dve")]


def dft_constants():
    def seq(s):
        half = s // 2
        n = np.arange(s).reshape(s // 256, P, 2)
        n = n.transpose(2, 0, 1).reshape(s // P, P)
        ang = 2 * np.pi * ((n[:, :, None] * np.arange(half)) % s) / s
        both = np.stack([np.cos(ang), -np.sin(ang)], 2) / np.sqrt(s * HD)
        return np.ascontiguousarray(both).astype(np.float32)

    ang = 2 * np.pi * (np.outer(np.arange(HD), np.arange(HD)) % HD) / HD
    head = np.zeros((P, 2, P))
    for q in range(2):
        head[HD * q:HD * (q + 1), 0, HD * q:HD * (q + 1)] = np.cos(ang)
        head[HD * q:HD * (q + 1), 1, HD * q:HD * (q + 1)] = np.sin(ang)
    return {"dft_0": seq(W[0]), "dft_1": seq(W[1]), "dft_head": head.astype(np.float32),
            "ident": np.eye(P, dtype=np.float32)}


def encoder_kernel(nc, a, y_p, y_s):
    K = 1024
    base = (nc.sbuf_base + 63) // 64 * 64

    def at(name, offset, shape, dt=F32):
        return nc.alloc_sbuf_tensor_at(name, [P] + shape, dt, offset=base + int(offset))

    def pair(name, offsets, shape, dt=F32):
        return [at(f"{name}{s}", offsets[s] * K, shape(W[s]), dt) for s in range(2)]

    hT = pair("hT", (0, 0), lambda w: [2, KB, w], F32R)
    Yhl = pair("Yhl", (0, 0), lambda w: [KB, 2, w], F32R)
    Y = pair("Y", (64, 64), lambda w: [KB, w])
    wring = pair("wring", (96, 40), lambda w: [RS, 2, D], F32R)
    silw = at("silw", 120 * K, [KB, P], F32R)
    stage = at("stage", 124 * K, [2, GW])
    wo = at("wo", 96 * K, [KB, 2, D], F32R)
    xg = pair("xg", (128, 32), lambda w: [w // GW, GT, D])
    ht_a = pair("ht_a", (160, 64), lambda w: [2, GW])
    ht_d = pair("ht_d", (164, 68), lambda w: [2, GW])
    xjunk = pair("xjunk", (168, 80), lambda w: [D])
    zc_sb = pair("zc_sb", (128, 80), lambda w: [w])
    a_pad = pair("a_pad", (132, 82), lambda w: [w + 2])
    cv = pair("cv", (137, 85), lambda w: [w])
    zfT = pair("zfT", (142, 88), lambda w: [2, w])
    vF = pair("vF", (150, 92), lambda w: [2, GW])
    vjunk = pair("vjunk", (132, 82), lambda w: [SGU_W])
    brow = at("brow", 76 * K, [GW])
    v = pair("v", (156, 160), lambda w: [w // P, SGU_W])
    AB = pair("AB", (168, 168), lambda w: [w // P, 2, 2, P])
    SQ = pair("SQ", (168, 168), lambda w: [3, w])
    sqt = [pair("sqt0", (180, 174), lambda w: [w]), pair("sqt1", (160, 160), lambda w: [w])]
    wraw = at("wraw", 184 * K, [RS, D])
    svt = at("svt", 196 * K, [GW])
    e_sb = at("e_sb", 196 * K, [GW])
    ada_lo = at("ada_lo", 196 * K, [GW])
    rows = at("rows", 196 * K, [P])
    gtm_b = at("gtm_b", 164 * K, [D])
    shf_b = at("shf_b", 168 * K, [D])
    gsf_b = at("gsf_b", 172 * K, [D])
    gffn_b = at("gffn_b", 176 * K, [D])
    h2T = at("h2T", 176 * K, [4, GW])
    xr = at("xr", 64 * K, [2, D])
    x2 = at("x2", 72 * K, [2, D])
    h2 = at("h2", 80 * K, [GT, D])
    lgT = at("lgT", 160 * K, [GW])
    L = at("L", 162 * K, [GT, 2, 32])
    L2 = at("L2", 163 * K, [GT, 2, NE])
    affm = at("affm", 163.5 * K, [TL[0], NE])
    aff = at("aff", 176 * K, [W[0]])
    vals = at("vals", 180 * K, [P])
    idxu = at("idxu", 180.5 * K, [P], U32)
    idxf = at("idxf", 181 * K, [P])
    wsp6 = at("wsp6", 172 * K, [N_SGU, P])
    xe = at("xe", 0, [2, D])
    xT = at("xT", 8 * K, [KB, 2 * CAP], F32R)
    hid = at("hid", 20 * K, [FB, 2 * CAP], F32R)
    raw = at("raw", 32 * K, [RAW, KB * CW])
    whi = at("whi", 64 * K, [SPL, KB * CW], F32R)
    wlo = at("wlo", 112 * K, [SPL, KB * CW], F32R)
    gu_l = at("gu_l", 160 * K, [2, 2, CAP])
    gu = at("gu", 163 * K, [2, 2, CAP])
    sg = at("sg", 166 * K, [2, CAP])
    hidf = at("hidf", 167.5 * K, [2, CAP])
    ye = at("ye", 170 * K, [2, D])
    gtf_b = at("gtf_b", 184 * K, [2, D])
    ysl = at("ysl", 192 * K, [D])
    gfin_b = at("gfin_b", 178 * K, [D])
    fin = at("fin", 32 * K, [NT, D])
    fjunk = at("fjunk", 80 * K, [D])
    top = [198 * K]

    def small(name, shape, dt=F32):
        t = at(name, top[0], shape, dt)
        n = 4
        for x in shape:
            n *= x
        top[0] += (n + 31) // 32 * 32
        return t

    ident = small("ident_sb", [P])
    ones = small("ones", [1])
    VT = small("VT", [V_N])
    silc = small("silc", [16])
    modrow = small("modrow", [P])
    modT = small("modT", [2, 16])
    gsm = small("gsm", [2, KB])
    ssx = small("ssx", [NT])
    rsx = small("rsx", [NT])
    ssv = small("ssv", [NT])
    ssy = small("ssy", [NT, 3])
    rsy = small("rsy", [NT, 3])
    ss2 = small("ss2", [NT])
    rs2 = small("rs2", [NT])
    ssf = small("ssf", [NT])
    rsf = small("rsf", [NT])
    wrt = small("wrt", [KB, NE])
    chs = small("chs", [2, P])
    wspT = small("wspT", [N_SGU, P])
    bsp = small("bsp", [3, P])
    gates = small("gates", [2, NE])
    rowid = small("rowid", [2, NE], U32)
    gcur = small("gcur", [2])
    icur = small("icur", [2], U32)
    iscat = small("iscat", [2], U32)
    smax = small("smax", [TL[0]])
    tick = small("tick", [2])
    assert base + top[0] <= nc.sbuf_usable_end, (base + top[0], nc.sbuf_usable_end)

    ps = nc.alloc_psum_tensor("ps", [P, 8, GW], F32)

    mod_d = nc.dram_tensor("mod_d", [2, 6 * D], F32).ap()
    h2_d = nc.dram_tensor("h2_d", [TOK, D], F32).ap()
    acc_d = nc.dram_tensor("acc_d", [TOK, D], F32).ap()

    sem = nc.alloc_semaphore

    def sems(*names):
        return [sem(n) for n in names]

    jobs = bank_jobs()
    index = {k: n for n, (k, _) in enumerate(jobs)}
    drainer = dict(jobs)
    nth = {}
    for who in ("act", "dve", "dve_sums"):
        nth |= {k: n + 1 for n, k in enumerate(k for k, w in jobs if w == who)}
    bank_filled = sem("bank_filled")
    drained = {"act": sem("bank_drained_by_act"), "dve": sem("bank_drained_by_dve"),
               "dve_sums": sem("bank_of_sums_drained")}

    def wait_filled(eng, *key):
        eng.wait_ge(bank_filled, index[key] + 1)

    def wait_drained(eng, *key):
        eng.wait_ge(drained[drainer[key]], nth[key])

    def bank(*key):
        return ps[:, index[key] % 8, :]

    stream = weight_stream()
    raw_n = {c: n for n, c in enumerate(stream)}
    split_n = {c: n for n, c in enumerate(c for c in stream if c[0] != "dft")}
    ring = [c for c in stream if c[0] in ("ada", "wi")]
    ring_n = {c: n for n, c in enumerate(ring)}
    first_s = min(n for n, c in enumerate(ring) if c[:2] == ("wi", 1))
    ada_parts = {c: n for n, c in enumerate(c for c in ring if c[0] == "ada" and c[2] < 3)}
    dft_n = {c: n for n, c in enumerate(c for c in stream if c[0] == "dft" and (c[2] + 1) % (TL[c[1]] // 2))}
    ws_in = [sem(f"ws_in{i}") for i in range(RS)]
    ws_hi, ws_lo, ada_part_used, dft_used = sems("ws_hi", "ws_lo", "ada_part_used", "dft_used")

    def slot_of(c):
        n = ring_n[c]
        return wring[0][:, n % RS, :, :] if n < first_s else wring[1][:, (n - first_s + 1) % RS, :, :]

    def wait_used(eng, c):
        if c in ada_parts:
            eng.wait_ge(ada_part_used, ada_parts[c] + 1)
        elif c[0] == "ada":
            wait_filled(eng, "ada", c[1])
        else:
            wait_filled(eng, c[2], c[1], c[3], NG[c[1]] - 1)

    def wait_h2t_slot(eng, s, g, b):
        n = T0[s] // GT + g
        if b >= 4:
            eng.wait_ge(lg_used, (KB - 1) * n + b - 3)
        elif n:
            wait_filled(eng, "lg", *((s, g - 1) if g else (s - 1, NG[s - 1] - 1)))

    def chunks_of(s, kind, i):
        return [("ada", i, q) for q in range(4)] if kind == "ada" else [("wi", s, kind, i)] if kind in COL else []

    rows_in, brow_in, small_in, wsp_in, bsp_in = sems("rows_in", "brow_in", "small_in", "wsp_in", "bsp_in")
    x_in = [sem(f"x_in{i}") for i in range(3)]
    mod_out, modrow_in, gtm_in, ffn_in, gtf_in = sems("mod_out", "modrow_in", "gtm_in", "ffn_in", "gtf_in")
    xr_in = [sem(f"xr_in{i}") for i in range(2)]
    x2_out, h2_out = [sem(f"x2_out{i}") for i in range(2)], [sem(f"h2_out{i}") for i in range(GT)]
    raw_in = [sem(f"raw_in{i}") for i in range(RAW)]
    gfin_in, fin_in, fin_out = sem("gfin_in"), [sem(f"fin_in{i}") for i in range(NT)], sem("fin_out")
    xe_in, scattered = sems("xe_in", "scattered")
    sp_tick, pool_tick = sems("sp_tick", "pool_tick")
    dve_step, act_step = sems("dve_step", "act_step")
    ones_set, silw_zero, silc_ready, silw_hi, silw_ready = sems(
        "ones_set", "silw_zero", "silc_ready", "silw_hi", "silw_ready")
    ssx_ready, var_x, std_x, xn_ready = sems("ssx_ready", "var_x", "std_x", "xn_ready")
    gsm_ready, ht_mod, hT_hi, hT_lo, ada_lo_ready = sems(
        "gsm_ready", "ht_mod", "hT_hi", "hT_lo", "ada_lo_ready")
    var_v, std_v, v_ready, pads_set = sems("var_v", "std_v", "v_ready", "pads_set")
    y_hi, y_lo, sq_done, sq_added, var_y, std_y, rsy_ready = sems(
        "y_hi", "y_lo", "sq_done", "sq_added", "var_y", "std_y", "rsy_ready")
    gsf_ready, x2_ready, ss2_ready, var_2, std_2, h2_ready = sems(
        "gsf_ready", "x2_ready", "ss2_ready", "var_2", "std_2", "h2_ready")
    lg_used, lgt_zero, exp_in, exp_out, aff_ready, topk_ready, routed = sems(
        "lg_used", "lgt_zero", "exp_in", "exp_out", "aff_ready", "topk_ready", "routed")
    w_hi, w_split = sems("w_hi", "w_split")
    t_filled, t_hi, t_lo = sems("t_filled", "t_hi", "t_lo")
    gu_filled, lo_copied, gu_summed = sems("gu_filled", "lo_copied", "gu_summed")
    silu_done, hid_done, hid_hi, hid_lo = sems("silu_done", "hid_done", "hid_hi", "hid_lo")
    d_used, ysl_copied, ye_sum, ye_ready, ye_free = sems("d_used", "ysl_copied", "ye_sum", "ye_ready", "ye_free")
    gate_cur, idx_cur = sems("gate_cur", "idx_cur")
    ssf_ready, var_f, std_f, rsf_ready, fin_ready = sems("ssf_ready", "var_f", "std_f", "rsf_ready", "fin_ready")

    x_of = (a["x_prompt"][0], a["x_sample"][0])
    seq_of = [0] * TL[0] + [1] * TL[1]

    def x_rows(tt):
        s = seq_of[tt]
        return x_of[s][P * (tt - T0[s]):P * (tt - T0[s] + 1), :]

    def out_rows(tt):
        s = seq_of[tt]
        return (y_p, y_s)[s][0, P * (tt - T0[s]):P * (tt - T0[s] + 1), :]

    w_in, w_ada, w_out = a["w_in"][0], a["w_ada"][0], a["w_out"][0]
    w_g = a["w_gate"][0].rearrange("e (k p) f -> e p k f", p=P)
    w_u = a["w_up"][0].rearrange("e (k p) f -> e p k f", p=P)
    w_d = a["w_down"][0].rearrange("e (k p) f -> e p k f", p=P)

    def load_chunk(eng, e, j):
        slot = raw[:, j % RAW, :]
        if j < 8:
            src = (w_g, w_u)[j % 2][e, :, :, CW * (j // 2):CW * (j // 2 + 1)]
            dst = slot.rearrange("p (k f) -> p k f", k=KB)
        else:
            src = w_d[e, :, 2 * (j - 8):2 * (j - 8) + 2, :]
            dst = slot.rearrange("p (k f) -> p k f", k=2)
        eng.dma_start(dst, src).then_inc(raw_in[j % RAW], 16)

    with nc.Block() as block:

        @block.sync
        def _(sp):
            for name, at_row, n in (("c_prompt", V_C, 8), ("c_sample", V_C + 8, 8), ("g_mix", V_GMIX, 8),
                                    ("g_grp", V_GGRP, 8), ("g_sgu", V_GSGU, 3)):
                sp.dma_start(rows[at_row:at_row + n, :], a[name].rearrange("a (b n) -> (a b) n", n=P)
                             ).then_inc(rows_in, 16)
            sp.dma_start(rows[V_CONV:V_CONV + 9, :], a["conv_w"].rearrange("a k (b n) -> (a k b) n", n=P)
                         ).then_inc(rows_in, 16)

            def load_stream(n):
                c = stream[n]
                if n >= RS:
                    before = stream[n - RS]
                    if before in dft_n:
                        sp.wait_ge(dft_used, dft_n[before] + 1)
                    elif before[0] == "dft":
                        wait_filled(sp, ("even", "odd")[2 * before[2] // TL[before[1]]], before[1], 1)
                    else:
                        sp.wait_ge(ws_lo, split_n[before] + 1)
                slot = wraw[:, n % RS, :]
                if c[0] == "ada":
                    _, j, q = c
                    src = w_ada[2 * P * q:2 * P * (q + 1), GW * j:GW * (j + 1)].rearrange("(k p) n -> p k n", p=P)
                    slot = slot.rearrange("p (k n) -> p k n", k=2)
                elif c[0] == "wi":
                    col = COL[c[2]] + P * c[3]
                    src = w_in[:, col:col + P].rearrange("(k p) n -> p k n", p=P)
                    slot = slot.rearrange("p (k n) -> p k n", k=KB)
                elif c[0] == "wo":
                    src = w_out[P * c[1]:P * (c[1] + 1), :]
                else:
                    src = a[f"dft_{c[1]}"][c[2]].rearrange("p a n -> p (a n)")
                    slot = slot[:, 0:W[c[1]]]
                sp.dma_start(slot, src).then_inc(ws_in[n % RS], 16)

            def load_x(s, g):
                sp.dma_start(xg[s][:, g, :, :], x_of[s][GW * g:GW * (g + 1), :].rearrange("(t p) d -> p t d", p=P)
                             ).then_inc(x_in[2 * s + g], 16)

            def load_xr(tt):
                sp.dma_start(xr[:, tt % 2, :], x_rows(tt)).then_inc(xr_in[tt % 2], 16)

            n_next = [0]

            def stream_until(c):
                stop = len(stream) if c is None else raw_n[c]
                while n_next[0] < stop:
                    load_stream(n_next[0])
                    n_next[0] += 1

            stream_until(("ada", 0, 3))
            load_x(0, 0)
            stream_until(("ada", 1, 2))
            load_x(0, 1)
            stream_until(("ada", 3, 0))
            for s in range(2):
                stream_until(None if s else ("wi", 1, "zc", 0))
                wait_filled(sp, "ssq", s)
                sp.wait_ge(y_lo, KB * (s + 1))
                load_xr(T0[s])
                load_xr(T0[s] + 1)
                for col, dst, arrived in ((2 * D, gtm_b, gtm_in), (3 * D, shf_b, ffn_in), (4 * D, gsf_b, ffn_in)):
                    sp.dma_start(dst[:, :], mod_d[s:s + 1, col:col + D].to_broadcast([P, D])).then_inc(arrived, 16)
                sp.dma_start(gffn_b[:, :], a["g_ffn"].to_broadcast([P, D])).then_inc(ffn_in, 16)
                if s == 0:
                    for n in range(RS):
                        load_stream(n_next[0])
                        n_next[0] += 1
                else:
                    for s2 in range(2):
                        sp.dma_start(gtf_b[:, s2, :], mod_d[s2:s2 + 1, 5 * D:6 * D].to_broadcast([P, D])
                                     ).then_inc(gtf_in, 16)
                    for j in range(RAW):
                        load_chunk(sp, 0, j)
                for t in range(TL[s]):
                    tt = T0[s] + t
                    sp.wait_ge(h2_ready, tt + 1)
                    sp.dma_start(acc_d[P * tt:P * (tt + 1), :], x2[:, tt % 2, :]).then_inc(x2_out[tt % 2], 16)
                    sp.dma_start(h2_d[P * tt:P * (tt + 1), :], h2[:, tt % GT, :]).then_inc(h2_out[tt % GT], 16)
                    if t + 2 < TL[s]:
                        load_xr(tt + 2)
                if s == 0:
                    wait_filled(sp, "out", 0, TL[0] - 1, 2, 1)
                    load_x(1, 0)

            with sp.Fori(0, NE - 1) as e:
                for j in range(N_CH):
                    sp.wait_ge(w_split, e * N_CH + (j + 1))
                    sp.sem_inc(sp_tick, 1)
                    if j < N_CH - RAW:
                        load_chunk(sp, e, j + RAW)
                    else:
                        load_chunk(sp, e + 1, j + RAW - N_CH)
            for j in range(N_CH - RAW):
                sp.wait_ge(w_split, (NE - 1) * N_CH + j + 1)
                load_chunk(sp, NE - 1, j + RAW)
            sp.dma_start(gfin_b[:, :], a["g_final"].rearrange("(a n) -> a n", a=1).to_broadcast([P, D])
                         ).then_inc(gfin_in, 16)

            sp.wait_ge(ye_free, NE + 1)
            for tt in range(NT):
                sp.dma_start(fin[:, tt, :], acc_d[P * tt:P * (tt + 1), :]).then_inc(fin_in[tt], 16)
            for tt in range(NT):
                sp.wait_ge(fin_ready, tt + 1)
                sp.dma_start(out_rows(tt), fin[:, tt, :]).then_inc(fin_out, 16)
            sp.wait_ge(fin_out, 16 * NT)

        @block.gpsimd
        def _(pool):
            pool.memset(ones[:, :], 1.0).then_inc(ones_set, 1)
            pool.memset(silw[:, :, :].bitcast(F32), 0.0).then_inc(silw_zero, 1)
            for h in range(N_SGU):
                pool.dma_start(bsp[HD * (h % 2):HD * (h % 2) + HD, h // 2, :],
                               a["b_spatial"][0, h:h + 1, :].to_broadcast([HD, P])).then_inc(bsp_in, 16)
            for j in range(N_ADA):
                cols = slice(GW * j, GW * (j + 1))
                if j:
                    wait_drained(pool, "ada", j - 1)
                for s in range(2):
                    pool.dma_start(brow[s:s + 1, :], a["b_ada"][0:1, cols]).then_inc(brow_in, 16)
                wait_drained(pool, "ada", j)
                pool.dma_start(mod_d[:, cols], stage[0:2, j % 2, :]).then_inc(mod_out, 16)
                if j == 3:
                    pool.wait_ge(mod_out, 16 * (j + 1))
                    for s in range(2):
                        pool.dma_start(modrow[16 * s:16 * s + 16, :],
                                       mod_d[s, 0:2 * D].rearrange("(j n) -> j n", n=P)).then_inc(modrow_in, 16)

            def gather(e, copies):
                pool.tensor_copy(icur[:, :], rowid[:, :, bass.ds(e, 1)].rearrange("p a b -> p (a b)")
                                 ).then_inc(idx_cur, 1)
                pool.wait_ge(idx_cur, copies)
                pool.sem_inc(pool_tick, 1)
                pool.indirect_dma_start(xe[:, 0, :], None, h2_d, bass.IndirectOffsetOnAxis(ap=icur[:, 0:1], axis=0)
                                        ).then_inc(xe_in, 16)
                pool.indirect_dma_start(xe[0:CAP_S, 1, :], None, h2_d,
                                        bass.IndirectOffsetOnAxis(ap=icur[0:CAP_S, 1:2], axis=0)
                                        ).then_inc(xe_in, 16)

            def scatter(e, copies):
                pool.tensor_copy(iscat[:, :], rowid[:, :, bass.ds(e, 1)].rearrange("p a b -> p (a b)")
                                 ).then_inc(idx_cur, 1)
                pool.wait_ge(idx_cur, copies)
                pool.wait_ge(ye_ready, e * 3 + 3)
                pool.sem_inc(pool_tick, 1)
                pool.indirect_dma_start(acc_d, bass.IndirectOffsetOnAxis(ap=iscat[:, 0:1], axis=0), ye[:, 0, :],
                                        None, compute_op=ALU.add).then_inc(scattered, 16)
                pool.indirect_dma_start(acc_d, bass.IndirectOffsetOnAxis(ap=iscat[0:CAP_S, 1:2], axis=0),
                                        ye[0:CAP_S, 1, :], None, compute_op=ALU.add).then_inc(scattered, 16)
                pool.wait_ge(scattered, e * 32 + 32)
                pool.nop().then_inc(ye_free, 1)

            pool.wait_ge(routed, 4)
            for i in range(2):
                pool.wait_ge(x2_out[i], 16 * NT // 2)
            for i in range(GT):
                pool.wait_ge(h2_out[i], 16 * NT // GT)
            pool.nop().then_inc(ye_free, 1)
            gather(0, 1)
            with pool.Fori(0, NE - 1) as e:
                pool.wait_ge(t_filled, e * 4 + 4)
                gather(e + 1, e * 2 + 2)
                scatter(e, e * 2 + 3)
            scatter(NE - 1, NE * 2)

        @block.scalar
        def _(act):
            n_step, n_split = [0], [0]

            def step(ins):
                ins.then_inc(act_step, 1)
                n_step[0] += 1

            def after_step():
                act.wait_ge(act_step, n_step[0])

            def drain(ins, *key):
                assert drainer[key] == "act"
                ins.then_inc(drained["act"], 1)

            def split_hi(c):
                n = raw_n[c]
                act.wait_ge(ws_in[n % RS], 16 * (n // RS + 1))
                if c[0] == "wo":
                    dst = wo[:, c[1], 0, :]
                    if c[1] == 3:
                        act.wait_ge(mod_out, 16 * N_ADA)
                    if c[1] == KB - 1:
                        wait_filled(act, "sv", 0, 2, NG[0] - 1)
                else:
                    dst = slot_of(c)[:, 0, :]
                    if ring_n[c] >= RS:
                        wait_used(act, ring[ring_n[c] - RS])
                act.activation(dst, wraw[:, n % RS, :], ACT.Copy).then_inc(ws_hi, 1)

            def split_ahead(chunks):
                last = ring_n[chunks[-1]] + 2
                end = len(ring) if ring_n[chunks[0]] >= first_s else first_s
                while n_split[0] <= min(last, end - 1):
                    split_hi(ring[n_split[0]])
                    n_split[0] += 1

            act.dma_start(ident[:, :], a["ident"]).then_inc(small_in, 16)
            act.dma_start(chs[:, :, :], a["dft_head"]).then_inc(small_in, 16)
            act.dma_start(wrt[:, :, :], a["w_router"][0].rearrange("(k p) n -> p k n", p=P)).then_inc(small_in, 16)
            act.dma_start(wsp6[:, :, :], a["w_spatial"][0].rearrange("h p q -> p h q")).then_inc(wsp_in, 16)
            wait_drained(act, "vec")
            act.activation(silc[:, :], VT[:, V_C:V_C + 16], ACT.Silu).then_inc(silc_ready, 1)
            act.wait_ge(silc_ready, 1)
            act.wait_ge(silw_zero, 1)
            act.activation(silw[:, :, 0:2], silc[:, :].rearrange("p (s k) -> p k s", s=2), ACT.Copy).then_inc(silw_hi, 1)

            def ada_drain(j):
                wait_filled(act, "ada", j)
                if j:
                    wait_drained(act, "ada", j - 1)
                act.activation(ada_lo[0:2, :], bank("ada", j)[64:66, :], ACT.Copy).then_inc(ada_lo_ready, 1)

            def x_stats(s, g):
                tt = T0[s] + GT * g
                act.wait_ge(x_in[2 * s + g], 16)
                if s:
                    for i in range(GT):
                        act.wait_ge(h2_out[i], 16 * TL[0] // GT)
                for t in range(tt, tt + GT):
                    if t:
                        act.wait_ge(ssx_ready, t)
                    act.activation(xjunk[s][:, :], xg[s][:, g, t % GT, :], ACT.Square,
                                   accum_out=ssx[:, t:t + 1]).then_inc(ssx_ready, 1)
                act.wait_ge(var_x, tt // GT + 1)
                act.activation(rsx[:, tt:tt + GT], rsx[:, tt:tt + GT], ACT.Sqrt).then_inc(std_x, 1)

            def hT_drains(s, g):
                act.wait_ge(gsm_ready, 2)
                cols = slice(GW * g, GW * (g + 1))
                n_even = (s * NG[0] + g) * KB // 2
                for b in range(KB):
                    i = n_even + b // 2
                    if b % 2:
                        act.wait_ge(ht_mod, i + 1)
                        act.activation(hT[s][:, 0, b, cols], ht_d[s][:, (b // 2) % 2, :], ACT.Copy).then_inc(hT_hi, 1)
                    else:
                        wait_filled(act, "hT", s, g, b)
                        if i >= 2:
                            act.wait_ge(hT_lo, i - 1)
                        tmp = ht_a[s][:, (b // 2) % 2, :]
                        step(act.activation(tmp, bank("hT", s, g, b), ACT.Identity, bias=modT[:, s, b:b + 1],
                                            scale=gsm[:, s, b:b + 1]))
                        after_step()
                        drain(act.activation(hT[s][:, 0, b, cols], tmp, ACT.Copy), "hT", s, g, b)

            def mixers(s):
                for kind, i in z_steps(s):
                    chunks = chunks_of(s, kind, i)
                    if chunks:
                        split_ahead(chunks)
                    if kind == "ada":
                        ada_drain(i)
                    for g in range(NG[s]):
                        cols = slice(GW * g, GW * (g + 1))
                        if kind == "zc":
                            wait_filled(act, "zc", s, i, g)
                            if i:
                                wait_drained(act, "za", s, i - 1, g)
                            drain(act.activation(zc_sb[s][:, cols], bank("zc", s, i, g), ACT.Copy), "zc", s, i, g)
                        if kind == "zf":
                            wait_filled(act, "zf", s, i, g)
                            drain(act.activation(zfT[s][:, i, cols], bank("zf", s, i, g), ACT.Copy), "zf", s, i, g)
                        if kind == "zu":
                            wait_filled(act, "zu", s, i, g)
                            if s and not i and not g:
                                act.wait_ge(x2_out[0], 16 * TL[0] // 2)
                                act.wait_ge(x2_out[1], 16 * TL[0] // 2)
                            drain(act.activation(Y[s][:, 5 + i, cols], bank("zu", s, i, g), ACT.Gelu_apprx_tanh),
                                  "zu", s, i, g)
                        if kind == "zv":
                            n = NG[s] * i + g
                            wait_filled(act, "zv", s, i, g)
                            if n >= 2:
                                wait_filled(act, "vt", s, (n - 2) // NG[s], (n - 2) % NG[s])
                            drain(act.activation(vF[s][:, n % 2, :], bank("zv", s, i, g), ACT.Gelu_apprx_tanh),
                                  "zv", s, i, g)
                    if kind == "ab":
                        act.wait_ge(var_v, s + 1)
                        r = ssv[:, T0[s]:T0[s] + TL[s]]
                        act.activation(r, r, ACT.Sqrt).then_inc(std_v, 1)
                        for t in range(1, TL[s], 2):
                            wait_filled(act, "ab", s, t)
                            drain(act.activation(AB[s][:, t, :, :, :].rearrange("p a b c -> p (a b c)"),
                                                 bank("ab", s, t), ACT.Copy), "ab", s, t)

            def y_split_hi(s, blocks):
                for b in blocks:
                    act.activation(Yhl[s][:, b, 0, :], Y[s][:, b, :], ACT.Copy,
                                   scale=VT[:, V_GGRP + b:V_GGRP + b + 1]).then_inc(y_hi, 1)

            def mixers_end(s):
                wait_filled(act, "zu", s, 2, NG[s] - 1)
                if s == 0:
                    for b in range(4):
                        split_hi(("wo", b))
                wait_drained(act, "zb", s, 2, NG[s] - 1)
                y_split_hi(s, range(3))
                if s == 0:
                    for b in range(4, KB - 1):
                        split_hi(("wo", b))
                half = W[s] // 2
                wait_drained(act, "sv", s, 2, NG[s] - 1)
                y_split_hi(s, range(5, KB))
                if s == 0:
                    split_hi(("wo", KB - 1))
                for fb in range(2):
                    wait_filled(act, "even", s, fb)
                    if fb:
                        wait_drained(act, "odd", s, 0)
                    drain(act.activation(e_sb[:, 0:half], bank("even", s, fb)[:, 0:half], ACT.Copy), "even", s, fb)
                wait_drained(act, "odd", s, 1)
                y_split_hi(s, (3, 4))
                for b, dst, adds in ((0, SQ[s][:, 0, :], 0), (1, sqt[0][s][:, :], 0), (2, sqt[1][s][:, :], 0),
                                     (3, SQ[s][:, 1, :], 0), (4, sqt[0][s][:, :], 1), (5, SQ[s][:, 2, :], 0),
                                     (6, sqt[1][s][:, :], 2), (7, sqt[0][s][:, :], 3)):
                    if adds:
                        act.wait_ge(sq_added, 5 * s + adds)
                    act.activation(dst, Y[s][:, b, :], ACT.Square).then_inc(sq_done, 1)
                act.wait_ge(var_y, 3 * (s + 1))
                r = rsy[:, T0[s]:T0[s] + TL[s], :]
                act.activation(r, r, ACT.Sqrt).then_inc(std_y, 1)
                act.wait_ge(rsy_ready, s + 1)

            def router_drains(s, g):
                for b in range(0, KB, 2):
                    wait_filled(act, "h2T", s, g, b)
                    wait_h2t_slot(act, s, g, b)
                    drain(act.activation(h2T[:, b % 4, :], bank("h2T", s, g, b), ACT.Copy), "h2T", s, g, b)
                wait_filled(act, "lg", s, g)
                if not g:
                    act.wait_ge(lgt_zero, s + 1)
                drain(act.activation(lgT[32 * g:32 * g + NE, :], bank("lg", s, g)[0:NE, :], ACT.Copy), "lg", s, g)

            def residual(s):
                for t in range(TL[s]):
                    tt = T0[s] + t
                    for h in range(2):
                        wait_filled(act, "out", s, t, 0, h)
                        if tt >= 2:
                            act.wait_ge(x2_out[tt % 2], 16 * (tt // 2))
                        drain(act.activation(x2[:, tt % 2, GW * h:GW * (h + 1)], bank("out", s, t, 0, h), ACT.Copy,
                                             scale=rsy[:, tt, 0:1]), "out", s, t, 0, h)
                    if t == GT:
                        router_drains(s, 0)
                    act.wait_ge(x2_ready, tt + 1)
                    if t >= GT:
                        act.wait_ge(h2_out[tt % GT], 16 * (tt // GT))
                    act.activation(h2[:, tt % GT, :], x2[:, tt % 2, :], ACT.Square, accum_out=ss2[:, tt:tt + 1]
                                   ).then_inc(ss2_ready, 1)
                    act.wait_ge(var_2, tt + 1)
                    act.activation(rs2[:, tt:tt + 1], rs2[:, tt:tt + 1], ACT.Sqrt).then_inc(std_2, 1)
                router_drains(s, NG[s] - 1)

            def softmax_exp(s):
                act.wait_ge(exp_in, s + 1)
                n = NG[s]
                act.activation(L2[:, :, 0:n, :], L2[:, :, 0:n, :], ACT.Exp).then_inc(exp_out, 1)

            for j in range(4):
                split_ahead([("ada", j, q) for q in range(4)])
                ada_drain(j)
                if j < 2:
                    x_stats(0, j)
            for g in range(NG[0]):
                hT_drains(0, g)
            mixers(0)
            mixers_end(0)
            residual(0)
            softmax_exp(0)
            x_stats(1, 0)
            hT_drains(1, 0)
            mixers(1)
            mixers_end(1)
            residual(1)
            softmax_exp(1)

            def split(e, j, free=None):
                act.wait_ge(raw_in[j % RAW], e * (16 * N_CH // RAW) + 16 * (j // RAW + 1))
                if free:
                    act.wait_ge(*free)
                act.activation(whi[:, j % SPL, :], raw[:, j % RAW, :], ACT.Copy).then_inc(w_hi, 1)

            def tokens_hi(e):
                for k in range(4):
                    act.wait_ge(t_filled, e * 4 + (k + 1))
                    act.activation(xT[:, 2 * k:2 * k + 2, 0:CAP],
                                   ps[:, k, 0:2 * CAP].rearrange("p (a n) -> p a n", a=2), ACT.Copy).then_inc(t_hi, 1)

            def hidden_hi(e, f):
                act.wait_ge(hid_done, e * FB + (f + 1))
                act.activation(hid[:, f, 0:CAP], hidf[:, f % 2, :], ACT.Copy).then_inc(hid_hi, 1)

            def expert(e, last=False):
                for f in range(FB):
                    b = 2 * (f % 2)
                    act.wait_ge(gu_filled, e * FB + (f + 1))
                    act.activation(gu_l[:, f % 2, :, :], ps[:, b:b + 2, CAP:2 * CAP], ACT.Copy).then_inc(lo_copied, 1)
                    if f:
                        hidden_hi(e, f - 1)
                    split(e, f + 4)
                    act.wait_ge(gu_summed, e * FB + (f + 1))
                    act.activation(sg[:, f % 2, :], gu[:, f % 2, 0, :], ACT.Silu).then_inc(silu_done, 1)
                hidden_hi(e, FB - 1)
                if not last:
                    for i in range(2):
                        split(e + 1, i)
                    tokens_hi(e + 1)
                    for i in range(2):
                        split(e + 1, 2 + i, (d_used, e * 4 + (i + 1)))
                act.wait_ge(d_used, e * 4 + 4)
                act.activation(ysl[0:CAP_S, :].rearrange("p (a n) -> p a n", a=2), ps[CAP_S:2 * CAP_S, 6:8, :],
                               ACT.Copy).then_inc(ysl_copied, 1)

            act.wait_ge(routed, 4)
            for i in range(2):
                act.wait_ge(x2_out[i], 16 * NT // 2)
            for i in range(GT):
                act.wait_ge(h2_out[i], 16 * NT // GT)
            for i in range(4):
                split(0, i)
            tokens_hi(0)
            with act.Fori(0, NE - 1) as e:
                expert(e)
            expert(NE - 1, last=True)

            for t in range(NT):
                act.wait_ge(fin_in[t], 16)
                if t:
                    act.wait_ge(ssf_ready, t)
                act.activation(fjunk[:, :], fin[:, t, :], ACT.Square, accum_out=ssf[:, t:t + 1]
                               ).then_inc(ssf_ready, 1)
                act.wait_ge(var_f, t + 1)
                act.activation(rsf[:, t:t + 1], rsf[:, t:t + 1], ACT.Sqrt).then_inc(std_f, 1)

        @block.tensor
        def _(pe):
            order = [0]

            def open_bank(*key):
                n = index[key]
                assert n == order[0], (key, n, order[0])
                order[0] += 1
                if n >= 8:
                    wait_drained(pe, *jobs[n - 8][0])
                return ps[:, n % 8, :]

            def fill(ins):
                ins.then_inc(bank_filled, 1)

            def mm(out, lhsT, rhs, start, stop):
                return pe.matmul(out, lhsT, rhs, start=start, stop=stop, skip_group_check=True)

            def ada(j):
                out = open_bank("ada", j)
                for q in range(4):
                    c = ("ada", j, q)
                    pe.wait_ge(ws_lo, split_n[c] + 1)
                    for k in range(2):
                        for part in range(2):
                            ins = mm(out, silw[:, 2 * q + k, :], slot_of(c)[:, part, GW * k:GW * (k + 1)],
                                     q == k == part == 0, q == 3 and k == part == 1)
                    fill(ins) if q == 3 else ins.then_inc(ada_part_used, 1)

            def x_blocks(s):
                for g in range(NG[s]):
                    pe.wait_ge(xn_ready, T0[s] + GT * (g + 1))
                    for b in range(KB):
                        out = open_bank("hT", s, g, b)
                        for t in range(GT):
                            tr = pe.transpose(out[:, P * t:P * (t + 1)], xg[s][:, g, t, P * b:P * (b + 1)], ident[:, :])
                        fill(tr)

            def w_in_block(s, kind, i):
                c = ("wi", s, kind, i)
                out = [open_bank(kind, s, i, g) for g in range(NG[s])]
                pe.wait_ge(ws_lo, split_n[c] + 1)
                for k in range(KB):
                    cols = slice(P * k, P * (k + 1))
                    for w, h in ((0, 0), (0, 1), (1, 0)):
                        for g in range(NG[s]):
                            last = k == KB - 1 and w == 1
                            ins = mm(out[g], slot_of(c)[:, w, cols], hT[s][:, h, k, GW * g:GW * (g + 1)],
                                     k == w == h == 0, last)
                            if last:
                                fill(ins)

            def mixers(s):
                for b in (KB - 2, KB - 1):
                    wait_drained(pe, "hT", s, NG[s] - 1, b)
                pe.wait_ge(hT_lo, (T0[s] + TL[s]) // GT * KB // 2)
                for kind, i in z_steps(s):
                    if kind == "ada":
                        ada(i)
                    elif kind in COL:
                        w_in_block(s, kind, i)
                    elif kind == "vt":
                        for g in range(NG[s]):
                            wait_drained(pe, "zv", s, i, g)
                            out = open_bank("vt", s, i, g)
                            for t in range(GT):
                                tr = pe.transpose(out[:, P * t:P * (t + 1)],
                                                  vF[s][:, (NG[s] * i + g) % 2, P * t:P * (t + 1)], ident[:, :])
                            fill(tr)
                    else:
                        wait_drained(pe, "zf", s, 1, NG[s] - 1)
                        for t in range(TL[s]):
                            half = TL[s] // 2
                            first = 2 * P * (t % half) + t // half
                            out = open_bank("ab", s, t)
                            for fb in range(2):
                                ins = pe.matmul(out[:, 2 * P * fb:2 * P * (fb + 1)],
                                                zfT[s][:, fb, first:first + 2 * P - 1:2],
                                                chs[:, :, :].rearrange("p a n -> p (a n)"), start=True, stop=True)
                            fill(ins)

            def gating(s):
                pe.wait_ge(v_ready, T0[s] + TL[s])
                wait_drained(pe, "wsp", 1)
                for i in range(3):
                    for g in range(NG[s]):
                        out = open_bank("sv", s, i, g)
                        for t in range(GT):
                            for q in range(2):
                                h = 2 * i + q
                                ins = pe.matmul(out[HD * q:HD * (q + 1), P * t:P * (t + 1)],
                                                v[s][:, GT * g + t, HD * h:HD * (h + 1)], wspT[:, h, :],
                                                start=True, stop=True)
                        fill(ins)

            def sequence_dft(s):
                half, tiles = W[s] // 2, TL[s] // 2
                wait_drained(pe, "ab", s, TL[s] - 1)
                wait_drained(pe, "ab", s, TL[s] - 2)
                for par, name in enumerate(("even", "odd")):
                    out = [open_bank(name, s, fb) for fb in range(2)]
                    for m in range(tiles * par, tiles * (par + 1)):
                        n = raw_n["dft", s, m]
                        pe.wait_ge(ws_in[n % RS], 16 * (n // RS + 1))
                        last = m == tiles * (par + 1) - 1
                        for fb in range(2):
                            for ab in range(2):
                                ins = mm(out[fb][:, 0:half], AB[s][:, m, fb, ab, :],
                                         wraw[:, n % RS, half * ab:half * (ab + 1)],
                                         m == tiles * par and not ab, last and ab == 1)
                            if last:
                                fill(ins)
                        if not last:
                            ins.then_inc(dft_used, 1)

            def w_out_tile(s, t):
                tile = slice(P * t, P * (t + 1))
                for k, blocks in enumerate((range(0, 3), range(3, 5), range(5, 8))):
                    out = [open_bank("out", s, t, k, h) for h in range(2)]
                    if t == 0:
                        pe.wait_ge(y_lo, KB * s + (3, 8, 6)[k])
                        if s == 0:
                            pe.wait_ge(ws_lo, split_n["wo", blocks[-1]] + 1)
                    for b in blocks:
                        for y, w in ((0, 0), (0, 1), (1, 0)):
                            for h in range(2):
                                last = b == blocks[-1] and y == 1
                                ins = mm(out[h], Yhl[s][:, b, y, tile], wo[:, b, w, GW * h:GW * (h + 1)],
                                         b == blocks[0] and y == w == 0, last)
                                if last:
                                    fill(ins)

            def router(s, g):
                pe.wait_ge(h2_ready, T0[s] + GT * (g + 1))
                lg = ps[:, index["lg", s, g] % 8, :]
                for b in range(KB + 2):
                    if b < KB:
                        out = open_bank("h2T", s, g, b)
                        for t in range(GT):
                            tr = pe.transpose(out[:, P * t:P * (t + 1)], h2[:, t, P * b:P * (b + 1)], ident[:, :])
                        fill(tr)
                    if b >= 2:
                        wait_drained(pe, "h2T", s, g, b - 2)
                        if b == 2:
                            wait_drained(pe, *jobs[index["lg", s, g] - 8][0])
                        ins = pe.matmul(lg[0:NE, :], wrt[:, b - 2, :], h2T[:, (b - 2) % 4, :], start=b == 2,
                                        stop=b == KB + 1)
                        if b < KB + 1:
                            ins.then_inc(lg_used, 1)
                assert order[0] == index["lg", s, g]
                order[0] += 1
                fill(ins)

            def index_columns(s):
                pe.wait_ge(topk_ready, s + 1)
                out = open_bank("idx", s)
                cap = CAPS[s]
                pe.transpose(out[0:cap, 0:NE], vals[0:NE, 0:cap], ident[0:NE, 0:NE])
                fill(pe.transpose(out[0:cap, NE:2 * NE], idxf[0:NE, 0:cap], ident[0:NE, 0:NE]))

            pe.wait_ge(rows_in, 16 * 6)
            pe.wait_ge(small_in, 16 * 3)
            out = open_bank("vec")
            fill(pe.transpose(out[:, 0:V_N], rows[0:V_N, :], ident[0:V_N, 0:V_N]))
            pe.wait_ge(silw_ready, 1)
            for j in range(4):
                ada(j)
            pe.wait_ge(modrow_in, 32)
            out = open_bank("mod")
            fill(pe.transpose(out[:, 0:32], modrow[0:32, :], ident[0:32, 0:32]))
            x_blocks(0)
            pe.wait_ge(wsp_in, 16)
            for n, heads in enumerate((range(4), range(4, N_SGU))):
                out = open_bank("wsp", n)
                for i, h in enumerate(heads):
                    tr = pe.transpose(out[:, P * i:P * (i + 1)], wsp6[:, h, :], ident[:, :])
                fill(tr)
            for s in range(2):
                mixers(s)
                if s:
                    index_columns(0)
                gating(s)
                sequence_dft(s)
                for t in range(TL[s]):
                    w_out_tile(s, t)
                    if t == 0:
                        pe.wait_ge(sq_added, 5 * (s + 1))
                        pe.wait_ge(ones_set, 1)
                        out = open_bank("ssq", s)
                        for n in range(3 * TL[s]):
                            ins = pe.matmul(out[:, n:n + 1], SQ[s][:, n % 3, P * (n // 3):P * (n // 3 + 1)], ones[:, :],
                                            start=True, stop=True)
                        fill(ins)
                    if t == GT:
                        router(s, 0)
                router(s, NG[s] - 1)
                wait_drained(pe, "lg", s, NG[s] - 1)
                out = open_bank("lt", s)
                for t in range(GT):
                    tr = pe.transpose(out[:, 64 * t:64 * (t + 1)], lgT[0:64, P * t:P * (t + 1)], ident[0:64, 0:64])
                fill(tr)
                if s == 0:
                    x_blocks(1)
                pe.wait_ge(aff_ready, s + 1)
                for g in range(NG[s]):
                    out = open_bank("aff", s, g)
                    for t in range(GT):
                        tr = pe.transpose(out[0:NE, P * t:P * (t + 1)], affm[:, GT * g + t, :], ident[:, :])
                    fill(tr)
            index_columns(1)

            def tokens(e):
                pe.wait_ge(xe_in, e * 32 + 32)
                for k in range(4):
                    for i in range(2):
                        cols = slice(P * (2 * k + i), P * (2 * k + i + 1))
                        pe.transpose(ps[:, k, CAP * i:CAP * i + CAP_P], xe[:, 0, cols], ident[:, :])
                        tr = pe.transpose(ps[:, k, CAP * i + CAP_P:CAP * (i + 1)], xe[0:CAP_S, 1, cols],
                                          ident[0:CAP_S, 0:CAP_S])
                    tr.then_inc(t_filled, 1)

            def product(out, slot, f):
                for k in range(KB):
                    w = slice(CW * k + P * (f % 2), CW * k + P * (f % 2) + P)
                    if k:
                        pe.matmul(out[:, 0:CAP], wlo[:, slot, w], xT[:, k, 0:CAP], start=False, stop=False,
                                  skip_group_check=True)
                    mm = pe.matmul(out[:, 0:2 * CAP], whi[:, slot, w], xT[:, k, :], start=k == 0, stop=k == KB - 1,
                                   skip_group_check=True)
                    if not k:
                        pe.matmul(out[:, 0:CAP], wlo[:, slot, w], xT[:, k, 0:CAP], start=False, stop=False,
                                  skip_group_check=True)
                return mm

            def down(e, k):
                for f in (2 * k, 2 * k + 1):
                    part = slice(0, CAP_P), slice(2 * CAP - CAP_P, 2 * CAP)
                    start, stop = f == 0, f == FB - 1
                    for n in range(2):
                        w = slice(D * (f % 2) + GW * n, D * (f % 2) + GW * (n + 1))
                        pe.matmul(ps[:, 4 + n, :], hid[:, f, part[0]], whi[:, (8 + k) % SPL, w], start=start, stop=False)
                        pe.matmul(ps[:, 4 + n, :], hid[:, f, part[0]], wlo[:, (8 + k) % SPL, w], start=False, stop=False)
                    for n in range(2):
                        w = slice(D * (f % 2) + GW * n, D * (f % 2) + GW * (n + 1))
                        pe.matmul(ps[:, 4 + n, :], hid[:, f, part[1]], whi[:, (8 + k) % SPL, w], start=False, stop=stop)
                    both = hid[:, f, CAP_P:CAP_P + 2 * CAP_S]
                    for n in range(2):
                        w = slice(D * (f % 2) + GW * n, D * (f % 2) + GW * (n + 1))
                        pe.matmul(ps[:, 6 + n, :], both, whi[:, (8 + k) % SPL, w], start=start, stop=False)
                        mm = pe.matmul(ps[:, 6 + n, :], both, wlo[:, (8 + k) % SPL, w], start=False, stop=stop)
                mm.then_inc(d_used, 1)

            def expert(e, last=False):
                for f in range(FB):
                    c, b = f // 2, 2 * (f % 2)
                    if f == 0:
                        pe.wait_ge(t_lo, e * 4 + 4)
                    if f >= 2:
                        pe.wait_ge(gu_summed, e * FB + (f - 1))
                    if f % 2 == 0:
                        pe.wait_ge(w_split, e * N_CH + (2 * c + 1))
                    product(ps[:, b, :], 2 * c % SPL, f)
                    if f % 2 == 0:
                        pe.wait_ge(w_split, e * N_CH + (2 * c + 2))
                    product(ps[:, b + 1, :], (2 * c + 1) % SPL, f).then_inc(gu_filled, 1)
                for k in range(4):
                    pe.wait_ge(w_split, e * N_CH + (9 + k))
                    pe.wait_ge(hid_lo, e * (2 * FB) + (4 * k + 4))
                    if k == 0:
                        pe.wait_ge(ye_sum, e * 1 + 1)
                    down(e, k)
                    if k == 1 and not last:
                        pe.wait_ge(gu_summed, e * FB + FB)
                        tokens(e + 1)

            wait_drained(pe, "idx", 1)
            tokens(0)
            with pe.Fori(0, NE - 1) as e:
                expert(e)
            expert(NE - 1, last=True)

        @block.vector
        def _(dve):
            n_step, n_split = [0], [0]

            def step(ins):
                ins.then_inc(dve_step, 1)
                n_step[0] += 1

            def after_step():
                dve.wait_ge(dve_step, n_step[0])

            def drain(ins, *key):
                ins.then_inc(drained[drainer[key]], 1)

            def split_lo(c):
                dve.wait_ge(ws_hi, split_n[c] + 1)
                pair_of = wo[:, c[1], :, :] if c[0] == "wo" else slot_of(c)
                dve.tensor_tensor(pair_of[:, 1, :], wraw[:, raw_n[c] % RS, :], pair_of[:, 0, :].bitcast(F32),
                                  ALU.subtract).then_inc(ws_lo, 1)

            def split_ahead(chunks):
                last = ring_n[chunks[-1]] + 2
                end = len(ring) if ring_n[chunks[0]] >= first_s else first_s
                while n_split[0] <= min(last, end - 1):
                    split_lo(ring[n_split[0]])
                    n_split[0] += 1

            wait_filled(dve, "vec")
            drain(dve.tensor_copy(VT[:, :], bank("vec")[:, 0:V_N]), "vec")
            dve.wait_ge(silw_hi, 1)
            dve.tensor_tensor(silw[:, :, 64:66], silc[:, :].rearrange("p (s k) -> p k s", s=2),
                              silw[:, :, 0:2].bitcast(F32), ALU.subtract).then_inc(silw_ready, 1)

            def ada_drain(j):
                cols = stage[0:2, j % 2, :]
                wait_filled(dve, "ada", j)
                dve.wait_ge(brow_in, 32 * (j + 1))
                if j >= 2:
                    dve.wait_ge(mod_out, 16 * (j - 1))
                step(dve.tensor_tensor(cols, bank("ada", j)[0:2, :], brow[0:2, :], ALU.add))
                after_step()
                dve.wait_ge(ada_lo_ready, j + 1)
                drain(dve.tensor_tensor(cols, cols, ada_lo[0:2, :], ALU.add), "ada", j)

            def x_norm(s, g):
                tt = T0[s] + GT * g
                dve.wait_ge(ssx_ready, tt + GT)
                r = rsx[:, tt:tt + GT]
                dve.tensor_scalar(r, ssx[:, tt:tt + GT], 1.0 / D, EPS, ALU.mult, ALU.add).then_inc(var_x, 1)
                dve.wait_ge(std_x, tt // GT + 1)
                step(dve.reciprocal(r, r))
                after_step()
                for t in range(GT):
                    x = xg[s][:, g, t, :]
                    dve.tensor_scalar(x, x, rsx[:, tt + t:tt + t + 1], None, ALU.mult).then_inc(xn_ready, 1)

            def hT_drains(s, g):
                cols = slice(GW * g, GW * (g + 1))
                n = (T0[s] // GT + g) * KB // 2
                for i in range(KB // 2):
                    b = 2 * i + 1
                    tmp = ht_d[s][:, i % 2, :]
                    wait_filled(dve, "hT", s, g, b)
                    dve.tensor_scalar(tmp, bank("hT", s, g, b), gsm[:, s, b:b + 1], modT[:, s, b:b + 1],
                                      ALU.mult, ALU.add).then_inc(ht_mod, 1)
                    wait_drained(dve, "hT", s, g, b - 1)
                    dve.tensor_tensor(hT[s][:, 1, b - 1, cols], ht_a[s][:, i % 2, :],
                                      hT[s][:, 0, b - 1, cols].bitcast(F32), ALU.subtract).then_inc(hT_lo, 1)
                    dve.wait_ge(hT_hi, n + i + 1)
                    drain(dve.tensor_tensor(hT[s][:, 1, b, cols], tmp, hT[s][:, 0, b, cols].bitcast(F32),
                                            ALU.subtract), "hT", s, g, b)

            def convolution(s, i):
                w = [VT[:, V_CONV + 3 * k + i:V_CONV + 3 * k + i + 1] for k in range(3)]
                step(dve.tensor_scalar(cv[s][:, :], a_pad[s][:, 1:1 + W[s]], w[1], None, ALU.mult))
                for k in (0, 2):
                    after_step()
                    step(dve.scalar_tensor_tensor(out=cv[s][:, :], in0=a_pad[s][:, k:k + W[s]], scalar=w[k],
                                                  in1=cv[s][:, :], op0=ALU.mult, op1=ALU.add))
                after_step()

            def ab_and_v(s):
                r = ssv[:, T0[s]:T0[s] + TL[s]]
                wait_drained(dve, "vt", s, 2, NG[s] - 1)
                for t in range(TL[s]):
                    if t:
                        after_step()
                    step(dve.tensor_tensor_reduce(vjunk[s][:, :], v[s][:, t, :], v[s][:, t, :], 1.0, 0.0, ALU.mult,
                                                  ALU.add, r[:, t:t + 1]))
                after_step()
                dve.tensor_scalar(r, r, 1.0 / SGU_W, EPS, ALU.mult, ALU.add).then_inc(var_v, 1)
                for t in range(0, TL[s], 2):
                    wait_filled(dve, "ab", s, t)
                    drain(dve.tensor_copy(AB[s][:, t, :, :, :].rearrange("p a b c -> p (a b c)"), bank("ab", s, t)),
                          "ab", s, t)
                dve.wait_ge(std_v, s + 1)
                step(dve.reciprocal(r, r))
                after_step()
                for t in range(TL[s]):
                    dve.tensor_scalar(v[s][:, t, :], v[s][:, t, :], r[:, t:t + 1], None, ALU.mult).then_inc(v_ready, 1)

            def mixers(s, between):
                for n, col in enumerate((0, W[s] + 1)):
                    dve.memset(a_pad[s][:, col:col + 1], 0.0).then_inc(pads_set, 1)
                dve.wait_ge(pads_set, 2 * (s + 1))
                for kind, i in z_steps(s):
                    chunks = chunks_of(s, kind, i)
                    if chunks:
                        split_ahead(chunks)
                    if kind == "ada":
                        ada_drain(i)
                    for g in range(NG[s]):
                        cols = slice(GW * g, GW * (g + 1))
                        if kind == "za":
                            wait_filled(dve, "za", s, i, g)
                            wait_drained(dve, "zc", s, i, g)
                            drain(dve.tensor_tensor(a_pad[s][:, 1 + GW * g:1 + GW * (g + 1)], bank("za", s, i, g),
                                                    zc_sb[s][:, cols], ALU.mult), "za", s, i, g)
                        if kind == "zb":
                            wait_filled(dve, "zb", s, i, g)
                            drain(dve.tensor_tensor(Y[s][:, i, cols], bank("zb", s, i, g), cv[s][:, cols], ALU.mult),
                                  "zb", s, i, g)
                        if kind == "vt":
                            wait_filled(dve, "vt", s, i, g)
                            drain(dve.tensor_copy(v[s][:, GT * g:GT * (g + 1), P * i:P * (i + 1)],
                                                  bank("vt", s, i, g).rearrange("p (a n) -> p a n", a=GT)),
                                  "vt", s, i, g)
                    if kind == "za":
                        wait_drained(dve, "za", s, i, NG[s] - 1)
                        convolution(s, i)
                    if kind == "ab":
                        ab_and_v(s)
                    between()

            def gating(s):
                dve.wait_ge(bsp_in, 16 * N_SGU)
                for i in range(3):
                    for g in range(NG[s]):
                        cols = slice(GW * g, GW * (g + 1))
                        wait_filled(dve, "sv", s, i, g)
                        if i or g:
                            wait_drained(dve, *[("sv", s, i, g - 1), ("sv", s, i - 1, NG[s] - 1)][g == 0])
                        step(dve.scalar_tensor_tensor(
                            out=svt[:, :].rearrange("p (a n) -> p a n", a=GT),
                            in0=bank("sv", s, i, g).rearrange("p (a n) -> p a n", a=GT),
                            scalar=VT[:, V_GSGU + i:V_GSGU + i + 1],
                            in1=bsp[:, i:i + 1, :].to_broadcast([P, GT, P]), op0=ALU.mult, op1=ALU.add))
                        after_step()
                        wait_drained(dve, "zu", s, i, g)
                        drain(dve.tensor_tensor(Y[s][:, 5 + i, cols], Y[s][:, 5 + i, cols], svt[:, :], ALU.mult),
                              "sv", s, i, g)

            n_y = [0]

            def y_split_lo(s, blocks):
                for b in blocks:
                    n_y[0] += 1
                    dve.wait_ge(y_hi, n_y[0])
                    dve.scalar_tensor_tensor(out=Yhl[s][:, b, 1, :], in0=Y[s][:, b, :],
                                             scalar=VT[:, V_GGRP + b:V_GGRP + b + 1],
                                             in1=Yhl[s][:, b, 0, :].bitcast(F32), op0=ALU.mult, op1=ALU.subtract
                                             ).then_inc(y_lo, 1)

            def mixers_end(s):
                if s == 0:
                    for b in range(4):
                        split_lo(("wo", b))
                y_split_lo(s, range(3))
                if s == 0:
                    for b in range(4, KB - 1):
                        split_lo(("wo", b))
                if s:
                    chosen(0)
                gating(s)
                y_split_lo(s, range(5, KB))
                if s == 0:
                    split_lo(("wo", KB - 1))
                half = W[s] // 2
                for fb in range(2):
                    wait_filled(dve, "odd", s, fb)
                    wait_drained(dve, "even", s, fb)
                    o = bank("odd", s, fb)[:, 0:half]
                    step(dve.tensor_tensor(Y[s][:, 3 + fb, 0:half], o, e_sb[:, 0:half], ALU.add))
                    after_step()
                    drain(dve.tensor_tensor(Y[s][:, 3 + fb, half:2 * half], e_sb[:, 0:half], o, ALU.subtract),
                          "odd", s, fb)
                y_split_lo(s, (3, 4))
                for n, (k, i, need) in enumerate(((0, 0, 2), (0, 1, 3), (1, 0, 5), (2, 1, 7), (2, 0, 8))):
                    dve.wait_ge(sq_done, KB * s + need)
                    if n:
                        dve.wait_ge(sq_added, 5 * s + n)
                    dve.tensor_tensor(SQ[s][:, k, :], SQ[s][:, k, :], sqt[i][s][:, :], ALU.add).then_inc(sq_added, 1)
                dve.memset(lgT[:, :], 0.0).then_inc(lgt_zero, 1)
                wait_filled(dve, "ssq", s)
                tiles = slice(T0[s], T0[s] + TL[s])
                drain(dve.tensor_copy(ssy[:, tiles, :].rearrange("p t k -> p (t k)"), bank("ssq", s)[:, 0:3 * TL[s]]),
                      "ssq", s)
                wait_drained(dve, "ssq", s)
                for k, width in enumerate((CONV_W, FOUR_W, SGU_W)):
                    dve.tensor_scalar(rsy[:, tiles, k:k + 1], ssy[:, tiles, k:k + 1], 1.0 / width, EPS, ALU.mult,
                                      ALU.add).then_inc(var_y, 1)
                dve.wait_ge(std_y, s + 1)
                dve.reciprocal(rsy[:, tiles, :], rsy[:, tiles, :]).then_inc(rsy_ready, 1)
                dve.wait_ge(rsy_ready, s + 1)

            def router_drains(s, g):
                for b in range(1, KB, 2):
                    wait_filled(dve, "h2T", s, g, b)
                    wait_h2t_slot(dve, s, g, b)
                    drain(dve.tensor_copy(h2T[:, b % 4, :], bank("h2T", s, g, b)), "h2T", s, g, b)

            def residual(s):
                dve.wait_ge(ffn_in, 48 * (s + 1))
                dve.scalar_tensor_tensor(out=gsf_b[:, :], in0=gsf_b[:, :], scalar=1.0, in1=gffn_b[:, :],
                                         op0=ALU.add, op1=ALU.mult).then_inc(gsf_ready, 1)
                dve.wait_ge(gsf_ready, s + 1)
                dve.wait_ge(gtm_in, 16 * (s + 1))
                for t in range(TL[s]):
                    tt = T0[s] + t
                    for k in (1, 2):
                        for h in range(2):
                            o = x2[:, tt % 2, GW * h:GW * (h + 1)]
                            wait_filled(dve, "out", s, t, k, h)
                            wait_drained(dve, "out", s, t, k - 1, h)
                            drain(dve.scalar_tensor_tensor(out=o, in0=bank("out", s, t, k, h),
                                                           scalar=rsy[:, tt, k:k + 1], in1=o, op0=ALU.mult,
                                                           op1=ALU.add), "out", s, t, k, h)
                    wait_drained(dve, "out", s, t, 2, 1)
                    o = x2[:, tt % 2, :]
                    step(dve.tensor_tensor(o, o, gtm_b[:, :], ALU.mult))
                    dve.wait_ge(xr_in[tt % 2], 16 * (tt // 2 + 1))
                    after_step()
                    dve.tensor_tensor(o, o, xr[:, tt % 2, :], ALU.add).then_inc(x2_ready, 1)
                    if t == GT:
                        router_drains(s, 0)
                    r = rs2[:, tt:tt + 1]
                    dve.wait_ge(ss2_ready, tt + 1)
                    dve.tensor_scalar(r, ss2[:, tt:tt + 1], 1.0 / D, EPS, ALU.mult, ALU.add).then_inc(var_2, 1)
                    dve.wait_ge(std_2, tt + 1)
                    step(dve.reciprocal(r, r))
                    after_step()
                    hh = h2[:, tt % GT, :]
                    step(dve.scalar_tensor_tensor(out=hh, in0=x2[:, tt % 2, :], scalar=r, in1=gsf_b[:, :],
                                                  op0=ALU.mult, op1=ALU.mult))
                    after_step()
                    dve.tensor_tensor(hh, hh, shf_b[:, :], ALU.add).then_inc(h2_ready, 1)
                router_drains(s, NG[s] - 1)

            def softmax(s):
                n = NG[s]
                wait_filled(dve, "lt", s)
                drain(dve.tensor_copy(L[:, :, :, :].rearrange("p a b c -> p (a b c)"), bank("lt", s)[:, 0:GT * 64]),
                      "lt", s)
                wait_drained(dve, "lt", s)
                for t in range(GT):
                    step(dve.tensor_reduce(smax[:, n * t:n * (t + 1)], L[:, t, 0:n, 0:NE], AX.X, ALU.max))
                after_step()
                for i in range(n * GT):
                    t, g = i // n, i % n
                    ins = dve.tensor_scalar(L2[:, t, g, :], L[:, t, g, 0:NE], smax[:, i:i + 1], None, ALU.subtract)
                    step(ins) if i < n * GT - 1 else ins.then_inc(exp_in, 1)
                dve.wait_ge(exp_out, s + 1)
                for t in range(GT):
                    step(dve.tensor_reduce(smax[:, n * t:n * (t + 1)], L2[:, t, 0:n, :], AX.X, ALU.add))
                after_step()
                step(dve.reciprocal(smax[:, 0:n * GT], smax[:, 0:n * GT]))
                after_step()
                for i in range(n * GT):
                    t, g = i // n, i % n
                    ins = dve.tensor_scalar(affm[:, GT * g + t, :], L2[:, t, g, :], smax[:, i:i + 1], None, ALU.mult)
                    step(ins) if i < n * GT - 1 else ins.then_inc(aff_ready, 1)

            def aff_drains(s):
                for g in range(NG[s]):
                    wait_filled(dve, "aff", s, g)
                    drain(dve.tensor_copy(aff[0:NE, GW * g:GW * (g + 1)], bank("aff", s, g)[0:NE, :]), "aff", s, g)
                wait_drained(dve, "aff", s, NG[s] - 1)

            def topk_eight(s, n):
                eight, row = slice(8 * n, 8 * n + 8), aff[0:NE, 0:W[s]]
                after_step()
                step(dve.max(vals[0:NE, eight], row))
                after_step()
                step(dve.max_index(idxu[0:NE, eight], vals[0:NE, eight], row))
                step(dve.match_replace(row, vals[0:NE, eight], row, -2.0))

            def topk_end(s):
                after_step()
                dve.tensor_copy(idxf[0:NE, 0:CAPS[s]], idxu[0:NE, 0:CAPS[s]]).then_inc(topk_ready, 1)

            def chosen(s):
                cap = CAPS[s]
                wait_filled(dve, "idx", s)
                if s:
                    step(dve.memset(gates[cap:P, s, :], 0.0))
                    step(dve.memset(rowid[cap:P, s, :], 0))
                    after_step()
                dve.tensor_copy(gates[0:cap, s, :], bank("idx", s)[0:cap, 0:NE]).then_inc(routed, 1)
                dve.tensor_scalar(rowid[0:cap, s, :], bank("idx", s)[0:cap, NE:2 * NE], float(BASE[s]), None, ALU.add
                                  ).then_inc(routed, 1)
                dve.wait_ge(routed, 2 * (s + 1))
                drain(dve.memset(tick[:, 0:1], 0.0), "idx", s)
                wait_drained(dve, "idx", s)

            for j in range(4):
                split_ahead([("ada", j, q) for q in range(4)])
                ada_drain(j)
                if j < 2:
                    x_norm(0, j)
            wait_filled(dve, "mod")
            drain(dve.tensor_copy(modT[:, :, :].rearrange("p a n -> p (a n)"), bank("mod")[:, 0:32]), "mod")
            wait_drained(dve, "mod")
            for s in range(2):
                dve.scalar_tensor_tensor(out=gsm[:, s, :], in0=modT[:, s, 8:16], scalar=1.0,
                                         in1=VT[:, V_GMIX:V_GMIX + KB], op0=ALU.add, op1=ALU.mult).then_inc(gsm_ready, 1)
            dve.wait_ge(gsm_ready, 2)
            for g in range(NG[0]):
                hT_drains(0, g)
            for n, (h0, h1) in enumerate(((0, 4), (4, N_SGU))):
                wait_filled(dve, "wsp", n)
                drain(dve.tensor_copy(wspT[:, h0:h1, :].rearrange("p a n -> p (a n)"),
                                      bank("wsp", n)[:, 0:P * (h1 - h0)]), "wsp", n)
            mixers(0, lambda: None)
            mixers_end(0)
            residual(0)
            softmax(0)
            x_norm(1, 0)
            hT_drains(1, 0)
            aff_drains(0)
            n_top = [0]

            def next_eight():
                if n_top[0] < CAP_P // 8:
                    topk_eight(0, n_top[0])
                    n_top[0] += 1

            mixers(1, next_eight)
            topk_end(0)
            mixers_end(1)
            residual(1)
            softmax(1)
            aff_drains(1)
            for n in range(CAP_S // 8):
                topk_eight(1, n)
            topk_end(1)
            chosen(1)

            def split(e, j):
                dve.wait_ge(w_hi, e * N_CH + (j + 1))
                dve.tensor_tensor(wlo[:, j % SPL, :], raw[:, j % RAW, :], whi[:, j % SPL, :].bitcast(F32), ALU.subtract
                                  ).then_inc(w_split, 1)

            def tokens_lo(e):
                for k in range(4):
                    dve.wait_ge(t_hi, e * 4 + (k + 1))
                    dve.tensor_tensor(xT[:, 2 * k:2 * k + 2, CAP:2 * CAP],
                                      ps[:, k, 0:2 * CAP].rearrange("p (a n) -> p a n", a=2),
                                      xT[:, 2 * k:2 * k + 2, 0:CAP].bitcast(F32), ALU.subtract).then_inc(t_lo, 1)

            def hidden_lo(e, f):
                dve.wait_ge(hid_hi, e * FB + (f + 1))
                for dst, src in ((CAP, slice(CAP_P, CAP)), (CAP + CAP_S, slice(0, CAP_P))):
                    n = src.stop - src.start
                    dve.tensor_tensor(hid[:, f, dst:dst + n], hidf[:, f % 2, src], hid[:, f, src].bitcast(F32), ALU.subtract
                                      ).then_inc(hid_lo, 1)

            def outputs(e):
                dve.tensor_copy(gcur[:, :], gates[:, :, bass.ds(e, 1)].rearrange("p a b -> p (a b)")
                                ).then_inc(gate_cur, 1)
                dve.wait_ge(gate_cur, e + 1)
                dve.wait_ge(ye_free, e + 1)
                dve.wait_ge(d_used, e * 4 + 4)
                for n in range(2):
                    cols = slice(GW * n, GW * (n + 1))
                    dve.scalar_tensor_tensor(out=ye[:, 0, cols], in0=ps[:, 4 + n, :], scalar=gcur[:, 0:1],
                                             in1=gtf_b[:, 0, cols], op0=ALU.mult, op1=ALU.mult).then_inc(ye_ready, 1)
                dve.wait_ge(ysl_copied, e + 1)
                y = ye[0:CAP_S, 1, :]
                dve.tensor_tensor(y.rearrange("p (a n) -> p a n", a=2), ps[0:CAP_S, 6:8, :],
                                  ysl[0:CAP_S, :].rearrange("p (a n) -> p a n", a=2), ALU.add).then_inc(ye_sum, 1)
                dve.wait_ge(ye_sum, e + 2)
                dve.scalar_tensor_tensor(out=y, in0=y, scalar=gcur[0:CAP_S, 1:2], in1=gtf_b[0:CAP_S, 1, :],
                                         op0=ALU.mult, op1=ALU.mult).then_inc(ye_ready, 1)

            def expert(e, last=False):
                for f in range(FB):
                    b = 2 * (f % 2)
                    dve.wait_ge(lo_copied, e * FB + (f + 1))
                    dve.tensor_tensor(gu[:, f % 2, :, :], ps[:, b:b + 2, 0:CAP], gu_l[:, f % 2, :, :], ALU.add).then_inc(gu_summed, 1)
                    if f:
                        hidden_lo(e, f - 1)
                    split(e, f + 4)
                    dve.wait_ge(silu_done, e * FB + (f + 1))
                    dve.tensor_tensor(hidf[:, f % 2, :], sg[:, f % 2, :], gu[:, f % 2, 1, :], ALU.mult).then_inc(hid_done, 1)
                hidden_lo(e, FB - 1)
                if not last:
                    for i in range(2):
                        split(e + 1, i)
                    tokens_lo(e + 1)
                    for i in range(2):
                        split(e + 1, 2 + i)
                outputs(e)

            dve.memset(tick[:, 0:1], 0.0).then_inc(ye_sum, 1)
            dve.wait_ge(gtf_in, 32)
            for i in range(4):
                split(0, i)
            tokens_lo(0)
            with dve.Fori(0, NE - 1) as e:
                expert(e)
            expert(NE - 1, last=True)

            dve.wait_ge(gfin_in, 16)
            for t in range(NT):
                dve.wait_ge(ssf_ready, t + 1)
                r = rsf[:, t:t + 1]
                dve.tensor_scalar(r, ssf[:, t:t + 1], 1.0 / D, EPS, ALU.mult, ALU.add).then_inc(var_f, 1)
                dve.wait_ge(std_f, t + 1)
                dve.reciprocal(r, r).then_inc(rsf_ready, 1)
                dve.wait_ge(rsf_ready, t + 1)
                y = fin[:, t, :]
                dve.scalar_tensor_tensor(out=y, in0=y, scalar=r, in1=gfin_b[:, :], op0=ALU.mult, op1=ALU.mult
                                         ).then_inc(fin_ready, 1)


_INS = ["x_prompt", "x_sample", "c_prompt", "c_sample", "w_ada", "b_ada", "g_mix", "w_in", "conv_w", "g_sgu",
        "w_spatial", "b_spatial", "g_grp", "w_out", "g_ffn", "w_router", "w_gate", "w_up", "w_down", "g_final"]
_OUTS = [(1, w, D) for w in W]


def kernel(**inputs):
    import concourse.bacc as bacc
    from concourse.bass_utils import run_bass_kernel_spmd

    nc = bacc.Bacc("TRN2", target_bir_lowering=False, num_devices=1)
    sent, aps = {}, {}
    arrays = {name: np.ascontiguousarray(inputs[name]) for name in _INS} | dft_constants()
    for name, x in arrays.items():
        sent[f"in_{name}"] = x
        aps[name] = nc.dram_tensor(f"in_{name}", x.shape, mybir.dt.from_np(x.dtype), kind="ExternalInput").ap()
    outs = [nc.dram_tensor(f"out_{i}", s, F32, kind="ExternalOutput").ap() for i, s in enumerate(_OUTS)]
    encoder_kernel(nc, aps, *outs)
    r = run_bass_kernel_spmd(nc, [sent], core_ids=[0])
    return tuple(r.results[0][f"out_{i}"] for i in range(2))
```

```python
import numpy as np
import concourse.bass as bass
from concourse import mybir

P = 128
D = 1024
KB = D // P
W = (1024, 512)
BASE = (0, W[0])
TOK = sum(W)
NT = TOK // P
GT = 4
GW = GT * P
NG = tuple(w // GW for w in W)
TL = tuple(w // P for w in W)
T0 = (0, TL[0])
CONV_W, FOUR_W, SGU_W = 384, 256, 384
HD = 64
N_SGU = SGU_W // HD
COL = {"zb": 0, "zc": CONV_W, "za": 2 * CONV_W, "zf": 3 * CONV_W, "zu": 3 * CONV_W + FOUR_W,
       "zv": 3 * CONV_W + FOUR_W + SGU_W}
EPS = 1e-6
NE = 16
CAP_P, CAP_S = 2 * W[0] // NE, 2 * W[1] // NE
CAP = CAP_P + CAP_S
CAPS = (CAP_P, CAP_S)
AW = 256
N_MIX = 2 * D // GW
N_ADA = N_MIX + 4 * D // AW
RS, SR = 3, 4
CW = 256
N_CH = 12
RAW = 4
SPL = 6
FB = D // P

F32, F32R, U32 = mybir.dt.float32, mybir.dt.float32r, mybir.dt.uint32
ACT = mybir.ActivationFunctionType
ALU = mybir.AluOpType
AX = mybir.AxisListType

V_C, V_GMIX, V_GGRP, V_CONV, V_GSGU, V_N = 0, 16, 24, 32, 41, 44


LT_STEP, AFF_STEP = 0, 2
NORMS = (0, 2, 1)
BLOCKS = (range(0, 3), range(3, 5), range(5, 8))


def z_steps(s):
    out, blocks, ada = [], 0, N_MIX
    for i in range(3):
        out += [("zc", i), ("za", i), ("zb", i)]
    out += [("zv", 0), ("zv", 1), ("vt", 0), ("zv", 2), ("vt", 1), ("zf", 0), ("vt", 2), ("zf", 1), ("zu", 0),
            ("ab", 0), ("zu", 1), ("zu", 2)]
    if s:
        return out
    mixed = []
    for n, step in enumerate(out):
        mixed.append(step)
        blocks += step[0] in COL
        if ada < N_ADA and ada - N_MIX < blocks and out[min(n + 1, len(out) - 1)][0] != "vt":
            mixed.append(("ada", ada))
            ada += 1
    assert ada == N_ADA
    return mixed


def ada_cols(j):
    first = GW * j if j < N_MIX else 2 * D + AW * (j - N_MIX)
    return slice(first, first + width_of(j))


def width_of(j):
    return GW if j < N_MIX else AW


def weight_stream():
    out = []
    for s in range(2):
        for kind, i in z_steps(s):
            if kind == "ada":
                out += [("ada", i, q) for q in range(2)]
            elif kind in COL:
                out.append(("wi", s, kind, i))
        if s == 0:
            for m in range(TL[0]):
                out += [("wo", m), ("dft", 0, m)]
        else:
            out += [("dft", 1, m) for m in range(TL[1])]
    return out


def bank_jobs():
    who = {"zc": "act", "za": "dve", "zb": "dve", "zf": "act", "zu": "act", "zv": "act", "vt": "dve"}
    jobs = [(("vec",), "dve")]

    def x_blocks(s):
        return [(("hT", s, g, b), "act" if b % 2 == 0 else "dve") for g in range(NG[s]) for b in range(KB)]

    def router(s, g):
        r = []
        for b in range(KB):
            r.append((("h2T", s, g, b), "act" if b % 2 == 0 else "dve"))
        return r + [(("lg", s, g), "act")]

    x = x_blocks(0)
    for j in range(N_MIX):
        if j == N_MIX - 1:
            jobs += x[0:4]
        jobs += [(("ada", j), "dve_mod")] + ([(("mod", j - 1), "dve_mod")] if j else [])
    jobs += [(("mod", N_MIX - 1), "dve_mod")] + x[4:] + [(("wsp", 0), "dve"), (("wsp", 1), "dve")]
    for s in range(2):
        for n, (kind, i) in enumerate(z_steps(s)):
            if kind == "ada":
                jobs.append((("ada", i), "dve"))
            elif kind == "ab":
                jobs += [(("ab", s, t), "act" if t % 2 else "dve") for t in range(TL[s])]
            else:
                jobs += [((kind, s, i, g), who[kind]) for g in range(NG[s])]
            if s and n == LT_STEP:
                jobs.append((("lt", 0), "dve"))
            if s and n == AFF_STEP:
                jobs += [(("aff", 0, g), "dve") for g in range(NG[0])]
        jobs += [(("sv", s, i, g), "dve") for i in range(3) for g in range(NG[s])]
        if s:
            jobs.append((("idx", 0), "dve"))
        jobs += [(("even", s, fb), "act") for fb in range(2)] + [(("odd", s, fb), "dve") for fb in range(2)]
        for t in range(TL[s]):
            jobs += [(("out", s, t, k, h), "act" if k == 0 else "dve") for k in NORMS for h in range(2)]
            if t == 0:
                jobs.append((("ssq", s), "dve_sums"))
            if t == GT:
                jobs += router(s, 0)
        if s == 0:
            jobs += x_blocks(1)
        jobs += router(s, NG[s] - 1)
    jobs += [(("lt", 1), "dve")] + [(("aff", 1, g), "dve") for g in range(NG[1])]
    return jobs + [(("idx", 1), "dve")]


def dft_constants():
    def seq(s):
        half = s // 2
        n = np.arange(s).reshape(s // 256, P, 2)
        n = n.transpose(2, 0, 1).reshape(s // P, P)
        ang = 2 * np.pi * ((n[:, :, None] * np.arange(half)) % s) / s
        both = np.stack([np.cos(ang), -np.sin(ang)], 2) / np.sqrt(s * HD)
        return np.ascontiguousarray(both).astype(np.float32)

    ang = 2 * np.pi * (np.outer(np.arange(HD), np.arange(HD)) % HD) / HD
    head = np.zeros((P, 2, P))
    for q in range(2):
        head[HD * q:HD * (q + 1), 0, HD * q:HD * (q + 1)] = np.cos(ang)
        head[HD * q:HD * (q + 1), 1, HD * q:HD * (q + 1)] = np.sin(ang)
    return {"dft_0": seq(W[0]), "dft_1": seq(W[1]), "dft_head": head.astype(np.float32),
            "ident": np.eye(P, dtype=np.float32)}


def encoder_kernel(nc, a, y_p, y_s):
    K = 1024
    base = (nc.sbuf_base + 63) // 64 * 64

    def at(name, offset, shape, dt=F32):
        return nc.alloc_sbuf_tensor_at(name, [P] + shape, dt, offset=base + int(offset))

    def pair(name, offsets, shape, dt=F32):
        return [at(f"{name}{s}", offsets[s] * K, shape(W[s]), dt) for s in range(2)]

    hT = pair("hT", (0, 32), lambda w: [2, KB, w], F32R)
    Yhl = pair("Yhl", (0, 32), lambda w: [w // GW, KB, 2, GW], F32R)
    Y = pair("Y", (64, 64), lambda w: [KB, w])
    wring = pair("wring", (96, 0), lambda w: [SR, 2, D], F32R)
    stages = [at("stage0", 84 * K, [2, GW]), at("stage1", 154 * K, [2, AW])]
    wo = at("wo", 96 * K, [KB, 2, D], F32R)
    xg = pair("xg", (128, 0), lambda w: [w // GW, GT, D])
    ht_a = pair("ht_a", (160, 64), lambda w: [2, GW])
    ht_d = pair("ht_d", (164, 68), lambda w: [2, GW])
    xjunk = pair("xjunk", (168, 16), lambda w: [D])
    zc_sb = pair("zc_sb", (128, 80), lambda w: [w])
    a_pad = pair("a_pad", (132, 82), lambda w: [w + 2])
    cv = pair("cv", (137, 85), lambda w: [w])
    zfT = pair("zfT", (142, 88), lambda w: [2, w])
    vF = pair("vF", (150, 92), lambda w: [2, GW])
    vjunk = pair("vjunk", (132, 82), lambda w: [SGU_W])
    brow = at("brow", 76 * K, [4, GW])
    ada_w = at("ada_w", 0, [N_MIX, KB, GW])
    v = pair("v", (156, 160), lambda w: [w // P, SGU_W])
    AB = pair("AB", (168, 168), lambda w: [w // P, 2, 2, P])
    SQ = [pair(f"SQ{k}_", o, lambda w: [w]) for k, o in enumerate(((160, 160), (176, 172), (168, 168)))]
    sqt = [pair(f"sqt{k}_", o, lambda w: [w]) for k, o in enumerate(((164, 162), (180, 174), (172, 170)))]
    wraw = at("wraw", 184 * K, [RS, D])
    svt = at("svt", 196 * K, [GW])
    ada_lo = at("ada_lo", 196 * K, [GW])
    rows = at("rows", 196 * K, [P])
    gtm_b = at("gtm_b", 164 * K, [D])
    shf_b = at("shf_b", 168 * K, [D])
    gsf_b = at("gsf_b", 172 * K, [D])
    gffn_b = at("gffn_b", 176 * K, [D])
    h2T = at("h2T", 176 * K, [4, GW])
    xr = at("xr", 64 * K, [2, D])
    x2 = at("x2", 72 * K, [2, D])
    h2 = at("h2", 80 * K, [GT, D])
    lgT = at("lgT", 160 * K, [GW])
    L = at("L", 162 * K, [GT, 2, 32])
    L2 = at("L2", 163 * K, [GT, 2, NE])
    affm = at("affm", 163.5 * K, [TL[0], NE])
    aff = at("aff", 176 * K, [W[0]])
    vals = at("vals", 180 * K, [P])
    idxu = at("idxu", 180.5 * K, [P], U32)
    idxf = at("idxf", 181 * K, [P])
    wsp6 = at("wsp6", 172 * K, [N_SGU, P])
    raw = at("raw", 0, [RAW, KB * CW])
    xe = at("xe", 32 * K, [2, D])
    xT = at("xT", 40 * K, [KB, 2 * CAP], F32R)
    hid = at("hid", 52 * K, [FB, 2 * CAP], F32R)
    whi = at("whi", 64 * K, [SPL, KB * CW], F32R)
    wlo = at("wlo", 112 * K, [SPL, KB * CW], F32R)
    gu_l = at("gu_l", 160 * K, [2, 2, CAP])
    gu = at("gu", 163 * K, [2, 2, CAP])
    sg = at("sg", 166 * K, [2, CAP])
    hidf = at("hidf", 167.5 * K, [2, CAP])
    ye = at("ye", 170 * K, [2, D])
    gtf_b = at("gtf_b", 184 * K, [2, D])
    ysl = at("ysl", 192 * K, [D])
    gfin_b = at("gfin_b", 178 * K, [D])
    fin = at("fin", 32 * K, [NT, D])
    fjunk = at("fjunk", 80 * K, [D])
    top = [198 * K]

    def small(name, shape, dt=F32):
        t = at(name, top[0], shape, dt)
        n = 4
        for x in shape:
            n *= x
        top[0] += (n + 31) // 32 * 32
        return t

    silw = small("silw", [KB, 34], F32R)
    ident = small("ident_sb", [P])
    ones = small("ones", [1])
    VT = small("VT", [V_N])
    silc = small("silc", [16])
    modT = small("modT", [2, 16])
    gsm = small("gsm", [2, KB])
    ssx = small("ssx", [NT])
    rsx = small("rsx", [NT])
    ssv = small("ssv", [NT])
    ssy = small("ssy", [NT, 3])
    rsy = small("rsy", [NT, 3])
    ss2 = small("ss2", [NT])
    rs2 = small("rs2", [NT])
    ssf = small("ssf", [NT])
    rsf = small("rsf", [NT])
    wrt = small("wrt", [KB, NE])
    chs = small("chs", [2, P])
    wspT = small("wspT", [N_SGU, P])
    bsp = small("bsp", [3, P])
    gates = small("gates", [2, NE])
    rowid = small("rowid", [2, NE], U32)
    gcur = small("gcur", [2])
    icur = small("icur", [2], U32)
    iscat = small("iscat", [2], U32)
    smax = small("smax", [TL[0]])
    tick = small("tick", [2])
    assert base + top[0] <= nc.sbuf_usable_end, (base + top[0], nc.sbuf_usable_end)

    ps = nc.alloc_psum_tensor("ps", [P, 8, GW], F32)

    mod_d = nc.dram_tensor("mod_d", [2, 6 * D], F32).ap()
    h2_d = nc.dram_tensor("h2_d", [TOK, D], F32).ap()
    acc_d = nc.dram_tensor("acc_d", [TOK, D], F32).ap()

    sem = nc.alloc_semaphore

    def sems(*names):
        return [sem(n) for n in names]

    jobs = bank_jobs()
    index = {k: n for n, (k, _) in enumerate(jobs)}
    drainer = dict(jobs)
    nth = {}
    for who in ("act", "dve", "dve_sums", "dve_mod"):
        nth |= {k: n + 1 for n, k in enumerate(k for k, w in jobs if w == who)}
    bank_filled = sem("bank_filled")
    drained = {"act": sem("bank_drained_by_act"), "dve": sem("bank_drained_by_dve"),
               "dve_sums": sem("bank_of_sums_drained"), "dve_mod": sem("bank_of_mod_drained")}

    def wait_filled(eng, *key):
        eng.wait_ge(bank_filled, index[key] + 1)

    def wait_drained(eng, *key):
        eng.wait_ge(drained[drainer[key]], nth[key])

    def bank(*key):
        return ps[:, index[key] % 8, :]

    stream = weight_stream()
    raw_n = {c: n for n, c in enumerate(stream)}
    split_n = {c: n for n, c in enumerate(c for c in stream if c[0] != "dft")}
    ring = [c for c in stream if c[0] in ("ada", "wi")]
    ring_n = {c: n for n, c in enumerate(ring)}
    first_s = min(n for n, c in enumerate(ring) if c[:2] == ("wi", 1))
    ada_parts = {c: n for n, c in enumerate(c for c in ring if c[0] == "ada" and c[2] == 0)}
    dft_n = {c: n for n, c in enumerate(c for c in stream if c[0] == "dft" and (c[2] + 1) % (TL[c[1]] // 2))}
    ws_in = [sem(f"ws_in{i}") for i in range(RS)]
    ws_hi, ws_lo, ada_part_used, dft_used = sems("ws_hi", "ws_lo", "ada_part_used", "dft_used")

    def stage(j):
        return stages[j >= N_MIX][0:2, j % 2, :]

    def slot_of(c):
        n = ring_n[c]
        return wring[0][:, n % SR, :, :] if n < first_s else wring[1][:, (n - first_s + 2) % SR, :, :]

    def wait_used(eng, c):
        if c in ada_parts:
            eng.wait_ge(ada_part_used, ada_parts[c] + 1)
        elif c[0] == "ada":
            wait_filled(eng, "ada", c[1])
        else:
            wait_filled(eng, c[2], c[1], c[3], NG[c[1]] - 1)

    def wait_h2t_slot(eng, s, g, b):
        n = T0[s] // GT + g
        if b >= 4:
            eng.wait_ge(lg_used, (KB - 1) * n + b - 3)
        elif n:
            wait_filled(eng, "lg", *((s, g - 1) if g else (s - 1, NG[s - 1] - 1)))

    def chunks_of(s, kind, i):
        return [("ada", i, q) for q in range(2)] if kind == "ada" else [("wi", s, kind, i)] if kind in COL else []

    rows_in, small_in, wsp_in, bsp_in = sems("rows_in", "small_in", "wsp_in", "bsp_in")
    brow_in, ada_in = [sem(f"brow_in{i}") for i in range(4)], [sem(f"ada_in{i}") for i in range(2 * N_MIX)]
    x_in = [sem(f"x_in{i}") for i in range(3)]
    gtm_in, ffn_in, gtf_in = sems("gtm_in", "ffn_in", "gtf_in")
    mod_out = [sem(f"mod_out{i}") for i in range(2)]
    xr_in = [sem(f"xr_in{i}") for i in range(2)]
    x2_out, h2_out = [sem(f"x2_out{i}") for i in range(2)], [sem(f"h2_out{i}") for i in range(GT)]
    raw_in = [sem(f"raw_in{i}") for i in range(RAW)]
    gfin_in, fin_in, fin_out = sem("gfin_in"), [sem(f"fin_in{i}") for i in range(NT)], sem("fin_out")
    xe_in, scattered = sems("xe_in", "scattered")
    sp_tick, pool_tick = sems("sp_tick", "pool_tick")
    dve_step, act_step = sems("dve_step", "act_step")
    ones_set, silw_zero, silc_ready, silw_hi, silw_ready = sems(
        "ones_set", "silw_zero", "silc_ready", "silw_hi", "silw_ready")
    ssx_ready, var_x, std_x, xn_ready = sems("ssx_ready", "var_x", "std_x", "xn_ready")
    gsm_ready, ht_mod, hT_hi, hT_lo, ada_lo_ready = sems(
        "gsm_ready", "ht_mod", "hT_hi", "hT_lo", "ada_lo_ready")
    var_v, std_v, v_ready, pads_set = sems("var_v", "std_v", "v_ready", "pads_set")
    y_hi, y_lo, sq_done, sq_added, var_y, std_y, rsy_ready = sems(
        "y_hi", "y_lo", "sq_done", "sq_added", "var_y", "std_y", "rsy_ready")
    gsf_ready, x2_ready, ss2_ready, var_2, std_2, h2_ready = sems(
        "gsf_ready", "x2_ready", "ss2_ready", "var_2", "std_2", "h2_ready")
    lg_used, lgt_zero, exp_in, exp_out, aff_ready, topk_ready, routed = sems(
        "lg_used", "lgt_zero", "exp_in", "exp_out", "aff_ready", "topk_ready", "routed")
    w_hi, w_split = sems("w_hi", "w_split")
    t_filled, t_hi, t_lo = sems("t_filled", "t_hi", "t_lo")
    gu_filled, lo_copied, gu_summed = sems("gu_filled", "lo_copied", "gu_summed")
    silu_done, hid_done, hid_hi, hid_lo = sems("silu_done", "hid_done", "hid_hi", "hid_lo")
    d_used, ysl_copied, ye_sum, ye_ready, ye_free = sems("d_used", "ysl_copied", "ye_sum", "ye_ready", "ye_free")
    gate_cur, idx_cur = sems("gate_cur", "idx_cur")
    ssf_ready, var_f, std_f, rsf_ready, fin_ready = sems("ssf_ready", "var_f", "std_f", "rsf_ready", "fin_ready")

    x_of = (a["x_prompt"][0], a["x_sample"][0])
    seq_of = [0] * TL[0] + [1] * TL[1]

    def x_rows(tt):
        s = seq_of[tt]
        return x_of[s][P * (tt - T0[s]):P * (tt - T0[s] + 1), :]

    def out_rows(tt):
        s = seq_of[tt]
        return (y_p, y_s)[s][0, P * (tt - T0[s]):P * (tt - T0[s] + 1), :]

    w_in, w_ada, w_out = a["w_in"][0], a["w_ada"][0], a["w_out"][0]
    w_g = a["w_gate"][0].rearrange("e (k p) f -> e p k f", p=P)
    w_u = a["w_up"][0].rearrange("e (k p) f -> e p k f", p=P)
    w_d = a["w_down"][0].rearrange("e (k p) f -> e p k f", p=P)

    def load_chunk(eng, e, j):
        slot = raw[:, j % RAW, :]
        if j < 8:
            src = (w_g, w_u)[j % 2][e, :, :, CW * (j // 2):CW * (j // 2 + 1)]
            dst = slot.rearrange("p (k f) -> p k f", k=KB)
        else:
            src = w_d[e, :, 2 * (j - 8):2 * (j - 8) + 2, :]
            dst = slot.rearrange("p (k f) -> p k f", k=2)
        eng.dma_start(dst, src).then_inc(raw_in[j % RAW], 16)

    with nc.Block() as block:

        @block.sync
        def _(sp):
            for name, at_row, n in (("c_prompt", V_C, 8), ("c_sample", V_C + 8, 8), ("g_mix", V_GMIX, 8),
                                    ("g_grp", V_GGRP, 8), ("g_sgu", V_GSGU, 3)):
                sp.dma_start(rows[at_row:at_row + n, :], a[name].rearrange("a (b n) -> (a b) n", n=P)
                             ).then_inc(rows_in, 16)
            sp.dma_start(rows[V_CONV:V_CONV + 9, :], a["conv_w"].rearrange("a k (b n) -> (a k b) n", n=P)
                         ).then_inc(rows_in, 16)

            def load_stream(n):
                c = stream[n]
                if n >= RS:
                    before = stream[n - RS]
                    if before in dft_n:
                        sp.wait_ge(dft_used, dft_n[before] + 1)
                    elif before[0] == "dft":
                        wait_filled(sp, ("even", "odd")[2 * before[2] // TL[before[1]]], before[1], 1)
                    else:
                        sp.wait_ge(ws_lo, split_n[before] + 1)
                slot = wraw[:, n % RS, :]
                if c[0] == "ada":
                    _, j, q = c
                    src = w_ada[GW * q:GW * (q + 1), ada_cols(j)].rearrange("(k p) n -> p k n", p=P)
                    slot = slot.rearrange("p (k n) -> p k n", k=4)
                elif c[0] == "wi":
                    col = COL[c[2]] + P * c[3]
                    src = w_in[:, col:col + P].rearrange("(k p) n -> p k n", p=P)
                    slot = slot.rearrange("p (k n) -> p k n", k=KB)
                elif c[0] == "wo":
                    src = w_out[P * c[1]:P * (c[1] + 1), :]
                else:
                    src = a[f"dft_{c[1]}"][c[2]].rearrange("p a n -> p (a n)")
                    slot = slot[:, 0:W[c[1]]]
                sp.dma_start(slot, src).then_inc(ws_in[n % RS], 16)

            def load_x(s, g):
                sp.dma_start(xg[s][:, g, :, :], x_of[s][GW * g:GW * (g + 1), :].rearrange("(t p) d -> p t d", p=P)
                             ).then_inc(x_in[2 * s + g], 16)

            def load_xr(tt):
                sp.dma_start(xr[:, tt % 2, :], x_rows(tt)).then_inc(xr_in[tt % 2], 16)

            n_next = [0]

            def stream_until(c):
                stop = len(stream) if c is None else raw_n[c]
                while n_next[0] < stop:
                    load_stream(n_next[0])
                    n_next[0] += 1

            for n in range(2 * N_MIX):
                j, h = n // 2, n % 2
                src = w_ada[GW * h:GW * (h + 1), GW * j:GW * (j + 1)].rearrange("(k p) n -> p k n", p=P)
                sp.dma_start(ada_w[:, j, 4 * h:4 * h + 4, :], src).then_inc(ada_in[n], 16)
                if n in (3, 5):
                    load_x(0, (n - 3) // 2)
            stream_until(ring[RS])
            for s in range(2):
                stream_until(None if s else ("wi", 1, "zc", 0))
                wait_filled(sp, "ssq", s)
                sp.wait_ge(y_lo, KB * (s + 1))
                load_xr(T0[s])
                load_xr(T0[s] + 1)
                for col, dst, arrived in ((2 * D, gtm_b, gtm_in), (3 * D, shf_b, ffn_in), (4 * D, gsf_b, ffn_in)):
                    sp.dma_start(dst[:, :], mod_d[s:s + 1, col:col + D].to_broadcast([P, D])).then_inc(arrived, 16)
                sp.dma_start(gffn_b[:, :], a["g_ffn"].to_broadcast([P, D])).then_inc(ffn_in, 16)
                if s == 0:
                    for n in range(RS):
                        load_stream(n_next[0])
                        n_next[0] += 1
                else:
                    for s2 in range(2):
                        sp.dma_start(gtf_b[:, s2, :], mod_d[s2:s2 + 1, 5 * D:6 * D].to_broadcast([P, D])
                                     ).then_inc(gtf_in, 16)
                    for j in range(RAW):
                        load_chunk(sp, 0, j)
                for t in range(TL[s]):
                    tt = T0[s] + t
                    if s == 0 and t == GT:
                        wait_filled(sp, "out", 0, GT - 1, 1, 1)
                        load_x(1, 0)
                    sp.wait_ge(h2_ready, tt + 1)
                    sp.dma_start(acc_d[P * tt:P * (tt + 1), :], x2[:, tt % 2, :]).then_inc(x2_out[tt % 2], 16)
                    sp.dma_start(h2_d[P * tt:P * (tt + 1), :], h2[:, tt % GT, :]).then_inc(h2_out[tt % GT], 16)
                    if t + 2 < TL[s]:
                        load_xr(tt + 2)

            with sp.Fori(0, NE - 1) as e:
                for j in range(N_CH):
                    sp.wait_ge(w_split, e * N_CH + (j + 1))
                    sp.sem_inc(sp_tick, 1)
                    if j < N_CH - RAW:
                        load_chunk(sp, e, j + RAW)
                    else:
                        load_chunk(sp, e + 1, j + RAW - N_CH)
            for j in range(N_CH - RAW):
                sp.wait_ge(w_split, (NE - 1) * N_CH + j + 1)
                load_chunk(sp, NE - 1, j + RAW)
            sp.dma_start(gfin_b[:, :], a["g_final"].rearrange("(a n) -> a n", a=1).to_broadcast([P, D])
                         ).then_inc(gfin_in, 16)

            sp.wait_ge(ye_free, NE + 1)
            for tt in range(NT):
                sp.dma_start(fin[:, tt, :], acc_d[P * tt:P * (tt + 1), :]).then_inc(fin_in[tt], 16)
            for tt in range(NT):
                sp.wait_ge(fin_ready, tt + 1)
                sp.dma_start(out_rows(tt), fin[:, tt, :]).then_inc(fin_out, 16)
            sp.wait_ge(fin_out, 16 * NT)

        @block.gpsimd
        def _(pool):
            pool.memset(ones[:, :], 1.0).then_inc(ones_set, 1)
            pool.memset(silw[:, :, :].bitcast(F32), 0.0).then_inc(silw_zero, 1)
            def load_bias(j):
                for s in range(2):
                    pool.dma_start(brow[s:s + 1, j % 4, 0:width_of(j)], a["b_ada"][0:1, ada_cols(j)]
                                   ).then_inc(brow_in[j % 4], 16)

            for j in range(4):
                load_bias(j)
            for h in range(N_SGU):
                pool.dma_start(bsp[HD * (h % 2):HD * (h % 2) + HD, h // 2, :],
                               a["b_spatial"][0, h:h + 1, :].to_broadcast([HD, P])).then_inc(bsp_in, 16)
            for j in range(N_ADA):
                wait_drained(pool, "ada", j)
                pool.dma_start(mod_d[:, ada_cols(j)], stage(j)).then_inc(mod_out[j % 2], 16)
                if j + 4 < N_ADA:
                    load_bias(j + 4)

            def gather(e, copies):
                pool.tensor_copy(icur[:, :], rowid[:, :, bass.ds(e, 1)].rearrange("p a b -> p (a b)")
                                 ).then_inc(idx_cur, 1)
                pool.wait_ge(idx_cur, copies)
                pool.sem_inc(pool_tick, 1)
                pool.indirect_dma_start(xe[:, 0, :], None, h2_d, bass.IndirectOffsetOnAxis(ap=icur[:, 0:1], axis=0)
                                        ).then_inc(xe_in, 16)
                pool.indirect_dma_start(xe[0:CAP_S, 1, :], None, h2_d,
                                        bass.IndirectOffsetOnAxis(ap=icur[0:CAP_S, 1:2], axis=0)
                                        ).then_inc(xe_in, 16)

            def scatter(e, copies):
                pool.tensor_copy(iscat[:, :], rowid[:, :, bass.ds(e, 1)].rearrange("p a b -> p (a b)")
                                 ).then_inc(idx_cur, 1)
                pool.wait_ge(idx_cur, copies)
                pool.wait_ge(ye_ready, e * 3 + 3)
                pool.sem_inc(pool_tick, 1)
                pool.indirect_dma_start(acc_d, bass.IndirectOffsetOnAxis(ap=iscat[:, 0:1], axis=0), ye[:, 0, :],
                                        None, compute_op=ALU.add).then_inc(scattered, 16)
                pool.indirect_dma_start(acc_d, bass.IndirectOffsetOnAxis(ap=iscat[0:CAP_S, 1:2], axis=0),
                                        ye[0:CAP_S, 1, :], None, compute_op=ALU.add).then_inc(scattered, 16)
                pool.wait_ge(scattered, e * 32 + 32)
                pool.nop().then_inc(ye_free, 1)

            pool.wait_ge(routed, 4)
            for i in range(2):
                pool.wait_ge(x2_out[i], 16 * NT // 2)
            for i in range(GT):
                pool.wait_ge(h2_out[i], 16 * NT // GT)
            pool.nop().then_inc(ye_free, 1)
            gather(0, 1)
            with pool.Fori(0, NE - 1) as e:
                pool.wait_ge(t_filled, e * 4 + 4)
                gather(e + 1, e * 2 + 2)
                scatter(e, e * 2 + 3)
            scatter(NE - 1, NE * 2)

        @block.scalar
        def _(act):
            n_step, n_split = [0], [0]

            def step(ins):
                ins.then_inc(act_step, 1)
                n_step[0] += 1

            def after_step():
                act.wait_ge(act_step, n_step[0])

            def drain(ins, *key):
                assert drainer[key] == "act"
                ins.then_inc(drained["act"], 1)

            def split_hi(c):
                n = raw_n[c]
                act.wait_ge(ws_in[n % RS], 16 * (n // RS + 1))
                if c[0] == "wo":
                    dst = wo[:, c[1], 0, :]
                    if c[1] == KB - 1:
                        for i in range(2):
                            act.wait_ge(mod_out[i], 16 * N_ADA // 2)
                else:
                    dst = slot_of(c)[:, 0, :]
                    if ring_n[c] >= SR:
                        wait_used(act, ring[ring_n[c] - SR])
                act.activation(dst, wraw[:, n % RS, :], ACT.Copy).then_inc(ws_hi, 1)

            def split_ahead(chunks):
                last = ring_n[chunks[-1]] + SR - 1
                end = len(ring) if ring_n[chunks[0]] >= first_s else first_s
                while n_split[0] <= min(last, end - 1):
                    split_hi(ring[n_split[0]])
                    n_split[0] += 1

            def split_first_of_sample():
                for _ in range(2):
                    split_hi(ring[n_split[0]])
                    n_split[0] += 1

            act.dma_start(ident[:, :], a["ident"]).then_inc(small_in, 16)
            act.dma_start(chs[:, :, :], a["dft_head"]).then_inc(small_in, 16)
            act.dma_start(wrt[:, :, :], a["w_router"][0].rearrange("(k p) n -> p k n", p=P)).then_inc(small_in, 16)
            act.dma_start(wsp6[:, :, :], a["w_spatial"][0].rearrange("h p q -> p h q")).then_inc(wsp_in, 16)
            wait_drained(act, "vec")
            act.activation(silc[:, :], VT[:, V_C:V_C + 16], ACT.Silu).then_inc(silc_ready, 1)
            act.wait_ge(silc_ready, 1)
            act.wait_ge(silw_zero, 1)
            act.activation(silw[:, :, 0:2], silc[:, :].rearrange("p (s k) -> p k s", s=2), ACT.Copy).then_inc(silw_hi, 1)

            def ada_drain(j):
                wait_filled(act, "ada", j)
                wait_drained(act, "ada", j - 1)
                act.activation(ada_lo[0:2, 0:AW], bank("ada", j)[32:34, 0:AW], ACT.Copy).then_inc(ada_lo_ready, 1)

            def x_stats(s, g):
                tt = T0[s] + GT * g
                act.wait_ge(x_in[2 * s + g], 16)
                for t in range(tt, tt + GT):
                    if t:
                        act.wait_ge(ssx_ready, t)
                    act.activation(xjunk[s][:, :], xg[s][:, g, t % GT, :], ACT.Square,
                                   accum_out=ssx[:, t:t + 1]).then_inc(ssx_ready, 1)
                act.wait_ge(var_x, tt // GT + 1)
                act.activation(rsx[:, tt:tt + GT], rsx[:, tt:tt + GT], ACT.Sqrt).then_inc(std_x, 1)

            def hT_drains(s, g):
                act.wait_ge(gsm_ready, 2)
                cols = slice(GW * g, GW * (g + 1))
                n_even = (s * NG[0] + g) * KB // 2
                for b in range(KB):
                    i = n_even + b // 2
                    if b % 2:
                        act.wait_ge(ht_mod, i + 1)
                        act.activation(hT[s][:, 0, b, cols], ht_d[s][:, (b // 2) % 2, :], ACT.Copy).then_inc(hT_hi, 1)
                    else:
                        wait_filled(act, "hT", s, g, b)
                        if i >= 2:
                            act.wait_ge(hT_lo, i - 1)
                        tmp = ht_a[s][:, (b // 2) % 2, :]
                        step(act.activation(tmp, bank("hT", s, g, b), ACT.Identity, bias=modT[:, s, b:b + 1],
                                            scale=gsm[:, s, b:b + 1]))
                        after_step()
                        drain(act.activation(hT[s][:, 0, b, cols], tmp, ACT.Copy), "hT", s, g, b)

            def mixers(s):
                if s:
                    for i in range(GT):
                        act.wait_ge(h2_out[i], 16 * TL[0] // GT)
                for n, (kind, i) in enumerate(z_steps(s)):
                    chunks = chunks_of(s, kind, i)
                    if chunks:
                        split_ahead(chunks)
                    if kind == "ada":
                        ada_drain(i)
                    for g in range(NG[s]):
                        cols = slice(GW * g, GW * (g + 1))
                        if kind == "zc":
                            wait_filled(act, "zc", s, i, g)
                            if i:
                                wait_drained(act, "za", s, i - 1, g)
                            drain(act.activation(zc_sb[s][:, cols], bank("zc", s, i, g), ACT.Copy), "zc", s, i, g)
                        if kind == "zf":
                            wait_filled(act, "zf", s, i, g)
                            drain(act.activation(zfT[s][:, i, cols], bank("zf", s, i, g), ACT.Copy), "zf", s, i, g)
                        if kind == "zu":
                            wait_filled(act, "zu", s, i, g)
                            if s and not i and not g:
                                act.wait_ge(x2_out[0], 16 * TL[0] // 2)
                                act.wait_ge(x2_out[1], 16 * TL[0] // 2)
                            drain(act.activation(Y[s][:, 5 + i, cols], bank("zu", s, i, g), ACT.Gelu_apprx_tanh),
                                  "zu", s, i, g)
                        if kind == "zv":
                            m = NG[s] * i + g
                            wait_filled(act, "zv", s, i, g)
                            if m >= 2:
                                wait_filled(act, "vt", s, (m - 2) // NG[s], (m - 2) % NG[s])
                            drain(act.activation(vF[s][:, m % 2, :], bank("zv", s, i, g), ACT.Gelu_apprx_tanh),
                                  "zv", s, i, g)
                    if kind == "ab":
                        act.wait_ge(var_v, s + 1)
                        r = ssv[:, T0[s]:T0[s] + TL[s]]
                        act.activation(r, r, ACT.Sqrt).then_inc(std_v, 1)
                        for t in range(1, TL[s], 2):
                            wait_filled(act, "ab", s, t)
                            drain(act.activation(AB[s][:, t, :, :, :].rearrange("p a b c -> p (a b c)"),
                                                 bank("ab", s, t), ACT.Copy), "ab", s, t)
                    if s and n == LT_STEP:
                        softmax_exp(0)

            def y_split_hi(s, blocks):
                for b in blocks:
                    act.activation(Yhl[s][:, :, b, 0, :], Y[s][:, b, :].rearrange("p (g n) -> p g n", n=GW), ACT.Copy,
                                   scale=VT[:, V_GGRP + b:V_GGRP + b + 1]).then_inc(y_hi, 1)

            def mixers_end(s):
                half = W[s] // 2

                def w_out_hi(*blocks):
                    for b in blocks if s == 0 else ():
                        split_hi(("wo", b))

                def squares(k):
                    for n, b in enumerate(BLOCKS[k]):
                        if n == 2:
                            act.wait_ge(sq_added, 5 * s + (1, 0, 3)[k])
                        act.activation((sqt if n else SQ)[k][s][:, :], Y[s][:, b, :], ACT.Square).then_inc(sq_done, 1)

                wait_filled(act, "zu", s, 2, NG[s] - 1)
                w_out_hi(0, 1)
                wait_drained(act, "zb", s, 2, NG[s] - 1)
                y_split_hi(s, range(3))
                w_out_hi(2)
                wait_drained(act, "sv", s, 2, NG[s] - 1)
                y_split_hi(s, range(5, KB))
                w_out_hi(3, 4)
                squares(0)
                for fb in range(2):
                    wait_filled(act, "even", s, fb)
                    drain(act.activation(Y[s][:, 3 + fb, half:2 * half], bank("even", s, fb)[:, 0:half], ACT.Copy),
                          "even", s, fb)
                w_out_hi(5, 6, 7)
                squares(2)
                for fb in range(2):
                    wait_drained(act, "odd", s, fb)
                    y_split_hi(s, [3 + fb])
                squares(1)
                act.wait_ge(var_y, 3 * (s + 1))
                r = rsy[:, T0[s]:T0[s] + TL[s], :]
                act.activation(r, r, ACT.Sqrt).then_inc(std_y, 1)
                act.wait_ge(rsy_ready, s + 1)

            def router_drains(s, g):
                for b in range(0, KB, 2):
                    wait_filled(act, "h2T", s, g, b)
                    wait_h2t_slot(act, s, g, b)
                    drain(act.activation(h2T[:, b % 4, :], bank("h2T", s, g, b), ACT.Copy), "h2T", s, g, b)
                wait_filled(act, "lg", s, g)
                if not g:
                    act.wait_ge(lgt_zero, s + 1)
                drain(act.activation(lgT[32 * g:32 * g + NE, :], bank("lg", s, g)[0:NE, :], ACT.Copy), "lg", s, g)

            def residual(s):
                for t in range(TL[s]):
                    tt = T0[s] + t
                    for h in range(2):
                        wait_filled(act, "out", s, t, 0, h)
                        if tt >= 2:
                            act.wait_ge(x2_out[tt % 2], 16 * (tt // 2))
                        drain(act.activation(x2[:, tt % 2, GW * h:GW * (h + 1)], bank("out", s, t, 0, h), ACT.Copy,
                                             scale=rsy[:, tt, 0:1]), "out", s, t, 0, h)
                    if t == GT:
                        router_drains(s, 0)
                    act.wait_ge(x2_ready, tt + 1)
                    if t >= GT:
                        act.wait_ge(h2_out[tt % GT], 16 * (tt // GT))
                    act.activation(h2[:, tt % GT, :], x2[:, tt % 2, :], ACT.Square, accum_out=ss2[:, tt:tt + 1]
                                   ).then_inc(ss2_ready, 1)
                    act.wait_ge(var_2, tt + 1)
                    act.activation(rs2[:, tt:tt + 1], rs2[:, tt:tt + 1], ACT.Sqrt).then_inc(std_2, 1)
                    if s == 0 and t == GT + 1:
                        x_stats(1, 0)
                    if s == 0 and t == GT + 2:
                        split_first_of_sample()
                if s == 0:
                    hT_drains(1, 0)
                router_drains(s, NG[s] - 1)

            def softmax_exp(s):
                act.wait_ge(exp_in, s + 1)
                n = NG[s]
                act.activation(L2[:, :, 0:n, :], L2[:, :, 0:n, :], ACT.Exp).then_inc(exp_out, 1)

            for g in range(NG[0]):
                x_stats(0, g)
            split_ahead([ring[0]])
            for g in range(NG[0]):
                hT_drains(0, g)
            mixers(0)
            mixers_end(0)
            residual(0)
            mixers(1)
            mixers_end(1)
            residual(1)
            softmax_exp(1)

            def split(e, j, free=None):
                act.wait_ge(raw_in[j % RAW], e * (16 * N_CH // RAW) + 16 * (j // RAW + 1))
                if free:
                    act.wait_ge(*free)
                act.activation(whi[:, j % SPL, :], raw[:, j % RAW, :], ACT.Copy).then_inc(w_hi, 1)

            def tokens_hi(e):
                for k in range(4):
                    act.wait_ge(t_filled, e * 4 + (k + 1))
                    act.activation(xT[:, 2 * k:2 * k + 2, 0:CAP],
                                   ps[:, k, 0:2 * CAP].rearrange("p (a n) -> p a n", a=2), ACT.Copy).then_inc(t_hi, 1)

            def hidden_hi(e, f):
                act.wait_ge(hid_done, e * FB + (f + 1))
                act.activation(hid[:, f, 0:CAP], hidf[:, f % 2, :], ACT.Copy).then_inc(hid_hi, 1)

            def expert(e, last=False):
                for f in range(FB):
                    b = 2 * (f % 2)
                    act.wait_ge(gu_filled, e * FB + (f + 1))
                    act.activation(gu_l[:, f % 2, :, :], ps[:, b:b + 2, CAP:2 * CAP], ACT.Copy).then_inc(lo_copied, 1)
                    if f:
                        hidden_hi(e, f - 1)
                    split(e, f + 4)
                    act.wait_ge(gu_summed, e * FB + (f + 1))
                    act.activation(sg[:, f % 2, :], gu[:, f % 2, 0, :], ACT.Silu).then_inc(silu_done, 1)
                hidden_hi(e, FB - 1)
                if not last:
                    for i in range(2):
                        split(e + 1, i)
                    tokens_hi(e + 1)
                    for i in range(2):
                        split(e + 1, 2 + i, (d_used, e * 4 + (i + 1)))
                act.wait_ge(d_used, e * 4 + 4)
                act.activation(ysl[0:CAP_S, :].rearrange("p (a n) -> p a n", a=2), ps[CAP_S:2 * CAP_S, 6:8, :],
                               ACT.Copy).then_inc(ysl_copied, 1)

            for i in range(2):
                act.wait_ge(x2_out[i], 16 * NT // 2)
            for i in range(GT):
                act.wait_ge(h2_out[i], 16 * NT // GT)
            for i in range(4):
                split(0, i)
            tokens_hi(0)
            with act.Fori(0, NE - 1) as e:
                expert(e)
            expert(NE - 1, last=True)

            for t in range(NT):
                act.wait_ge(fin_in[t], 16)
                if t:
                    act.wait_ge(ssf_ready, t)
                act.activation(fjunk[:, :], fin[:, t, :], ACT.Square, accum_out=ssf[:, t:t + 1]
                               ).then_inc(ssf_ready, 1)
                act.wait_ge(var_f, t + 1)
                act.activation(rsf[:, t:t + 1], rsf[:, t:t + 1], ACT.Sqrt).then_inc(std_f, 1)

        @block.tensor
        def _(pe):
            order = [0]

            def open_bank(*key):
                n = index[key]
                assert n == order[0], (key, n, order[0])
                order[0] += 1
                if n >= 8:
                    wait_drained(pe, *jobs[n - 8][0])
                return ps[:, n % 8, :]

            def fill(ins):
                ins.then_inc(bank_filled, 1)

            def mm(out, lhsT, rhs, start, stop):
                return pe.matmul(out, lhsT, rhs, start=start, stop=stop, skip_group_check=True)

            def ada_first(j):
                out = open_bank("ada", j)
                for k in range(KB):
                    if k % 4 == 0:
                        pe.wait_ge(ada_in[2 * j + k // 4], 16)
                    ins = pe.matmul(out[0:2, :], silc[:, k:16:KB], ada_w[:, j, k, :], start=k == 0, stop=k == KB - 1)
                fill(ins)

            def mod_columns(j):
                wait_drained(pe, "ada", j)
                out = open_bank("mod", j)
                for m in range(GT):
                    tr = pe.transpose(out[:, 2 * m:2 * m + 2], stage(j)[:, P * m:P * (m + 1)], ident[0:2, 0:2])
                fill(tr)

            def ada(j):
                out = open_bank("ada", j)
                for q in range(2):
                    c = ("ada", j, q)
                    pe.wait_ge(ws_lo, split_n[c] + 1)
                    for k in range(4):
                        for part in range(2):
                            ins = mm(out[0:34, 0:AW], silw[:, 4 * q + k, :], slot_of(c)[:, part, AW * k:AW * (k + 1)],
                                     q == k == part == 0, q == part == 1 and k == 3)
                    fill(ins) if q else ins.then_inc(ada_part_used, 1)

            def x_blocks(s, first=0, last=None):
                for n in range(first, last or KB * NG[s]):
                    g, b = n // KB, n % KB
                    if n == first or b == 0:
                        pe.wait_ge(xn_ready, T0[s] + GT * (g + 1))
                    out = open_bank("hT", s, g, b)
                    for t in range(GT):
                        tr = pe.transpose(out[:, P * t:P * (t + 1)], xg[s][:, g, t, P * b:P * (b + 1)], ident[:, :])
                    fill(tr)

            def w_in_block(s, kind, i):
                c = ("wi", s, kind, i)
                out = [open_bank(kind, s, i, g) for g in range(NG[s])]
                pe.wait_ge(ws_lo, split_n[c] + 1)
                for k in range(KB):
                    cols = slice(P * k, P * (k + 1))
                    for w, h in ((0, 0), (0, 1), (1, 0)):
                        for g in range(NG[s]):
                            last = k == KB - 1 and w == 1
                            ins = mm(out[g], slot_of(c)[:, w, cols], hT[s][:, h, k, GW * g:GW * (g + 1)],
                                     k == w == h == 0, last)
                            if last:
                                fill(ins)

            def mixers(s):
                for b in (KB - 2, KB - 1):
                    wait_drained(pe, "hT", s, NG[s] - 1, b)
                pe.wait_ge(hT_lo, (T0[s] + TL[s]) // GT * KB // 2)
                for n, (kind, i) in enumerate(z_steps(s)):
                    if kind == "ada":
                        ada(i)
                    elif kind in COL:
                        w_in_block(s, kind, i)
                    elif kind == "vt":
                        for g in range(NG[s]):
                            wait_drained(pe, "zv", s, i, g)
                            out = open_bank("vt", s, i, g)
                            for t in range(GT):
                                tr = pe.transpose(out[:, P * t:P * (t + 1)],
                                                  vF[s][:, (NG[s] * i + g) % 2, P * t:P * (t + 1)], ident[:, :])
                            fill(tr)
                    else:
                        wait_drained(pe, "zf", s, 1, NG[s] - 1)
                        for t in range(TL[s]):
                            half = TL[s] // 2
                            first = 2 * P * (t % half) + t // half
                            out = open_bank("ab", s, t)
                            for fb in range(2):
                                ins = pe.matmul(out[:, 2 * P * fb:2 * P * (fb + 1)],
                                                zfT[s][:, fb, first:first + 2 * P - 1:2],
                                                chs[:, :, :].rearrange("p a n -> p (a n)"), start=True, stop=True)
                            fill(ins)
                    if s and n == LT_STEP:
                        logits_to_tokens(0)
                    if s and n == AFF_STEP:
                        affinity_rows(0)

            def gating(s):
                pe.wait_ge(v_ready, T0[s] + TL[s])
                wait_drained(pe, "wsp", 1)
                for i in range(3):
                    for g in range(NG[s]):
                        out = open_bank("sv", s, i, g)
                        for t in range(GT):
                            for q in range(2):
                                h = 2 * i + q
                                ins = pe.matmul(out[HD * q:HD * (q + 1), P * t:P * (t + 1)],
                                                v[s][:, GT * g + t, HD * h:HD * (h + 1)], wspT[:, h, :],
                                                start=True, stop=True)
                        fill(ins)

            def sequence_dft(s):
                half, tiles = W[s] // 2, TL[s] // 2
                wait_drained(pe, "ab", s, TL[s] - 1)
                wait_drained(pe, "ab", s, TL[s] - 2)
                for par, name in enumerate(("even", "odd")):
                    out = [open_bank(name, s, fb) for fb in range(2)]
                    for m in range(tiles * par, tiles * (par + 1)):
                        n = raw_n["dft", s, m]
                        pe.wait_ge(ws_in[n % RS], 16 * (n // RS + 1))
                        last = m == tiles * (par + 1) - 1
                        for fb in range(2):
                            for ab in range(2):
                                ins = mm(out[fb][:, 0:half], AB[s][:, m, fb, ab, :],
                                         wraw[:, n % RS, half * ab:half * (ab + 1)],
                                         m == tiles * par and not ab, last and ab == 1)
                            if last:
                                fill(ins)
                        if not last:
                            ins.then_inc(dft_used, 1)

            def w_out_tile(s, t):
                tile = slice(P * (t % GT), P * (t % GT + 1))
                for k in NORMS:
                    blocks = BLOCKS[k]
                    out = [open_bank("out", s, t, k, h) for h in range(2)]
                    if t == 0:
                        pe.wait_ge(y_lo, KB * s + (3, 8, 6)[k])
                        if s == 0:
                            pe.wait_ge(ws_lo, split_n["wo", blocks[-1]] + 1)
                    for b in blocks:
                        for y, w in ((0, 0), (0, 1), (1, 0)):
                            for h in range(2):
                                last = b == blocks[-1] and y == 1
                                ins = mm(out[h], Yhl[s][:, t // GT, b, y, tile], wo[:, b, w, GW * h:GW * (h + 1)],
                                         b == blocks[0] and y == w == 0, last)
                                if last:
                                    fill(ins)

            def router(s, g):
                pe.wait_ge(h2_ready, T0[s] + GT * (g + 1))
                lg = ps[:, index["lg", s, g] % 8, :]
                for b in range(KB + 2):
                    if b < KB:
                        out = open_bank("h2T", s, g, b)
                        for t in range(GT):
                            tr = pe.transpose(out[:, P * t:P * (t + 1)], h2[:, t, P * b:P * (b + 1)], ident[:, :])
                        fill(tr)
                    if b >= 2:
                        wait_drained(pe, "h2T", s, g, b - 2)
                        if b == 2:
                            wait_drained(pe, *jobs[index["lg", s, g] - 8][0])
                        ins = pe.matmul(lg[0:NE, :], wrt[:, b - 2, :], h2T[:, (b - 2) % 4, :], start=b == 2,
                                        stop=b == KB + 1)
                        if b < KB + 1:
                            ins.then_inc(lg_used, 1)
                assert order[0] == index["lg", s, g]
                order[0] += 1
                fill(ins)

            def logits_to_tokens(s):
                wait_drained(pe, "lg", s, NG[s] - 1)
                out = open_bank("lt", s)
                for t in range(GT):
                    tr = pe.transpose(out[:, 64 * t:64 * (t + 1)], lgT[0:64, P * t:P * (t + 1)], ident[0:64, 0:64])
                fill(tr)

            def affinity_rows(s):
                pe.wait_ge(aff_ready, s + 1)
                for g in range(NG[s]):
                    out = open_bank("aff", s, g)
                    for t in range(GT):
                        tr = pe.transpose(out[0:NE, P * t:P * (t + 1)], affm[:, GT * g + t, :], ident[:, :])
                    fill(tr)

            def index_columns(s):
                pe.wait_ge(topk_ready, s + 1)
                out = open_bank("idx", s)
                cap = CAPS[s]
                pe.transpose(out[0:cap, 0:NE], vals[0:NE, 0:cap], ident[0:NE, 0:NE])
                fill(pe.transpose(out[0:cap, NE:2 * NE], idxf[0:NE, 0:cap], ident[0:NE, 0:NE]))

            pe.wait_ge(rows_in, 16 * 6)
            pe.wait_ge(small_in, 16 * 3)
            out = open_bank("vec")
            fill(pe.transpose(out[:, 0:V_N], rows[0:V_N, :], ident[0:V_N, 0:V_N]))
            pe.wait_ge(silc_ready, 1)
            for j in range(N_MIX):
                if j == N_MIX - 1:
                    x_blocks(0, 0, 4)
                ada_first(j)
                if j:
                    mod_columns(j - 1)
            mod_columns(N_MIX - 1)
            x_blocks(0, 4)
            pe.wait_ge(silw_ready, 1)
            pe.wait_ge(wsp_in, 16)
            for n, heads in enumerate((range(4), range(4, N_SGU))):
                out = open_bank("wsp", n)
                for i, h in enumerate(heads):
                    tr = pe.transpose(out[:, P * i:P * (i + 1)], wsp6[:, h, :], ident[:, :])
                fill(tr)
            for s in range(2):
                mixers(s)
                gating(s)
                if s:
                    index_columns(0)
                sequence_dft(s)
                for t in range(TL[s]):
                    w_out_tile(s, t)
                    if t == 0:
                        pe.wait_ge(sq_added, 5 * (s + 1))
                        pe.wait_ge(ones_set, 1)
                        out = open_bank("ssq", s)
                        for n in range(3 * TL[s]):
                            ins = pe.matmul(out[:, n:n + 1], SQ[n % 3][s][:, P * (n // 3):P * (n // 3 + 1)], ones[:, :],
                                            start=True, stop=True)
                        fill(ins)
                    if t == GT:
                        router(s, 0)
                if s == 0:
                    x_blocks(1)
                router(s, NG[s] - 1)
            logits_to_tokens(1)
            affinity_rows(1)
            index_columns(1)

            def tokens(e):
                pe.wait_ge(xe_in, e * 32 + 32)
                for k in range(4):
                    for i in range(2):
                        cols = slice(P * (2 * k + i), P * (2 * k + i + 1))
                        pe.transpose(ps[:, k, CAP * i:CAP * i + CAP_P], xe[:, 0, cols], ident[:, :])
                        tr = pe.transpose(ps[:, k, CAP * i + CAP_P:CAP * (i + 1)], xe[0:CAP_S, 1, cols],
                                          ident[0:CAP_S, 0:CAP_S])
                    tr.then_inc(t_filled, 1)

            def product(out, slot, f):
                for k in range(KB):
                    w = slice(CW * k + P * (f % 2), CW * k + P * (f % 2) + P)
                    if k:
                        pe.matmul(out[:, 0:CAP], wlo[:, slot, w], xT[:, k, 0:CAP], start=False, stop=False,
                                  skip_group_check=True)
                    mm = pe.matmul(out[:, 0:2 * CAP], whi[:, slot, w], xT[:, k, :], start=k == 0, stop=k == KB - 1,
                                   skip_group_check=True)
                    if not k:
                        pe.matmul(out[:, 0:CAP], wlo[:, slot, w], xT[:, k, 0:CAP], start=False, stop=False,
                                  skip_group_check=True)
                return mm

            def down(e, k):
                for f in (2 * k, 2 * k + 1):
                    part = slice(0, CAP_P), slice(2 * CAP - CAP_P, 2 * CAP)
                    start, stop = f == 0, f == FB - 1
                    for n in range(2):
                        w = slice(D * (f % 2) + GW * n, D * (f % 2) + GW * (n + 1))
                        pe.matmul(ps[:, 4 + n, :], hid[:, f, part[0]], whi[:, (8 + k) % SPL, w], start=start, stop=False)
                        pe.matmul(ps[:, 4 + n, :], hid[:, f, part[0]], wlo[:, (8 + k) % SPL, w], start=False, stop=False)
                    for n in range(2):
                        w = slice(D * (f % 2) + GW * n, D * (f % 2) + GW * (n + 1))
                        pe.matmul(ps[:, 4 + n, :], hid[:, f, part[1]], whi[:, (8 + k) % SPL, w], start=False, stop=stop)
                    both = hid[:, f, CAP_P:CAP_P + 2 * CAP_S]
                    for n in range(2):
                        w = slice(D * (f % 2) + GW * n, D * (f % 2) + GW * (n + 1))
                        pe.matmul(ps[:, 6 + n, :], both, whi[:, (8 + k) % SPL, w], start=start, stop=False)
                        mm = pe.matmul(ps[:, 6 + n, :], both, wlo[:, (8 + k) % SPL, w], start=False, stop=stop)
                mm.then_inc(d_used, 1)

            def expert(e, last=False):
                for f in range(FB):
                    c, b = f // 2, 2 * (f % 2)
                    if f == 0:
                        pe.wait_ge(t_lo, e * 4 + 4)
                    if f >= 2:
                        pe.wait_ge(gu_summed, e * FB + (f - 1))
                    if f % 2 == 0:
                        pe.wait_ge(w_split, e * N_CH + (2 * c + 1))
                    product(ps[:, b, :], 2 * c % SPL, f)
                    if f % 2 == 0:
                        pe.wait_ge(w_split, e * N_CH + (2 * c + 2))
                    product(ps[:, b + 1, :], (2 * c + 1) % SPL, f).then_inc(gu_filled, 1)
                for k in range(4):
                    pe.wait_ge(w_split, e * N_CH + (9 + k))
                    pe.wait_ge(hid_lo, e * (2 * FB) + (4 * k + 4))
                    if k == 0:
                        pe.wait_ge(ye_sum, e * 1 + 1)
                    down(e, k)
                    if k == 1 and not last:
                        pe.wait_ge(gu_summed, e * FB + FB)
                        tokens(e + 1)

            wait_drained(pe, "idx", 1)
            tokens(0)
            with pe.Fori(0, NE - 1) as e:
                expert(e)
            expert(NE - 1, last=True)

        @block.vector
        def _(dve):
            n_step, n_split = [0], [0]

            def step(ins):
                ins.then_inc(dve_step, 1)
                n_step[0] += 1

            def after_step():
                dve.wait_ge(dve_step, n_step[0])

            def drain(ins, *key):
                ins.then_inc(drained[drainer[key]], 1)

            def split_lo(c):
                dve.wait_ge(ws_hi, split_n[c] + 1)
                pair_of = wo[:, c[1], :, :] if c[0] == "wo" else slot_of(c)
                dve.tensor_tensor(pair_of[:, 1, :], wraw[:, raw_n[c] % RS, :], pair_of[:, 0, :].bitcast(F32),
                                  ALU.subtract).then_inc(ws_lo, 1)

            def split_ahead(chunks):
                last = ring_n[chunks[-1]] + SR - 1
                end = len(ring) if ring_n[chunks[0]] >= first_s else first_s
                while n_split[0] <= min(last, end - 1):
                    split_lo(ring[n_split[0]])
                    n_split[0] += 1

            wait_filled(dve, "vec")
            drain(dve.tensor_copy(VT[:, :], bank("vec")[:, 0:V_N]), "vec")
            dve.wait_ge(silw_hi, 1)
            dve.tensor_tensor(silw[:, :, 32:34], silc[:, :].rearrange("p (s k) -> p k s", s=2),
                              silw[:, :, 0:2].bitcast(F32), ALU.subtract).then_inc(silw_ready, 1)

            def ada_drain(j):
                n = width_of(j)
                cols = stage(j)
                wait_filled(dve, "ada", j)
                dve.wait_ge(brow_in[j % 4], 32 * (j // 4 + 1))
                if j >= 2:
                    dve.wait_ge(mod_out[j % 2], 16 * (j // 2))
                plus_bias = dve.tensor_tensor(cols, bank("ada", j)[0:2, 0:n], brow[0:2, j % 4, 0:n], ALU.add)
                if j < N_MIX:
                    drain(plus_bias, "ada", j)
                    return
                step(plus_bias)
                after_step()
                dve.wait_ge(ada_lo_ready, j - N_MIX + 1)
                drain(dve.tensor_tensor(cols, cols, ada_lo[0:2, 0:n], ALU.add), "ada", j)

            def x_norm(s, g):
                tt = T0[s] + GT * g
                dve.wait_ge(ssx_ready, tt + GT)
                r = rsx[:, tt:tt + GT]
                dve.tensor_scalar(r, ssx[:, tt:tt + GT], 1.0 / D, EPS, ALU.mult, ALU.add).then_inc(var_x, 1)
                dve.wait_ge(std_x, tt // GT + 1)
                step(dve.reciprocal(r, r))
                after_step()
                for t in range(GT):
                    x = xg[s][:, g, t, :]
                    dve.tensor_scalar(x, x, rsx[:, tt + t:tt + t + 1], None, ALU.mult).then_inc(xn_ready, 1)

            def hT_drains(s, g):
                cols = slice(GW * g, GW * (g + 1))
                n = (T0[s] // GT + g) * KB // 2
                for i in range(KB // 2):
                    b = 2 * i + 1
                    tmp = ht_d[s][:, i % 2, :]
                    wait_filled(dve, "hT", s, g, b)
                    dve.tensor_scalar(tmp, bank("hT", s, g, b), gsm[:, s, b:b + 1], modT[:, s, b:b + 1],
                                      ALU.mult, ALU.add).then_inc(ht_mod, 1)
                    wait_drained(dve, "hT", s, g, b - 1)
                    dve.tensor_tensor(hT[s][:, 1, b - 1, cols], ht_a[s][:, i % 2, :],
                                      hT[s][:, 0, b - 1, cols].bitcast(F32), ALU.subtract).then_inc(hT_lo, 1)
                    dve.wait_ge(hT_hi, n + i + 1)
                    drain(dve.tensor_tensor(hT[s][:, 1, b, cols], tmp, hT[s][:, 0, b, cols].bitcast(F32),
                                            ALU.subtract), "hT", s, g, b)

            def convolution(s, i):
                w = [VT[:, V_CONV + 3 * k + i:V_CONV + 3 * k + i + 1] for k in range(3)]
                step(dve.tensor_scalar(cv[s][:, :], a_pad[s][:, 1:1 + W[s]], w[1], None, ALU.mult))
                for k in (0, 2):
                    after_step()
                    step(dve.scalar_tensor_tensor(out=cv[s][:, :], in0=a_pad[s][:, k:k + W[s]], scalar=w[k],
                                                  in1=cv[s][:, :], op0=ALU.mult, op1=ALU.add))
                after_step()

            def ab_and_v(s):
                r = ssv[:, T0[s]:T0[s] + TL[s]]
                wait_drained(dve, "vt", s, 2, NG[s] - 1)
                for t in range(TL[s]):
                    if t:
                        after_step()
                    step(dve.tensor_tensor_reduce(vjunk[s][:, :], v[s][:, t, :], v[s][:, t, :], 1.0, 0.0, ALU.mult,
                                                  ALU.add, r[:, t:t + 1]))
                after_step()
                dve.tensor_scalar(r, r, 1.0 / SGU_W, EPS, ALU.mult, ALU.add).then_inc(var_v, 1)
                for t in range(0, TL[s], 2):
                    wait_filled(dve, "ab", s, t)
                    drain(dve.tensor_copy(AB[s][:, t, :, :, :].rearrange("p a b c -> p (a b c)"), bank("ab", s, t)),
                          "ab", s, t)
                dve.wait_ge(std_v, s + 1)
                step(dve.reciprocal(r, r))
                after_step()
                for t in range(TL[s]):
                    dve.tensor_scalar(v[s][:, t, :], v[s][:, t, :], r[:, t:t + 1], None, ALU.mult).then_inc(v_ready, 1)

            def mixers(s, between):
                if s:
                    for i in range(GT):
                        dve.wait_ge(h2_out[i], 16 * TL[0] // GT)
                for n, col in enumerate((0, W[s] + 1)):
                    dve.memset(a_pad[s][:, col:col + 1], 0.0).then_inc(pads_set, 1)
                dve.wait_ge(pads_set, 2 * (s + 1))
                for n, (kind, i) in enumerate(z_steps(s)):
                    chunks = chunks_of(s, kind, i)
                    if chunks:
                        split_ahead(chunks)
                    if kind == "ada":
                        ada_drain(i)
                    for g in range(NG[s]):
                        cols = slice(GW * g, GW * (g + 1))
                        if kind == "za":
                            wait_filled(dve, "za", s, i, g)
                            wait_drained(dve, "zc", s, i, g)
                            drain(dve.tensor_tensor(a_pad[s][:, 1 + GW * g:1 + GW * (g + 1)], bank("za", s, i, g),
                                                    zc_sb[s][:, cols], ALU.mult), "za", s, i, g)
                        if kind == "zb":
                            wait_filled(dve, "zb", s, i, g)
                            drain(dve.tensor_tensor(Y[s][:, i, cols], bank("zb", s, i, g), cv[s][:, cols], ALU.mult),
                                  "zb", s, i, g)
                        if kind == "vt":
                            wait_filled(dve, "vt", s, i, g)
                            drain(dve.tensor_copy(v[s][:, GT * g:GT * (g + 1), P * i:P * (i + 1)],
                                                  bank("vt", s, i, g).rearrange("p (a n) -> p a n", a=GT)),
                                  "vt", s, i, g)
                    if kind == "za":
                        wait_drained(dve, "za", s, i, NG[s] - 1)
                        convolution(s, i)
                    if kind == "ab":
                        ab_and_v(s)
                    between(n)

            def gating(s):
                dve.wait_ge(bsp_in, 16 * N_SGU)
                wait_drained(dve, "ada", N_ADA - 1)
                for i in range(3):
                    for g in range(NG[s]):
                        cols = slice(GW * g, GW * (g + 1))
                        wait_filled(dve, "sv", s, i, g)
                        if i or g:
                            wait_drained(dve, *[("sv", s, i, g - 1), ("sv", s, i - 1, NG[s] - 1)][g == 0])
                        step(dve.scalar_tensor_tensor(
                            out=svt[:, :].rearrange("p (a n) -> p a n", a=GT),
                            in0=bank("sv", s, i, g).rearrange("p (a n) -> p a n", a=GT),
                            scalar=VT[:, V_GSGU + i:V_GSGU + i + 1],
                            in1=bsp[:, i:i + 1, :].to_broadcast([P, GT, P]), op0=ALU.mult, op1=ALU.add))
                        after_step()
                        wait_drained(dve, "zu", s, i, g)
                        drain(dve.tensor_tensor(Y[s][:, 5 + i, cols], Y[s][:, 5 + i, cols], svt[:, :], ALU.mult),
                              "sv", s, i, g)

            n_y = [0]

            def y_split_lo(s, blocks):
                for b in blocks:
                    n_y[0] += 1
                    dve.wait_ge(y_hi, n_y[0])
                    dve.scalar_tensor_tensor(out=Yhl[s][:, :, b, 1, :],
                                             in0=Y[s][:, b, :].rearrange("p (g n) -> p g n", n=GW),
                                             scalar=VT[:, V_GGRP + b:V_GGRP + b + 1],
                                             in1=Yhl[s][:, :, b, 0, :].bitcast(F32), op0=ALU.mult, op1=ALU.subtract
                                             ).then_inc(y_lo, 1)

            def mixers_end(s):
                half = W[s] // 2

                def w_out_lo(*blocks):
                    for b in blocks if s == 0 else ():
                        split_lo(("wo", b))

                def add_square(n):
                    k, need = ((0, 2), (0, 3), (2, 5), (2, 6), (1, 8))[n]
                    dve.wait_ge(sq_done, KB * s + need)
                    if n:
                        dve.wait_ge(sq_added, 5 * s + n)
                    dve.tensor_tensor(SQ[k][s][:, :], SQ[k][s][:, :], sqt[k][s][:, :], ALU.add).then_inc(sq_added, 1)

                w_out_lo(0)
                gating(s)
                if s:
                    chosen(0)
                w_out_lo(1)
                y_split_lo(s, range(3))
                w_out_lo(2)
                y_split_lo(s, range(5, KB))
                w_out_lo(3, 4)
                add_square(0)
                add_square(1)
                w_out_lo(5, 6, 7)
                add_square(2)
                add_square(3)
                for fb in range(2):
                    wait_filled(dve, "odd", s, fb)
                    wait_drained(dve, "even", s, fb)
                    o, e = bank("odd", s, fb)[:, 0:half], Y[s][:, 3 + fb, half:2 * half]
                    step(dve.tensor_tensor(Y[s][:, 3 + fb, 0:half], o, e, ALU.add))
                    after_step()
                    drain(dve.tensor_tensor(e, e, o, ALU.subtract), "odd", s, fb)
                y_split_lo(s, (3, 4))
                add_square(4)
                wait_filled(dve, "ssq", s)
                tiles = slice(T0[s], T0[s] + TL[s])
                drain(dve.tensor_copy(ssy[:, tiles, :].rearrange("p t k -> p (t k)"), bank("ssq", s)[:, 0:3 * TL[s]]),
                      "ssq", s)
                wait_drained(dve, "ssq", s)
                for k, width in enumerate((CONV_W, FOUR_W, SGU_W)):
                    dve.tensor_scalar(rsy[:, tiles, k:k + 1], ssy[:, tiles, k:k + 1], 1.0 / width, EPS, ALU.mult,
                                      ALU.add).then_inc(var_y, 1)
                dve.wait_ge(std_y, s + 1)
                dve.reciprocal(rsy[:, tiles, :], rsy[:, tiles, :]).then_inc(rsy_ready, 1)
                dve.wait_ge(rsy_ready, s + 1)
                dve.memset(lgT[:, :], 0.0).then_inc(lgt_zero, 1)

            def router_drains(s, g):
                for b in range(1, KB, 2):
                    wait_filled(dve, "h2T", s, g, b)
                    wait_h2t_slot(dve, s, g, b)
                    drain(dve.tensor_copy(h2T[:, b % 4, :], bank("h2T", s, g, b)), "h2T", s, g, b)

            def residual(s):
                dve.wait_ge(ffn_in, 48 * (s + 1))
                dve.scalar_tensor_tensor(out=gsf_b[:, :], in0=gsf_b[:, :], scalar=1.0, in1=gffn_b[:, :],
                                         op0=ALU.add, op1=ALU.mult).then_inc(gsf_ready, 1)
                dve.wait_ge(gsf_ready, s + 1)
                dve.wait_ge(gtm_in, 16 * (s + 1))
                for t in range(TL[s]):
                    tt = T0[s] + t
                    for k, before in ((2, 0), (1, 2)):
                        for h in range(2):
                            o = x2[:, tt % 2, GW * h:GW * (h + 1)]
                            wait_filled(dve, "out", s, t, k, h)
                            wait_drained(dve, "out", s, t, before, h)
                            drain(dve.scalar_tensor_tensor(out=o, in0=bank("out", s, t, k, h),
                                                           scalar=rsy[:, tt, k:k + 1], in1=o, op0=ALU.mult,
                                                           op1=ALU.add), "out", s, t, k, h)
                    wait_drained(dve, "out", s, t, 1, 1)
                    o = x2[:, tt % 2, :]
                    step(dve.tensor_tensor(o, o, gtm_b[:, :], ALU.mult))
                    dve.wait_ge(xr_in[tt % 2], 16 * (tt // 2 + 1))
                    after_step()
                    dve.tensor_tensor(o, o, xr[:, tt % 2, :], ALU.add).then_inc(x2_ready, 1)
                    if t == GT:
                        router_drains(s, 0)
                    r = rs2[:, tt:tt + 1]
                    dve.wait_ge(ss2_ready, tt + 1)
                    dve.tensor_scalar(r, ss2[:, tt:tt + 1], 1.0 / D, EPS, ALU.mult, ALU.add).then_inc(var_2, 1)
                    dve.wait_ge(std_2, tt + 1)
                    step(dve.reciprocal(r, r))
                    after_step()
                    hh = h2[:, tt % GT, :]
                    step(dve.scalar_tensor_tensor(out=hh, in0=x2[:, tt % 2, :], scalar=r, in1=gsf_b[:, :],
                                                  op0=ALU.mult, op1=ALU.mult))
                    after_step()
                    dve.tensor_tensor(hh, hh, shf_b[:, :], ALU.add).then_inc(h2_ready, 1)
                    if s == 0 and t == GT + 1:
                        x_norm(1, 0)
                    if s == 0 and t == GT + 2:
                        for _ in range(2):
                            split_lo(ring[n_split[0]])
                            n_split[0] += 1
                if s == 0:
                    hT_drains(1, 0)
                router_drains(s, NG[s] - 1)

            def softmax(s):
                n = NG[s]
                wait_filled(dve, "lt", s)
                drain(dve.tensor_copy(L[:, :, :, :].rearrange("p a b c -> p (a b c)"), bank("lt", s)[:, 0:GT * 64]),
                      "lt", s)
                wait_drained(dve, "lt", s)
                for t in range(GT):
                    step(dve.tensor_reduce(smax[:, n * t:n * (t + 1)], L[:, t, 0:n, 0:NE], AX.X, ALU.max))
                after_step()
                for i in range(n * GT):
                    t, g = i // n, i % n
                    ins = dve.tensor_scalar(L2[:, t, g, :], L[:, t, g, 0:NE], smax[:, i:i + 1], None, ALU.subtract)
                    step(ins) if i < n * GT - 1 else ins.then_inc(exp_in, 1)
                dve.wait_ge(exp_out, s + 1)
                for t in range(GT):
                    step(dve.tensor_reduce(smax[:, n * t:n * (t + 1)], L2[:, t, 0:n, :], AX.X, ALU.add))
                after_step()
                step(dve.reciprocal(smax[:, 0:n * GT], smax[:, 0:n * GT]))
                after_step()
                for i in range(n * GT):
                    t, g = i // n, i % n
                    ins = dve.tensor_scalar(affm[:, GT * g + t, :], L2[:, t, g, :], smax[:, i:i + 1], None, ALU.mult)
                    step(ins) if i < n * GT - 1 else ins.then_inc(aff_ready, 1)

            def aff_drains(s):
                for g in range(NG[s]):
                    wait_filled(dve, "aff", s, g)
                    drain(dve.tensor_copy(aff[0:NE, GW * g:GW * (g + 1)], bank("aff", s, g)[0:NE, :]), "aff", s, g)
                wait_drained(dve, "aff", s, NG[s] - 1)

            def topk_eight(s, n):
                eight, row = slice(8 * n, 8 * n + 8), aff[0:NE, 0:W[s]]
                after_step()
                step(dve.max(vals[0:NE, eight], row))
                after_step()
                step(dve.max_index(idxu[0:NE, eight], vals[0:NE, eight], row))
                step(dve.match_replace(row, vals[0:NE, eight], row, -2.0))

            def topk_end(s):
                after_step()
                dve.tensor_copy(idxf[0:NE, 0:CAPS[s]], idxu[0:NE, 0:CAPS[s]]).then_inc(topk_ready, 1)

            def chosen(s):
                cap = CAPS[s]
                wait_filled(dve, "idx", s)
                if s:
                    step(dve.memset(gates[cap:P, s, :], 0.0))
                    step(dve.memset(rowid[cap:P, s, :], 0))
                    after_step()
                dve.tensor_copy(gates[0:cap, s, :], bank("idx", s)[0:cap, 0:NE]).then_inc(routed, 1)
                dve.tensor_scalar(rowid[0:cap, s, :], bank("idx", s)[0:cap, NE:2 * NE], float(BASE[s]), None, ALU.add
                                  ).then_inc(routed, 1)
                dve.wait_ge(routed, 2 * (s + 1))
                drain(dve.memset(tick[:, 0:1], 0.0), "idx", s)
                wait_drained(dve, "idx", s)

            def mod_drain(j):
                wait_filled(dve, "mod", j)
                drain(dve.tensor_copy(modT[:, :, 4 * j:4 * j + 4].rearrange("p s m -> p m s"),
                                      bank("mod", j)[:, 0:8].rearrange("p (m s) -> p m s", s=2)), "mod", j)

            for j in range(N_MIX):
                if j >= 2:
                    x_norm(0, j - 2)
                ada_drain(j)
                if j:
                    mod_drain(j - 1)
            mod_drain(N_MIX - 1)
            wait_drained(dve, "mod", N_MIX - 1)
            for s in range(2):
                dve.scalar_tensor_tensor(out=gsm[:, s, :], in0=modT[:, s, 8:16], scalar=1.0,
                                         in1=VT[:, V_GMIX:V_GMIX + KB], op0=ALU.add, op1=ALU.mult).then_inc(gsm_ready, 1)
            dve.wait_ge(gsm_ready, 2)
            split_ahead([ring[0]])
            for g in range(NG[0]):
                hT_drains(0, g)
            for n, (h0, h1) in enumerate(((0, 4), (4, N_SGU))):
                wait_filled(dve, "wsp", n)
                drain(dve.tensor_copy(wspT[:, h0:h1, :].rearrange("p a n -> p (a n)"),
                                      bank("wsp", n)[:, 0:P * (h1 - h0)]), "wsp", n)
            mixers(0, lambda n: None)
            mixers_end(0)
            residual(0)

            def routing_of_prompt(n):
                if n == LT_STEP:
                    softmax(0)
                if n == AFF_STEP:
                    aff_drains(0)
                if AFF_STEP < n <= AFF_STEP + CAP_P // 8:
                    topk_eight(0, n - AFF_STEP - 1)

            assert len(z_steps(1)) > AFF_STEP + CAP_P // 8
            mixers(1, routing_of_prompt)
            topk_end(0)
            mixers_end(1)
            residual(1)
            softmax(1)
            aff_drains(1)
            for n in range(CAP_S // 8):
                topk_eight(1, n)
            topk_end(1)
            chosen(1)

            def split(e, j):
                dve.wait_ge(w_hi, e * N_CH + (j + 1))
                dve.tensor_tensor(wlo[:, j % SPL, :], raw[:, j % RAW, :], whi[:, j % SPL, :].bitcast(F32), ALU.subtract
                                  ).then_inc(w_split, 1)

            def tokens_lo(e):
                for k in range(4):
                    dve.wait_ge(t_hi, e * 4 + (k + 1))
                    dve.tensor_tensor(xT[:, 2 * k:2 * k + 2, CAP:2 * CAP],
                                      ps[:, k, 0:2 * CAP].rearrange("p (a n) -> p a n", a=2),
                                      xT[:, 2 * k:2 * k + 2, 0:CAP].bitcast(F32), ALU.subtract).then_inc(t_lo, 1)

            def hidden_lo(e, f):
                dve.wait_ge(hid_hi, e * FB + (f + 1))
                for dst, src in ((CAP, slice(CAP_P, CAP)), (CAP + CAP_S, slice(0, CAP_P))):
                    n = src.stop - src.start
                    dve.tensor_tensor(hid[:, f, dst:dst + n], hidf[:, f % 2, src], hid[:, f, src].bitcast(F32), ALU.subtract
                                      ).then_inc(hid_lo, 1)

            def outputs(e):
                dve.tensor_copy(gcur[:, :], gates[:, :, bass.ds(e, 1)].rearrange("p a b -> p (a b)")
                                ).then_inc(gate_cur, 1)
                dve.wait_ge(gate_cur, e + 1)
                dve.wait_ge(ye_free, e + 1)
                dve.wait_ge(d_used, e * 4 + 4)
                for n in range(2):
                    cols = slice(GW * n, GW * (n + 1))
                    dve.scalar_tensor_tensor(out=ye[:, 0, cols], in0=ps[:, 4 + n, :], scalar=gcur[:, 0:1],
                                             in1=gtf_b[:, 0, cols], op0=ALU.mult, op1=ALU.mult).then_inc(ye_ready, 1)
                dve.wait_ge(ysl_copied, e + 1)
                y = ye[0:CAP_S, 1, :]
                dve.tensor_tensor(y.rearrange("p (a n) -> p a n", a=2), ps[0:CAP_S, 6:8, :],
                                  ysl[0:CAP_S, :].rearrange("p (a n) -> p a n", a=2), ALU.add).then_inc(ye_sum, 1)
                dve.wait_ge(ye_sum, e + 2)
                dve.scalar_tensor_tensor(out=y, in0=y, scalar=gcur[0:CAP_S, 1:2], in1=gtf_b[0:CAP_S, 1, :],
                                         op0=ALU.mult, op1=ALU.mult).then_inc(ye_ready, 1)

            def expert(e, last=False):
                for f in range(FB):
                    b = 2 * (f % 2)
                    dve.wait_ge(lo_copied, e * FB + (f + 1))
                    dve.tensor_tensor(gu[:, f % 2, :, :], ps[:, b:b + 2, 0:CAP], gu_l[:, f % 2, :, :], ALU.add).then_inc(gu_summed, 1)
                    if f:
                        hidden_lo(e, f - 1)
                    split(e, f + 4)
                    dve.wait_ge(silu_done, e * FB + (f + 1))
                    dve.tensor_tensor(hidf[:, f % 2, :], sg[:, f % 2, :], gu[:, f % 2, 1, :], ALU.mult).then_inc(hid_done, 1)
                hidden_lo(e, FB - 1)
                if not last:
                    for i in range(2):
                        split(e + 1, i)
                    tokens_lo(e + 1)
                    for i in range(2):
                        split(e + 1, 2 + i)
                outputs(e)

            dve.memset(tick[:, 0:1], 0.0).then_inc(ye_sum, 1)
            dve.wait_ge(gtf_in, 32)
            for i in range(4):
                split(0, i)
            tokens_lo(0)
            with dve.Fori(0, NE - 1) as e:
                expert(e)
            expert(NE - 1, last=True)

            dve.wait_ge(gfin_in, 16)
            for t in range(NT):
                dve.wait_ge(ssf_ready, t + 1)
                r = rsf[:, t:t + 1]
                dve.tensor_scalar(r, ssf[:, t:t + 1], 1.0 / D, EPS, ALU.mult, ALU.add).then_inc(var_f, 1)
                dve.wait_ge(std_f, t + 1)
                dve.reciprocal(r, r).then_inc(rsf_ready, 1)
                dve.wait_ge(rsf_ready, t + 1)
                y = fin[:, t, :]
                dve.scalar_tensor_tensor(out=y, in0=y, scalar=r, in1=gfin_b[:, :], op0=ALU.mult, op1=ALU.mult
                                         ).then_inc(fin_ready, 1)


_INS = ["x_prompt", "x_sample", "c_prompt", "c_sample", "w_ada", "b_ada", "g_mix", "w_in", "conv_w", "g_sgu",
        "w_spatial", "b_spatial", "g_grp", "w_out", "g_ffn", "w_router", "w_gate", "w_up", "w_down", "g_final"]
_OUTS = [(1, w, D) for w in W]


def kernel(**inputs):
    import concourse.bacc as bacc
    from concourse.bass_utils import run_bass_kernel_spmd

    nc = bacc.Bacc("TRN2", target_bir_lowering=False, num_devices=1)
    sent, aps = {}, {}
    arrays = {name: np.ascontiguousarray(inputs[name]) for name in _INS} | dft_constants()
    for name, x in arrays.items():
        sent[f"in_{name}"] = x
        aps[name] = nc.dram_tensor(f"in_{name}", x.shape, mybir.dt.from_np(x.dtype), kind="ExternalInput").ap()
    outs = [nc.dram_tensor(f"out_{i}", s, F32, kind="ExternalOutput").ap() for i, s in enumerate(_OUTS)]
    encoder_kernel(nc, aps, *outs)
    r = run_bass_kernel_spmd(nc, [sent], core_ids=[0])
    return tuple(r.results[0][f"out_{i}"] for i in range(2))
```
